# Optimizing a Trainium2 kernel written in Bass

```python
import functools
import jax, jax.numpy as jnp
from jax import lax
import numpy as np
import math

D_MODEL = 1024
BATCH = 1
SEQ = 512
DEPTH = 1

HEAD_DIM = 64
GROUP_WIDTH = D_MODEL // 4
MIX_WIDTH = 4 * GROUP_WIDTH
N_GROUP_HEADS = GROUP_WIDTH // HEAD_DIM
SHORT_CONV_K = 3
DSWA_CONFIGS = ((128, 1), (512, 4), (2048, 16))
POOL_WINDOWS = (2, 4, 8, 16)
POOL_GROUP = GROUP_WIDTH // len(POOL_WINDOWS)
ROPE_THETA = 500000.0
ROPE_DIM = HEAD_DIM // 4
Q_BLOCK = 128
MEM_LEN = 256
XA_HEADS = 4
XA_HEAD_DIM = D_MODEL // XA_HEADS
D_FF = ((8 * D_MODEL // 3 + 127) // 128) * 128
FFN_CONV_K = 3
RMS_EPS = 1e-6
NEG_INF = -1e30
FORGET_BIAS_INIT = 3.0
N_IN = 3 * GROUP_WIDTH + 3 * GROUP_WIDTH + 3 * GROUP_WIDTH + N_GROUP_HEADS + GROUP_WIDTH


def rms_norm(t, g):
    tf = t.astype(jnp.float32)
    y = tf * lax.rsqrt(jnp.mean(tf * tf, axis=-1, keepdims=True) + RMS_EPS)
    return (y * g.astype(jnp.float32)).astype(t.dtype)

def causal_depthwise_conv(t, w):
    K, C = w.shape
    return lax.conv_general_dilated(
        t, w.astype(t.dtype)[:, None, :], window_strides=(1,), padding=((K - 1, 0),),
        dimension_numbers=("NWC", "WIO", "NWC"), feature_group_count=C)

def to_heads(t):
    B, S, W = t.shape
    return t.reshape(B, S, W // HEAD_DIM, HEAD_DIM).transpose(0, 2, 1, 3)

def from_heads(t):
    B, H, S, dh = t.shape
    return t.transpose(0, 2, 1, 3).reshape(B, S, H * dh)

def rope_tables(positions):
    inv_freq = ROPE_THETA ** (-jnp.arange(0, ROPE_DIM, 2, dtype=jnp.float32) / ROPE_DIM)
    ang = positions.astype(jnp.float32)[:, None, :, None] * inv_freq
    return jnp.cos(ang), jnp.sin(ang)

def apply_partial_rope(t, cos, sin):
    tf = t.astype(jnp.float32)
    r1, r2 = jnp.split(tf[..., :ROPE_DIM], 2, axis=-1)
    rot = jnp.concatenate([r1 * cos - r2 * sin, r2 * cos + r1 * sin], axis=-1)
    return jnp.concatenate([rot, tf[..., ROPE_DIM:]], axis=-1).astype(t.dtype)

def short_conv_mixer(p, w_conv):
    h, b_gate, c_gate = jnp.split(p, 3, axis=-1)
    return b_gate * causal_depthwise_conv(c_gate * h, w_conv)

def dilated_attention(q, k, v):
    B, H, S, dh = q.shape
    nb = S // Q_BLOCK
    qb = q.reshape(B, H, nb, Q_BLOCK, dh).transpose(2, 0, 1, 3, 4)
    kf = k.astype(jnp.float32)
    vf = v.astype(jnp.float32)
    scale = dh ** -0.5

    def block(args):
        i, qi = args
        t = i * Q_BLOCK + jnp.arange(Q_BLOCK)
        qs = qi.astype(jnp.float32) * scale
        scores, values = [], []
        for window, dil in DSWA_CONFIGS:
            idx = t[:, None] - dil * jnp.arange(window // dil + 1)[None, :]
            idxc = jnp.maximum(idx, 0)
            kg = kf[:, :, idxc]
            s = jnp.einsum("bhqd,bhqnd->bhqn", qs, kg)
            scores.append(jnp.where(idx >= 0, s, NEG_INF))
            values.append(vf[:, :, idxc])
        m = functools.reduce(jnp.maximum, [s.max(axis=-1, keepdims=True) for s in scores])
        num, den = 0.0, 0.0
        for s, vg in zip(scores, values):
            e = jnp.exp(s - m)
            num = num + jnp.einsum("bhqn,bhqnd->bhqd", e, vg)
            den = den + e.sum(axis=-1, keepdims=True)
        return num / den

    o = lax.map(block, (jnp.arange(nb), qb))
    return o.transpose(1, 2, 0, 3, 4).reshape(B, H, S, dh).astype(q.dtype)

def dilated_mixer(p, cos, sin):
    q, k, v = [to_heads(t) for t in jnp.split(p, 3, axis=-1)]
    q = apply_partial_rope(q, cos, sin)
    k = apply_partial_rope(k, cos, sin)
    return from_heads(dilated_attention(q, k, v))

def forgetting_attention(q, k, v, c):
    B, H, S, dh = q.shape
    nb = S // Q_BLOCK
    qb = q.reshape(B, H, nb, Q_BLOCK, dh).transpose(2, 0, 1, 3, 4)
    cb = c.reshape(B, H, nb, Q_BLOCK).transpose(2, 0, 1, 3)
    kf = k.astype(jnp.float32)
    vf = v.astype(jnp.float32)
    kpos = jnp.arange(S)
    scale = dh ** -0.5

    def block(args):
        i, qi, ci = args
        t = i * Q_BLOCK + jnp.arange(Q_BLOCK)
        s = jnp.einsum("bhqd,bhkd->bhqk", qi.astype(jnp.float32) * scale, kf)
        s = s + ci[..., None] - c[:, :, None, :]
        s = jnp.where(kpos[None, :] <= t[:, None], s, NEG_INF)
        return jnp.einsum("bhqk,bhkd->bhqd", jax.nn.softmax(s, axis=-1), vf)

    o = lax.map(block, (jnp.arange(nb), qb, cb))
    return o.transpose(1, 2, 0, 3, 4).reshape(B, H, S, dh).astype(q.dtype)

def forgetting_mixer(p, b_f):
    G = GROUP_WIDTH
    q, k, v = to_heads(p[..., :G]), to_heads(p[..., G:2 * G]), to_heads(p[..., 2 * G:3 * G])
    logf = jax.nn.log_sigmoid(p[..., 3 * G:].astype(jnp.float32) + b_f.astype(jnp.float32))
    c = jnp.cumsum(logf, axis=1).transpose(0, 2, 1)
    return from_heads(forgetting_attention(q, k, v, c))

def pool_mixer(p, w_pool, scale):
    B, S, _ = p.shape
    pf = p.astype(jnp.float32).reshape(B, S, len(POOL_WINDOWS), POOL_GROUP)
    cs = jnp.cumsum(pf, axis=1)
    cs0 = jnp.concatenate([jnp.zeros_like(cs[:, :1]), cs], axis=1)
    t = jnp.arange(S)
    outs = []
    for g, w in enumerate(POOL_WINDOWS):
        upper = cs0[:, 1:, g]
        lower = cs0[:, jnp.maximum(t + 1 - w, 0), g]
        cnt = jnp.minimum(t + 1, w).astype(jnp.float32)[None, :, None]
        outs.append((upper - lower) / cnt - pf[:, :, g])
    z = jnp.stack(outs, axis=2)
    y = jnp.einsum("bsgc,gcd->bsgd", z, w_pool.astype(jnp.float32)).reshape(B, S, GROUP_WIDTH)
    return (y * scale.astype(jnp.float32)).astype(p.dtype)

def memory_cross_attention(xn, memn, w_q, w_kv, w_o):
    B, S, D = xn.shape
    M = memn.shape[1]
    q = (xn @ w_q).reshape(B, S, XA_HEADS, XA_HEAD_DIM)
    k, v = jnp.split(memn @ w_kv, 2, axis=-1)
    k = k.reshape(B, M, XA_HEADS, XA_HEAD_DIM)
    v = v.reshape(B, M, XA_HEADS, XA_HEAD_DIM)
    s = jnp.einsum("bshd,bmhd->bhsm", q.astype(jnp.float32), k.astype(jnp.float32)) * XA_HEAD_DIM ** -0.5
    o = jnp.einsum("bhsm,bmhd->bshd", jax.nn.softmax(s, axis=-1), v.astype(jnp.float32))
    return o.reshape(B, S, D).astype(xn.dtype) @ w_o

def conv_ffn(xn, w_up, w_conv, w_down):
    u = causal_depthwise_conv(xn @ w_up, w_conv)
    a, g = jnp.split(u, 2, axis=-1)
    return (a * jax.nn.silu(g)) @ w_down

def first_inputs(seed: int = 0) -> dict:
    key = jax.random.key(seed)
    ks = jax.random.split(key, 24)
    f32 = jnp.float32
    nrm = lambda k, shape, s: jax.random.normal(k, shape, f32) * s
    L, D, G = DEPTH, D_MODEL, GROUP_WIDTH
    x = jax.random.normal(ks[0], (BATCH, SEQ, D), f32)
    mem = jax.random.normal(ks[1], (BATCH, MEM_LEN, D), f32)
    offset = jax.random.randint(ks[2], (BATCH, 1), 0, 1024, dtype=jnp.int32)
    positions = (jnp.arange(SEQ, dtype=jnp.int32)[None, :] + offset).astype(jnp.int32)
    return {
        "x": x,
        "mem": mem,
        "positions": positions,
        "g_mix": 1.0 + nrm(ks[3], (L, D), 0.02),
        "w_in": nrm(ks[4], (L, D, N_IN), D ** -0.5),
        "b_forget": FORGET_BIAS_INIT + nrm(ks[5], (L, N_GROUP_HEADS), 0.1),
        "w_sconv": nrm(ks[6], (L, SHORT_CONV_K, G), SHORT_CONV_K ** -0.5),
        "w_pool": nrm(ks[7], (L, len(POOL_WINDOWS), POOL_GROUP, POOL_GROUP), POOL_GROUP ** -0.5),
        "pool_scale": 1.0 + nrm(ks[8], (L, G), 0.02),
        "w_out": nrm(ks[9], (L, MIX_WIDTH, D), MIX_WIDTH ** -0.5),
        "g_xa": 1.0 + nrm(ks[10], (L, D), 0.02),
        "g_mem": 1.0 + nrm(ks[11], (L, D), 0.02),
        "w_xq": nrm(ks[12], (L, D, D), D ** -0.5),
        "w_xkv": nrm(ks[13], (L, D, 2 * D), D ** -0.5),
        "w_xo": nrm(ks[14], (L, D, D), D ** -0.5),
        "g_ffn": 1.0 + nrm(ks[15], (L, D), 0.02),
        "w_up": nrm(ks[16], (L, D, 2 * D_FF), D ** -0.5),
        "w_ffconv": nrm(ks[17], (L, FFN_CONV_K, 2 * D_FF), FFN_CONV_K ** -0.5),
        "w_down": nrm(ks[18], (L, D_FF, D), D_FF ** -0.5),
        "g_final": 1.0 + nrm(ks[19], (D,), 0.02),
    }

def first_block(x, mem, positions, g_mix, w_in, b_forget, w_sconv, w_pool, pool_scale, w_out,
              g_xa, g_mem, w_xq, w_xkv, w_xo, g_ffn, w_up, w_ffconv, w_down, g_final):
    G = GROUP_WIDTH
    cos, sin = rope_tables(positions)
    h = x
    for l in range(DEPTH):
        xn = rms_norm(h, g_mix[l])
        proj = xn @ w_in[l]
        pa, pb, pc, pd = jnp.split(proj, [3 * G, 6 * G, 9 * G + N_GROUP_HEADS], axis=-1)
        ya = short_conv_mixer(pa, w_sconv[l])
        yb = dilated_mixer(pb, cos, sin)
        yc = forgetting_mixer(pc, b_forget[l])
        yd = pool_mixer(pd, w_pool[l], pool_scale[l])
        h = h + jnp.concatenate([ya, yb, yc, yd], axis=-1) @ w_out[l]
        h = h + memory_cross_attention(rms_norm(h, g_xa[l]), rms_norm(mem, g_mem[l]),
                                       w_xq[l], w_xkv[l], w_xo[l])
        h = h + conv_ffn(rms_norm(h, g_ffn[l]), w_up[l], w_ffconv[l], w_down[l])
    return rms_norm(h, g_final)


N_MIXERS = 2
N_HYENA_LAYERS = (DEPTH + N_MIXERS - 1) // N_MIXERS
N_NA_LAYERS = DEPTH // N_MIXERS
GRID_W = 64
HY_SHORT_CONV = 3
HY_EMB_DIM = 33
HY_N_BANDS = (HY_EMB_DIM - 1) // 2
HY_FILTER_WIDTH = 64
HY_FAST_DECAY_PCT = 0.3
HY_SLOW_DECAY_PCT = 1.5
HY_DECAY_TARGET = 1e-2
NA_HEADS = 16
NA_HEAD_DIM = D_MODEL // NA_HEADS
NA_KH = 8
NA_KW = 16
FFN_HIDDEN = -(-8 * D_MODEL // (3 * 256)) * 256


def rmsnorm(x, g):
    x32 = x.astype(jnp.float32)
    y = x32 * lax.rsqrt(jnp.mean(x32 * x32, axis=-1, keepdims=True) + RMS_EPS)
    return (y * g.astype(jnp.float32)).astype(x.dtype)

def short_conv(z, w, b):
    c = z.shape[-1]
    pad = HY_SHORT_CONV // 2
    y = lax.conv_general_dilated(
        z, w[:, None, :].astype(z.dtype), window_strides=(1,), padding=((pad, pad),),
        dimension_numbers=("NWC", "WIO", "NWC"), feature_group_count=c)
    return y + b

def hyena_filter(L, w1, b1, w2, b2, w3, b3, freq, w_out, decay):
    f32 = jnp.float32
    t = jnp.linspace(0.0, 1.0, L, dtype=f32)[:, None]
    w = 2.0 * math.pi * jnp.arange(L, dtype=f32)[:, None] / L
    bands = jnp.linspace(1e-4, HY_N_BANDS - 1, HY_N_BANDS, dtype=f32)[None, :]
    feat = jnp.concatenate([t, jnp.cos(bands * w), -jnp.sin(bands * w)], axis=-1)
    fr = freq.astype(f32)
    act = lambda a: jnp.sin(fr * a)
    h = act(feat @ w1.astype(f32) + b1.astype(f32))
    h = act(h @ w2.astype(f32) + b2.astype(f32))
    h = act(h @ w3.astype(f32) + b3.astype(f32))
    h = (h @ w_out.astype(f32)).reshape(L, 2, D_MODEL)
    h = h * jnp.exp(-t[:, :, None] * jnp.abs(decay.astype(f32)))
    g = jnp.concatenate([h[:, 0], jnp.zeros((1, D_MODEL), f32), jnp.flip(h[1:, 1], axis=0)], axis=0)
    return g / jnp.sum(jnp.abs(g), axis=0, keepdims=True)

def hyena_mixer(u, w_in, b_in, conv_w, conv_b, f_w1, f_b1, f_w2, f_b2, f_w3, f_b3,
                f_freq, f_wout, decay, skip, w_out, b_out):
    L = u.shape[1]
    z = short_conv(u @ w_in + b_in, conv_w, conv_b)
    x0, x1, v = jnp.split(z, 3, axis=-1)
    s = (v * x1).astype(jnp.float32)
    g = hyena_filter(L, f_w1, f_b1, f_w2, f_b2, f_w3, f_b3, f_freq, f_wout, decay)
    n = 2 * L
    y = jnp.fft.irfft(jnp.fft.rfft(s, n=n, axis=1) * jnp.fft.rfft(g, n=n, axis=0)[None],
                      n=n, axis=1)[:, :L]
    y = (y + s * skip.astype(jnp.float32)).astype(u.dtype) * x0
    return y @ w_out + b_out

def na_mixer(u, w_qkv, b_qkv, rpb, w_o, b_o):
    B_, L, D = u.shape
    rows = L // GRID_W
    kh = min(NA_KH, rows)
    kw = NA_KW
    qkv = u @ w_qkv + b_qkv
    q, k, v = [a.reshape(B_, rows, GRID_W, NA_HEADS, NA_HEAD_DIM) for a in jnp.split(qkv, 3, axis=-1)]
    q = q * (NA_HEAD_DIM ** -0.5)
    col = jnp.arange(GRID_W)
    col_start = jnp.clip(col - kw // 2, 0, GRID_W - kw)
    col_idx = col_start[:, None] + jnp.arange(kw)[None, :]
    col_off = col_idx - col[:, None] + (NA_KW - 1)

    def row_block(r):
        r_start = jnp.clip(r - kh // 2, 0, rows - kh)
        k_rows = lax.dynamic_slice_in_dim(k, r_start, kh, axis=1)
        v_rows = lax.dynamic_slice_in_dim(v, r_start, kh, axis=1)
        k_win = k_rows[:, :, col_idx]
        v_win = v_rows[:, :, col_idx]
        q_r = lax.dynamic_index_in_dim(q, r, axis=1, keepdims=False)
        s = jnp.einsum("bwhd,biwjhd->bhwij", q_r, k_win)
        row_off = r_start + jnp.arange(kh) - r + (NA_KH - 1)
        bias = rpb[:, row_off[None, :, None], col_off[:, None, :]]
        s = (s + bias[None]).astype(jnp.float32).reshape(B_, NA_HEADS, GRID_W, kh * kw)
        p = jax.nn.softmax(s, axis=-1).reshape(B_, NA_HEADS, GRID_W, kh, kw).astype(v.dtype)
        return jnp.einsum("bhwij,biwjhd->bwhd", p, v_win)

    out = lax.map(row_block, jnp.arange(rows))
    out = jnp.transpose(out, (1, 0, 2, 3, 4)).reshape(B_, L, D)
    return out @ w_o + b_o

def swiglu(x, w_gate, w_up, w_down):
    return (jax.nn.silu(x @ w_gate) * (x @ w_up)) @ w_down

def second_inputs(seed: int = 0) -> dict:
    key = jax.random.key(seed)
    ks = iter(jax.random.split(key, 40))
    nrm = lambda shape, scale: scale * jax.random.normal(next(ks), shape, jnp.float32)
    D, F, NH, NN = D_MODEL, FFN_HIDDEN, N_HYENA_LAYERS, N_NA_LAYERS
    base_decay = jnp.abs(jnp.linspace(math.log(HY_DECAY_TARGET) / HY_SLOW_DECAY_PCT,
                                      math.log(HY_DECAY_TARGET) / HY_FAST_DECAY_PCT, D, dtype=jnp.float32))
    return {
        "x": nrm((BATCH, SEQ, D), 1.0),
        "norm_mix": 1.0 + nrm((DEPTH, D), 0.02),
        "norm_ffn": 1.0 + nrm((DEPTH, D), 0.02),
        "norm_final": 1.0 + nrm((D,), 0.02),
        "hy_w_in": nrm((NH, D, 3 * D), D ** -0.5),
        "hy_b_in": nrm((NH, 3 * D), 0.02),
        "hy_conv_w": nrm((NH, HY_SHORT_CONV, 3 * D), HY_SHORT_CONV ** -0.5),
        "hy_conv_b": nrm((NH, 3 * D), 0.02),
        "hy_f_w1": nrm((NH, HY_EMB_DIM, HY_FILTER_WIDTH), HY_EMB_DIM ** -0.5),
        "hy_f_b1": nrm((NH, HY_FILTER_WIDTH), 0.02),
        "hy_f_w2": nrm((NH, HY_FILTER_WIDTH, HY_FILTER_WIDTH), HY_FILTER_WIDTH ** -0.5),
        "hy_f_b2": nrm((NH, HY_FILTER_WIDTH), 0.02),
        "hy_f_w3": nrm((NH, HY_FILTER_WIDTH, HY_FILTER_WIDTH), HY_FILTER_WIDTH ** -0.5),
        "hy_f_b3": nrm((NH, HY_FILTER_WIDTH), 0.02),
        "hy_f_freq": 1.0 + nrm((NH, HY_FILTER_WIDTH), 0.02),
        "hy_f_wout": nrm((NH, HY_FILTER_WIDTH, 2 * D), HY_FILTER_WIDTH ** -0.5),
        "hy_decay": base_decay * (1.0 + nrm((NH, 2, D), 0.05)),
        "hy_skip": nrm((NH, D), 0.5),
        "hy_w_out": nrm((NH, D, D), D ** -0.5),
        "hy_b_out": nrm((NH, D), 0.02),
        "na_w_qkv": nrm((NN, D, 3 * D), D ** -0.5),
        "na_b_qkv": nrm((NN, 3 * D), 0.02),
        "na_rpb": nrm((NN, NA_HEADS, 2 * NA_KH - 1, 2 * NA_KW - 1), 0.02),
        "na_w_o": nrm((NN, D, D), D ** -0.5),
        "na_b_o": nrm((NN, D), 0.02),
        "ffn_w_gate": nrm((DEPTH, D, F), D ** -0.5),
        "ffn_w_up": nrm((DEPTH, D, F), D ** -0.5),
        "ffn_w_down": nrm((DEPTH, F, D), F ** -0.5),
    }

def second_block(x, norm_mix, norm_ffn, norm_final,
              hy_w_in, hy_b_in, hy_conv_w, hy_conv_b, hy_f_w1, hy_f_b1, hy_f_w2, hy_f_b2,
              hy_f_w3, hy_f_b3, hy_f_freq, hy_f_wout, hy_decay, hy_skip, hy_w_out, hy_b_out,
              na_w_qkv, na_b_qkv, na_rpb, na_w_o, na_b_o,
              ffn_w_gate, ffn_w_up, ffn_w_down):
    for i in range(DEPTH):
        h = rmsnorm(x, norm_mix[i])
        j = i // N_MIXERS
        if i % N_MIXERS == 0:
            mixed = hyena_mixer(h, hy_w_in[j], hy_b_in[j], hy_conv_w[j], hy_conv_b[j],
                                hy_f_w1[j], hy_f_b1[j], hy_f_w2[j], hy_f_b2[j], hy_f_w3[j], hy_f_b3[j],
                                hy_f_freq[j], hy_f_wout[j], hy_decay[j], hy_skip[j],
                                hy_w_out[j], hy_b_out[j])
        else:
            mixed = na_mixer(h, na_w_qkv[j], na_b_qkv[j], na_rpb[j], na_w_o[j], na_b_o[j])
        x = x + mixed
        x = x + swiglu(rmsnorm(x, norm_ffn[i]), ffn_w_gate[i], ffn_w_up[i], ffn_w_down[i])
    return rmsnorm(x, norm_final)


def setup_inputs(seed=0):
    out = dict(first_inputs(seed))
    for name, value in second_inputs(seed + 1).items():
        if name != "x":
            out[name + "_2"] = value
    return out


def reference(
    x, mem, positions, g_mix, w_in, b_forget, w_sconv, w_pool, pool_scale, w_out, g_xa, g_mem,
    w_xq, w_xkv, w_xo, g_ffn, w_up, w_ffconv, w_down, g_final, norm_mix_2, norm_ffn_2,
    norm_final_2, hy_w_in_2, hy_b_in_2, hy_conv_w_2, hy_conv_b_2, hy_f_w1_2, hy_f_b1_2,
    hy_f_w2_2, hy_f_b2_2, hy_f_w3_2, hy_f_b3_2, hy_f_freq_2, hy_f_wout_2, hy_decay_2, hy_skip_2,
    hy_w_out_2, hy_b_out_2, na_w_qkv_2, na_b_qkv_2, na_rpb_2, na_w_o_2, na_b_o_2, ffn_w_gate_2,
    ffn_w_up_2, ffn_w_down_2,
):
    x = first_block(
        x, mem, positions, g_mix, w_in, b_forget, w_sconv, w_pool, pool_scale, w_out, g_xa,
        g_mem, w_xq, w_xkv, w_xo, g_ffn, w_up, w_ffconv, w_down, g_final,
    )
    return second_block(
        x, norm_mix_2, norm_ffn_2, norm_final_2, hy_w_in_2, hy_b_in_2, hy_conv_w_2, hy_conv_b_2,
        hy_f_w1_2, hy_f_b1_2, hy_f_w2_2, hy_f_b2_2, hy_f_w3_2, hy_f_b3_2, hy_f_freq_2,
        hy_f_wout_2, hy_decay_2, hy_skip_2, hy_w_out_2, hy_b_out_2, na_w_qkv_2, na_b_qkv_2,
        na_rpb_2, na_w_o_2, na_b_o_2, ffn_w_gate_2, ffn_w_up_2, ffn_w_down_2,
    )


_drawn_inputs = setup_inputs


def setup_inputs(seed=0):
    import zlib

    import numpy as np

    out = dict(_drawn_inputs(seed))
    spreads = {}
    factors = {'b_forget': 64.0,
     'pool_scale': 5.553,
     'g_xa': 8.0,
     'g_mem': 8.0,
     'g_ffn': 3.406,
     'norm_mix_2': 3.19,
     'norm_ffn_2': 13.656,
     'norm_final_2': 23.158,
     'hy_b_in_2': 3.112,
     'hy_conv_b_2': 3.36,
     'hy_f_b1_2': 8.0,
     'hy_f_b2_2': 8.0,
     'hy_f_b3_2': 8.0,
     'hy_f_freq_2': 8.0,
     'hy_b_out_2': 27.577}
    for name, (base, spread) in spreads.items():
        noise = np.random.default_rng([zlib.crc32(name.encode()), seed]).standard_normal(out[name].shape)
        drawn = base * np.exp(spread * noise) if base else spread * noise
        out[name] = __import__('jax').numpy.asarray(drawn.astype(out[name].dtype))
    for name, factor in factors.items():
        out[name] = (out[name] * factor).astype(out[name].dtype)
    return out
```

```python
from contextlib import ExitStack

import concourse.bass as bass
import numpy as np
from concourse import mybir

F32 = mybir.dt.float32
F32R = mybir.dt.float32r
I32 = mybir.dt.int32
ACT = mybir.ActivationFunctionType
ALU = mybir.AluOpType
AX = mybir.AxisListType

P = 128
D = 1024
T = 512
M = 256
KT = D // P
NT = T // P
HD = 64
FF = 2816
FT = FF // P
FFN_GROUPS = (8, 8, 6)
CHUNK = KT * P
EPS = 1e-6
BIG = 1e30
MAGIC = 12582912.0
INV_2PI = float(np.float32(1.0 / (2.0 * np.pi)))
C1 = 6.28125
C2 = float(np.float32(np.round((2.0 * np.pi - C1) * 2.0 ** 20) / 2.0 ** 20))
C3 = float(np.float32(2.0 * np.pi - C1 - C2))
PI_IN = 3.1415925
HALF_PI = float(np.float32(np.pi / 2))

SECTIONS = [("w_in", 10), ("k_mem", 4), ("dft_g0", 2), ("v_mem", 4), ("dft_g1", 2), ("w_out", 4), ("xq", 4), ("xo", 4)]
for g in range(3):
    SECTIONS += [(f"up1_{g}", FFN_GROUPS[g]), (f"down1_{g}", 4)]
SECTIONS += [("hy_in", 12), ("dft_s0", 2), ("dft_s1a", 1), ("idft_0", 2), ("dft_s1b", 1), ("idft_1", 2),
             ("hy_out", 4)]
for g in range(3):
    SECTIONS += [(f"up2_{g}", FFN_GROUPS[g]), (f"down2_{g}", 4)]
FIRST = {}
n_pairs = 0
for name, pairs in SECTIONS:
    FIRST[name] = n_pairs
    n_pairs += pairs
PAIRS = n_pairs

VEC = {}
n_cols = 0
for name, cols in [("g_mix", 8), ("g_xa", 8), ("g_mem", 8), ("g_ffn", 8), ("g_final", 8), ("norm_mix_2", 8), ("norm_ffn_2", 8),
                   ("norm_final_2", 8), ("sconv", 6), ("pool_scale", 2), ("ffconv", 3 * 2 * FT), ("hy_conv", 72),
                   ("hy_conv_b", 24), ("hy_b_in", 24), ("hy_skip", 8), ("hy_b_out", 8), ("inv_freq", 1), ("pool_inv", 2),
                   ("pool_edge", 32), ("b_forget", 16), ("neg_t", 8)]:
    VEC[name] = n_cols
    n_cols += cols
VECS = n_cols

MLP_JOB = (2, 8, 12)


def program(nc, a):
    with ExitStack() as ctx:
        base = 16512

        def at(name, shape, dt, offset):
            return nc.alloc_sbuf_tensor_at(name, shape, dt, offset=base + offset)

        def sem(name):
            return ctx.enter_context(nc.semaphore(name))

        KB = 1024
        h = at("h", [P, KT, T], F32, 0)
        op_hi = [at("opA_hi", [P, KT, T], F32R, 16 * KB), at("opB_hi", [P, KT, T], F32R, 48 * KB)]
        op_lo = [at("opA_lo", [P, KT, T], F32R, 32 * KB), at("opB_lo", [P, KT, T], F32R, 64 * KB)]
        raw = at("raw", [P, 2, 2 * CHUNK], F32, 80 * KB)
        w_hi = at("w_hi", [P, 2, 2 * CHUNK], F32R, 96 * KB)
        w_lo = at("w_lo", [P, 2, 2 * CHUNK], F32R, 112 * KB)
        o = 128 * KB
        vecs = at("vecs", [P, VECS], F32, o); o += 4 * ((VECS + 7) // 8 * 8)
        ident = at("ident", [P, P], F32, o); o += 512
        ones = at("ones", [P, P], F32, o); o += 512
        rstd = at("rstd", [P, T], F32, o); o += 2048
        acc = at("acc", [P, T], F32, o); o += 2048
        sq = at("sq", [P, 2, T], F32, o)
        scores = at("scores", [P, 3 * T], F32, o); o += 4096
        mean = at("mean", [P, T], F32, o); o += 2048
        low = at("low", [P, 32], F32, o); o += 128
        total = at("total", [P, 32], F32, o); o += 128
        inv_total = at("inv_total", [P, 32], F32, o); o += 128
        gate_w = at("gate_w", [P, KT, 4], F32, o); o += 128
        rstd_tok = at("rstd_tok", [P, 4], F32, o); o += 32
        log_f = at("log_f", [P, 4, 4], F32, o); o += 64
        gate_tmp = at("gate_tmp", [P, 4, 16], F32, o); o += 256
        c_tok = at("c_tok", [P, 4, 4], F32, o); o += 64
        filter_norm = at("filter_norm", [P, 8], F32, o); o += 32
        gvec_first = at("gvec_first", [P, KT], F32, o); o += 32
        c1 = (o + 31) // 32 * 32
        qk = at("qk", [P, 8, T], F32, c1)
        v_mem = at("v_mem", [P, 2, D], F32, c1)
        v_tok = at("v_tok", [P, NT, T], F32, c1 + 16 * KB)
        mg_hi = at("mg_hi", [P, KT, M], F32R, c1 + 24 * KB)
        mg_lo = at("mg_lo", [P, KT, M], F32R, c1 + 32 * KB)
        xq = at("xq", [P, KT, T], F32, c1 + 24 * KB)
        k_mem = at("k_mem", [P, KT, M], F32, c1 + 40 * KB)
        mem_raw = at("mem_raw", [P, KT, M], F32, 48 * KB + 4 * KB)
        e0 = c1 + 40 * KB
        c2 = c1 + 48 * KB
        feat = at("feat", [33, 2 * T], F32, c1 + 24 * KB)
        mlp_h = [at("mlp_h0", [64, 2, T], F32, c1 + 28 * KB), at("mlp_h1", [64, 2, T], F32, c1 + 32 * KB),
                 at("mlp_h2", [64, 2, T], F32, 0)]
        mlp_x = at("mlp_x", [64, 2, T], F32, c1 + 36 * KB)
        mlp_k = at("mlp_k", [64, T], F32, e0 + 22 * KB)
        mlp_w = at("mlp_w", [64, 3, 64], F32, e0 + 24 * KB)
        mlp_b = at("mlp_b", [64, 4], F32, e0 + 24 * KB + 768)
        cos_t = at("cos_t", [P, T], F32, e0)
        sin_t = at("sin_t", [P, T], F32, e0 + 2 * KB)
        rope_tmp = at("rope_tmp", [P, 2, T], F32, e0 + 4 * KB)
        v_raw = at("v_raw", [P, 2, T], F32, e0 + 8 * KB)
        pos = at("pos", [P, T], I32, e0 + 12 * KB)
        ang = at("ang", [P, T], F32, e0 + 14 * KB)
        turns = at("turns", [P, T], F32, e0 + 16 * KB)
        rot = at("rot", [P, P], F32, e0 + 18 * KB)
        pool_x = at("pool_x", [P, 2, 528], F32, e0 + 8 * KB)
        pool_a = at("pool_a", [P, 2, 528], F32, e0 + 8 * KB + 4224)
        pool_b = at("pool_b", [P, 2, 528], F32, e0 + 8 * KB + 8448)
        sc_m = at("sc_m", [P, 2, 516], F32, e0)
        sc_y = at("sc_y", [P, 2, T], F32, e0 + 8 * KB)
        sc_c = at("sc_c", [P, T], F32, e0 + 4128)
        tri = at("tri", [P, T], F32, 12 * KB)
        c_row = at("c_row", [4, T], F32, 14 * KB)
        v_stage = at("v_stage", [P, 2, M], F32, 12 * KB)
        probs_t = at("probs_t", [P, 2, T], F32, c2)
        mask = at("mask", [P, T], F32, c2 + 4 * KB)
        c_keys = at("c_keys", [P, T], F32, c2 + 6 * KB)
        bias = at("bias", [P, T], F32, c2 + 8 * KB)
        gen = at("gen", [P, 4, T], F32, c2 + 10 * KB)
        pool_w = at("pool_w", [P, 2, P], F32, e0 + 21 * KB)
        f_out = at("f_out", [64, 2, T], F32, 4 * KB)
        decay = at("decay", [P, 2, T], F32, 8 * KB)
        z_pad = at("z_pad", [P, 2, 2, 520], F32, c1)
        conv = at("conv", [P, 2, 2, T], F32, c1 + 9 * KB)
        s_feat = at("s_feat", [P, KT, T], F32, c1 + 18 * KB)
        x0_feat = at("x0_feat", [P, KT, T], F32, c1 + 34 * KB)
        g_spec = at("g_spec", [P, 2, 2, T], F32, c1 + 9 * KB)
        spec = at("spec", [P, 2, 4, T], F32, c1 + 50 * KB)
        hy_tmp = at("hy_tmp", [P, 2, 2, T], F32, c1)
        sq_next = at("sq_next", [P, 2, T], F32, c1 + 50 * KB)
        acc_next = at("acc_next", [P, T], F32, c1 + 54 * KB)

        ps = ctx.enter_context(nc.psum_tensor("ps", [P, 8, T], F32))
        g_dram = nc.dram_tensor("g_dram", [2, 4, P, 2 * T], F32, kind="Internal").ap()

        x_in = [sem(f"x_in{i}") for i in range(4)]
        raw_in = [sem("raw_in0"), sem("raw_in1")]
        vecs_in, small_in, mem_in = sem("vecs_in"), sem("small_in"), sem("mem_in")
        tri_in, pool_in, late_in, mask_in, x_again = (sem(n) for n in (
            "tri_in", "pool_in", "late_in", "mask_in", "x_again"))
        g_out = [sem("g_out0"), sem("g_out1")]
        g_back = [sem("g_back0"), sem("g_back1")]
        hi_ready, lo_ready = sem("hi_ready"), sem("lo_ready")
        chunk_done, bank_read = sem("chunk_done"), sem("bank_read")
        made_ones = sem("made_ones")
        next_hi, next_lo, squared, summed = sem("next_hi"), sem("next_lo"), sem("squared"), sem("summed")
        norm_sum, norm_mean, norm_root, norm_rstd = sem("norm_sum"), sem("norm_mean"), sem("norm_root"), sem("norm_rstd")
        misc_done, misc_read = sem("misc_done"), sem("misc_read")
        vstep, gate_root = sem("vector_step"), sem("gate_root")
        gate_folded = sem("gate_folded")
        mlp_arg, mlp_sin = sem("mlp_arg"), sem("mlp_sin")
        rope_arg, rope_sin, roped = sem("rope_arg"), sem("rope_sin"), sem("roped")
        gate_z, gate_exp, gate_log, gate_ready, c_ready = (sem(n) for n in ("gate_z", "gate_exp", "gate_log", "gate_ready", "c_ready"))
        sc_mul, sc_tap, sc_out, pooled = sem("sc_mul"), sem("sc_tap"), sem("sc_out"), sem("pooled")
        mix_hi, mix_lo = sem("mix_hi"), sem("mix_lo")
        mem_hi, mem_lo, mem_sq, mem_sum = sem("mem_hi"), sem("mem_lo"), sem("mem_sq"), sem("mem_sum")
        qk_done, masked, exped, probs_ready, transposed, pt_ready, pv_done, pv_hi, pv_lo = (sem(n) for n in (
            "qk_done", "masked", "exped", "probs_ready", "transposed", "pt_ready", "pv_done", "pv_hi", "pv_lo"))
        bcast_done, bcast_read = sem("bcast_done"), sem("bcast_read")
        vt_done, vt_read = sem("vt_done"), sem("vt_read")
        gen_done, gen_exp, gen_taps, gen_abs, gen_fold, gen_hi, gen_lo = (sem(n) for n in (
            "gen_done", "gen_exp", "gen_taps", "gen_abs", "gen_fold", "gen_hi", "gen_lo"))
        decay_abs, fnorm_done, fnorm_read, g_staged = (sem(n) for n in ("decay_abs", "fnorm_done", "fnorm_read", "g_staged"))
        tapped, conved, gated, act_prod, act_hi, act_lo = (sem(n) for n in (
            "tapped", "conved", "gated", "act_prod", "act_hi", "act_lo"))
        hz_bias, hz_tap, hz_done = sem("hz_bias"), sem("hz_tap"), sem("hz_done")
        st_done, st_hi, st_lo = sem("st_done"), sem("st_hi"), sem("st_lo")
        spec_mul, spec_sum, y_hi, y_lo = sem("spec_mul"), sem("spec_sum"), sem("y_hi"), sem("y_lo")
        squared_next, summed_next, gen_acc, acc_zero = sem("squared_next"), sem("summed_next"), sem("gen_acc"), sem("acc_zero")
        skip_s, hy_val, u_hi, u_lo = sem("skip_s"), sem("hy_val"), sem("u_hi"), sem("u_lo")
        first_rstd, h2_scaled = sem("first_rstd"), sem("h2_scaled")
        h2_made, out_made, stored = sem("h2_made"), sem("out_made"), sem("stored")
        zeroed = sem("zeroed")

        block = ctx.enter_context(nc.Block())

        def vec(name, i=0, n=1):
            return vecs[:, VEC[name] + i:VEC[name] + i + n]

        S_CHUNK = [2 * FIRST["dft_s0"] + j for j in range(4)] + [2 * FIRST[name] + j for name in ("dft_s1a", "dft_s1b") for j in range(2)]

        UNITS = [(s, i) for s in range(8) for i in range(NT)]
        SCORE_AT = [0, P, 3 * P, 6 * P]

        def unit_scores(u):
            start, tiles = (SCORE_AT[u % 4], u % 4 + 1) if u < 32 else (M * (u % 4), M // P)
            return scores[:, start:start + tiles * P]

        class Steps:

            def __init__(self, eng, counter):
                self.eng, self.counter, self.n, self.origin = eng, counter, 0, None

            def link(self, ins):
                ins.then_inc(self.counter, 1)
                self.n += 1
                self.eng.wait_ge(self.counter, self.n if self.origin is None else self.origin + self.n)

            def start(self, i, per):
                self.origin, self.per, self.before = i * per, per, self.n

            def end(self, count):
                assert self.n - self.before == self.per, (self.n - self.before, self.per)
                self.origin, self.n = None, self.before + count * self.per

        @block.sync
        def _(sp):
            for i in range(4):
                sp.dma_start(h[:, 2 * i:2 * i + 2, :], a["x_t"][:, 2 * i:2 * i + 2, :]).then_inc(x_in[i], 16)
                if i % 2 == 0:
                    sp.dma_start(raw[:, i // 2, :], a["weights"][i // 2]).then_inc(raw_in[i // 2], 16)
            with sp.Fori(1, PAIRS // 2) as m:
                for p in range(2):
                    sp.wait_ge(lo_ready, 2 * m + (p - 1))
                    sp.dma_start(raw[:, p, :], a["weights"][bass.ds(2 * m + p, 1)].rearrange("o p n -> p (o n)")
                                 ).then_inc(raw_in[p], 16)

        @block.gpsimd
        def _(pool):
            pool.dma_start(gate_w[:], a["gate_w"]).then_inc(small_in, 16)
            pool.dma_start(mlp_w[:], a["mlp_w"]).then_inc(small_in, 16)
            pool.dma_start(mlp_b[:], a["mlp_b"]).then_inc(small_in, 16)
            pool.dma_start(feat[:], a["feat"]).then_inc(small_in, 16)
            pool.dma_start(pos[:], a["positions"]).then_inc(small_in, 16)
            pool.dma_start(rot[:], a["rot"]).then_inc(small_in, 16)
            pool.dma_start(mem_raw[:], a["mem_t"]).then_inc(mem_in, 16)
            pool.wait_ge(misc_done, 2)
            pool.wait_ge(next_lo, KT)
            pool.wait_ge(squared, KT)
            pool.dma_start(tri[:], a["tri"]).then_inc(tri_in, 16)
            pool.dma_start(pool_w[:], a["pool_w"]).then_inc(pool_in, 16)
            pool.dma_start(f_out[:], a["f_out"][:, :, 0:T]).then_inc(late_in, 16)
            pool.dma_start(decay[:], a["decay"][:, :, 0:T]).then_inc(late_in, 16)
            pool.wait_ge(mix_lo, 4)
            pool.dma_start(mask[:], a["masks"][0]).then_inc(mask_in, 16)
            for step in range(8):
                half = step // 4
                if step % 4 == 0:
                    pool.wait_ge(norm_mean, 2)
                    if half:
                        pool.wait_ge(fnorm_read, 1)
                    nc.gpsimd.memset(acc[:], 0.0).then_inc(acc_zero, 1)
                    pool.wait_ge(acc_zero, half + 1)
                for d in range(2):
                    pool.wait_ge(gen_abs, 2 * step + d + 1)
                    nc.gpsimd.tensor_tensor(acc[:], acc[:], gen[:, 2 * d, :], ALU.add).then_inc(gen_acc, 1)
                    pool.wait_ge(gen_acc, 2 * step + d + 1)
                nc.gpsimd.tensor_tensor(gen[:, 0, :], gen[:, 1, :], gen[:, 3, :], ALU.add).then_inc(gen_fold, 1)
                nc.gpsimd.tensor_tensor(gen[:, 2, :], gen[:, 1, :], gen[:, 3, :], ALU.subtract).then_inc(gen_fold, 1)
                if step == 3:
                    pool.wait_ge(gen_exp, 8)
                    pool.wait_ge(gen_done, 4)
                    pool.dma_start(f_out[:], a["f_out"][:, :, T:2 * T]).then_inc(late_in, 16)
                    pool.dma_start(decay[:], a["decay"][:, :, T:2 * T]).then_inc(late_in, 16)
                    pool.wait_ge(masked, 16)
                    pool.dma_start(mask[:], a["masks"][1]).then_inc(mask_in, 16)
                if step % 4 == 3:
                    for j in range(4):
                        pool.wait_ge(g_staged, 4 * half + j + 1)
                        pool.dma_start(g_dram[half, j], gen[:, 2 * (j % 2):2 * (j % 2) + 2, :].rearrange("p a t -> p (a t)")
                                       ).then_inc(g_out[j % 2], 16)
            pool.wait_ge(gen_exp, 16)
            pool.wait_ge(gen_done, 8)
            pool.wait_ge(bcast_done, 4)
            pool.wait_ge(vt_done, 4)
            pool.dma_start(h[:], a["x_t"]).then_inc(x_again, 16)
            pool.wait_ge(first_rstd, 1)
            for k in range(KT):
                nc.gpsimd.tensor_tensor(h[:, k, :], h[:, k, :], acc_next[:], ALU.mult).then_inc(h2_scaled, 1)
            pool.wait_ge(h2_scaled, KT)
            for k in range(KT):
                nc.gpsimd.tensor_tensor(h[:, k, :], h[:, k, :], vec("g_final", k).to_broadcast([P, T]), ALU.mult
                                        ).then_inc(h2_made, 1)
            pool.wait_ge(h2_made, KT)
            for p in range(2):
                pool.wait_ge(g_out[p], 64)
            pool.wait_ge(hz_done, 16)

            def load_spectrum(n):
                pool.dma_start(g_spec[:, n % 2].rearrange("p a t -> p (a t)"), g_dram[n // 4, n % 4]).then_inc(g_back[n % 2], 16)

            load_spectrum(0)
            load_spectrum(1)
            for n in range(8):
                t = spec[:, n % 2]
                pool.wait_ge(spec_mul, n + 1)
                if n + 2 < 8:
                    load_spectrum(n + 2)
                nc.gpsimd.tensor_tensor(t[:, 0, :], t[:, 0, :], t[:, 1, :], ALU.subtract).then_inc(spec_sum, 1)
                nc.gpsimd.tensor_tensor(t[:, 2, :], t[:, 2, :], t[:, 3, :], ALU.add).then_inc(spec_sum, 1)

        @block.scalar
        def _(act):
            A = nc.scalar

            def split_hi(m, p, first=False):
                act.wait_ge(raw_in[p], 16 * m + 16)
                if not first:
                    act.wait_ge(chunk_done, 4 * m + (2 * p - 2))
                A.copy(w_hi[:, p, :], raw[:, p, :]).then_inc(hi_ready, 1)

            def split_after(g):
                if g + 2 < PAIRS:
                    split_hi((g + 2) // 2, g % 2)

            def root(i, width=T):
                act.wait_ge(norm_mean, i + 1)
                A.activation(mean[:, 0:width], mean[:, 0:width], ACT.Sqrt).then_inc(norm_root, 1)

            act.dma_start(vecs[:], a["vecs"]).then_inc(vecs_in, 16)
            act.dma_start(ident[:], a["ident"]).then_inc(vecs_in, 16)
            act.wait_ge(vecs_in, 32)
            for k in range(KT):
                act.wait_ge(x_in[k // 2], 16)
                A.activation(op_hi[0][:, k, :], h[:, k, :], ACT.Copy, scale=vec("g_mix", k)).then_inc(next_hi, 1)
                if k == 1:
                    split_hi(0, 0, first=True)
            for k in range(KT):
                if k >= 2:
                    act.wait_ge(summed, k - 1)
                A.activation(sq[:, k % 2, :], h[:, k, :], ACT.Square).then_inc(squared, 1)
                if k == 1:
                    split_hi(0, 1, first=True)
            root(0)
            act.wait_ge(gate_z, 1)
            A.activation(rstd_tok[:], rstd_tok[:], ACT.Sqrt).then_inc(gate_root, 1)

            def mlp_sins(layer):
                for d in range(2):
                    act.wait_ge(mlp_arg, 2 * layer + d + 1)
                    A.activation(mlp_h[layer][:, d, :], mlp_x[:, d, :], ACT.Sin).then_inc(mlp_sin, 1)

            split_after(0)
            mlp_sins(0)
            split_after(1)
            for r, table in enumerate((sin_t, cos_t)):
                act.wait_ge(rope_arg, r + 1)
                A.activation(table[:], ang[:] if r else turns[:], ACT.Sin).then_inc(rope_sin, 1)
            act.wait_ge(gate_z, 2)
            A.activation(gate_tmp[:, 1, :], gate_tmp[:, 1, :], ACT.Exp, scale=-1.0).then_inc(gate_exp, 1)
            act.wait_ge(gate_exp, 1)
            A.activation(gate_tmp[:, 2, :], gate_tmp[:, 1, :], ACT.Ln, bias=1.0).then_inc(gate_log, 1)
            split_after(2)
            act.wait_ge(mem_in, 16)
            act.wait_ge(summed, KT)
            for r in range(4):
                if r >= 2:
                    act.wait_ge(mem_sum, r - 1)
                A.activation(sq[:, r % 2, :], mem_raw[:, 2 * r:2 * r + 2, :].rearrange("p k t -> p (k t)"),
                             ACT.Square).then_inc(mem_sq, 1)
            split_after(3)
            mlp_sins(1)
            split_after(4)
            mlp_sins(2)
            act.wait_ge(misc_done, 14)
            act.wait_ge(mlp_sin, 6)
            for k in range(KT):
                A.activation(mg_hi[:, k, :], mem_raw[:, k, :], ACT.Copy, scale=vec("g_mem", k)).then_inc(mem_hi, 1)
            split_after(5)
            split_after(6)
            for t in range(2):
                act.wait_ge(sc_mul, t + 1)
                A.activation(sc_y[:, t, :], sc_m[:, t, 2:2 + T], ACT.Copy, scale=vec("sconv", 2 * 2 + t)).then_inc(sc_tap, 1)
                split_after(7 + t)
                if t == 0:
                    for u in range(2):
                        act.wait_ge(misc_done, 19 + u)
                        A.activation(op_hi[1][:, 6 + u, :], ps[:, 6 + u % 2, :], ACT.Copy, scale=vec("pool_scale", u)
                                     ).then_inc(mix_hi, 1)
            split_after(9)
            for t in range(2):
                act.wait_ge(sc_out, t + 1)
                A.copy(op_hi[1][:, t, :], sc_y[:, t, :]).then_inc(mix_hi, 1)
            root(1, M)

            def exp_unit(u):
                act.wait_ge(masked, u + 1)
                A.activation(unit_scores(u), unit_scores(u), ACT.Exp, scale=-1.0,
                             bias=low[:, u:u + 1], accum_out=total[:, u:u + 1]).then_inc(exped, 1)

            def copy_transposed(u, width):
                act.wait_ge(transposed, u + 1)
                if u >= 2:
                    act.wait_ge(pv_done, u - 1)
                A.copy(probs_t[:, u % 2, 0:width], ps[:, 6, 0:width]).then_inc(pt_ready, 1)

            def out_tile(t):
                act.wait_ge(pv_done, 8 * (t - 1))
                A.copy(op_hi[1][:, t, :], ps[:, 7, :]).then_inc(pv_hi, 1)

            exp_unit(0)
            for u, (s, i) in enumerate(UNITS):
                half, n = s // 4, s % 4
                g = (FIRST["k_mem"] if s < 4 else FIRST["v_mem"] - 4) + s
                if u + 1 < len(UNITS) and u != 15:
                    exp_unit(u + 1)
                if u:
                    copy_transposed(u - 1, ((u - 1) % 4 + 1) * P)
                if i == 0:
                    act.wait_ge(decay_abs, half + 1)
                    if s > 0:
                        act.wait_ge(gen_lo, 2 * s)
                    if s == 4:
                        for p in range(2):
                            act.wait_ge(g_out[p], 32)
                    for d in range(2):
                        A.activation(gen[:, 2 * d, :], decay[:, d, :], ACT.Exp, scale=vec("neg_t", 4 * d + n)).then_inc(gen_exp, 1)
                if i == 1:
                    if n:
                        split_after(g - 1)
                    act.wait_ge(gen_taps, s + 1)
                    for d in range(2):
                        A.activation(gen[:, 2 * d, :], gen[:, 2 * d + 1, :], ACT.Abs).then_inc(gen_abs, 1)
                if i == 3:
                    for d in range(2):
                        act.wait_ge(gen_fold, 2 * s + d + 1)
                        if s == 4:
                            act.wait_ge(chunk_done, 2 * FIRST["dft_g0"] + 4)
                        A.copy(op_hi[0][:, 4 * d + n, :], gen[:, 2 * d, :]).then_inc(gen_hi, 1)
                if u in (9, 17, 25):
                    out_tile(2 + (u - 9) // 8)
                if u == 31:
                    copy_transposed(31, T)
                    out_tile(5)
                if u % 16 == 15:
                    split_after(g)
                    split_after(g + 1)
                    split_after(g + 2)
                if u == 15:
                    exp_unit(16)

            def tail(first, gname, dst, isq, iop, unroll=False):
                def two(m, p, d, n):
                    for j in range(2):
                        if j == 1 and p == 0 and not (unroll and 2 * m + 2 >= PAIRS):
                            split_hi(m + 1, p)
                        act.wait_ge(bank_read, 4 * m + (2 * p + j + 1))
                        act.wait_ge(summed, n + (j - 1 + 8 * isq))
                        tile = d + j if isinstance(d, int) else None
                        if gname:
                            if tile is None:
                                hi = op_hi[dst][:, bass.ds(d + j, 1), :].rearrange("p a t -> p (a t)")
                                g = (gvec_first[:, bass.ds(d + j, 1)] if gname == "gvec_first" else
                                     vecs[:, bass.ds(d + (VEC[gname] + j), 1)])
                            else:
                                hi = op_hi[dst][:, tile, :]
                                g = vec(gname, tile)
                            A.activation(hi, h[:, bass.ds(d + j, 1), :].rearrange("p a t -> p (a t)"), ACT.Copy,
                                         scale=g).then_inc(next_hi, 1)
                        A.activation(sq[:, j, :], h[:, bass.ds(d + j, 1), :].rearrange("p a t -> p (a t)"),
                                     ACT.Square).then_inc(squared, 1)
                        if gname == "gvec_first":
                            A.activation(sq_next[:, j, :], h[:, bass.ds(d + j, 1), :].rearrange("p a t -> p (a t)"), ACT.Square,
                                         scale=vecs[:, bass.ds(d + (VEC["g_final"] + j), 1)]).then_inc(squared_next, 1)
                if unroll:
                    for q in range(4):
                        two((FIRST[first] + q) // 2, q % 2, 2 * q, 2 * q)
                        if q % 2:
                            split_after(FIRST[first] + q)
                else:
                    with act.Fori(0, 2) as i:
                        for p in range(2):
                            m = FIRST[first] // 2 + i
                            two(m, p, 4 * i + 2 * p, 4 * i + 2 * p)
                            if p:
                                split_hi(m + 1, p)

            tail("w_out", "g_xa", 0, 1, 1)
            root(2)

            def exp_x(u):
                act.wait_ge(masked, 32 + u + 1)
                A.activation(unit_scores(32 + u), ps[:, 4 + u % 2, 0:M], ACT.Exp, scale=-1.0,
                             bias=low[:, u:u + 1], accum_out=total[:, u:u + 1]).then_inc(exped, 1)

            split_after(FIRST["xq"])
            split_after(FIRST["xq"] + 1)
            exp_x(0)
            for u in range(18):
                if u + 1 < 16:
                    exp_x(u + 1)
                if 1 <= u <= 16:
                    copy_transposed(32 + u - 1, M)
                if u >= 2:
                    v = u - 2
                    act.wait_ge(pv_done, 32 + v + 1)
                    A.copy(op_hi[1][:, 2 * (v // 4):2 * (v // 4) + 2, (v % 4) * P:(v % 4 + 1) * P],
                           ps[:, 7, 0:M].rearrange("p (a t) -> p a t", a=2)).then_inc(pv_hi, 1)
                if u in (3, 7):
                    split_after(FIRST["xq"] + 2 + u // 4)

            tail("xo", "g_ffn", 0, 2, 2)
            root(3)

            def ffn_up(section, count, base_tiles, gated_only):
                with act.Fori(0, count // 2) as i:
                    for p in range(2):
                        m = FIRST[section] // 2 + i
                        n = 2 * i + (base_tiles + p)
                        if not gated_only:
                            for j in range(2):
                                if j == 1:
                                    split_hi(m + 1, p)
                                act.wait_ge(bank_read, 4 * m + (2 * p + j + 1))
                                A.activation(conv[:, p, j, :], z_pad[:, p, j, 2:2 + T], ACT.Copy,
                                             scale=vecs[:, bass.ds(2 * i + (VEC["ffconv"] + 2 * 2 * FT + j * FT + base_tiles + p), 1)]
                                             ).then_inc(tapped, 1)
                            act.wait_ge(conved, n + 1)
                            A.activation(conv[:, p, 1, :], conv[:, p, 1, :], ACT.Silu).then_inc(gated, 1)
                        else:
                            act.wait_ge(bank_read, 4 * m + (2 * p + 1))
                            A.activation(conv[:, p, 0, :], z_pad[:, p, 0, 0:T], ACT.Silu).then_inc(gated, 1)
                            split_hi(m + 1, p)
                        act.wait_ge(act_prod, n + (FT * gated_only + 1))
                        A.copy(op_hi[1][:, bass.ds(2 * i + p, 1), :].rearrange("p a t -> p (a t)"),
                               conv[:, p, 0, :] if not gated_only else conv[:, p, 1, :]).then_inc(act_hi, 1)

            def ffn_down(section):
                with act.Fori(0, 2) as i:
                    for p in range(2):
                        split_hi(FIRST[section] // 2 + i + 1, p)

            for g in range(3):
                ffn_up(f"up1_{g}", FFN_GROUPS[g], 8 * g, 0)
                if g < 2:
                    ffn_down(f"down1_{g}")
            tail("down1_2", "gvec_first", 0, 3, 3, unroll=False)
            root(4)
            root(5)

            def hy_taps(i, p):
                m = FIRST["hy_in"] // 2 + i
                for j in range(2):
                    if j == 1:
                        split_hi(m + 1, p)
                    f = 4 * i + (2 * p + j)
                    act.wait_ge(bank_read, 4 * m + (2 * p + j + 1))
                    A.activation(z_pad[:, p, j, 1:1 + T], z_pad[:, p, j, 1:1 + T], ACT.Identity,
                                 bias=vecs[:, bass.ds(f + VEC["hy_b_in"], 1)]).then_inc(hz_bias, 1)
                    act.wait_ge(hz_bias, f + 1)
                    A.activation(conv[:, p, j, :], z_pad[:, p, j, 1:1 + T], ACT.Identity,
                                 scale=vecs[:, bass.ds(f + (VEC["hy_conv"] + 24), 1)],
                                 bias=vecs[:, bass.ds(f + VEC["hy_conv_b"], 1)]).then_inc(hz_tap, 1)

            with act.Fori(0, 4) as i:
                for p in range(2):
                    hy_taps(i, p)
            for q in range(4):
                hy_taps(4 + q // 2, q % 2)
                for n in (2 * q, 2 * q + 1):
                    act.wait_ge(st_done, n + 1)
                    A.copy(op_hi[1][:, n, :], ps[:, 4 + n % 4, :]).then_inc(st_hi, 1)
            def spectrum_hi(n):
                if n == 4:
                    act.wait_ge(chunk_done, 2 * FIRST["idft_0"] + 4)
                for r in range(2):
                    act.wait_ge(spec_sum, 2 * n + r + 1)
                    A.copy(op_hi[0][:, 2 * (n % 4) + r, :], spec[:, n % 2, 2 * r, :]).then_inc(y_hi, 1)

            def skip(c):
                if c >= 2:
                    act.wait_ge(hy_val, c - 1)
                A.activation(hy_tmp[:, c % 2, 0, :], s_feat[:, c, :], ACT.Copy, scale=vec("hy_skip", c)).then_inc(skip_s, 1)

            def hyena_out_hi(half):
                for c in range(4 * half, 4 * half + 4):
                    act.wait_ge(hy_val, c + 1)
                    A.copy(op_hi[1][:, c, :], hy_tmp[:, c % 2, 1, :]).then_inc(u_hi, 1)
                    if c + 2 < 8:
                        skip(c + 2)

            s0, s1a, i0, s1b, i1 = (FIRST[name] for name in ("dft_s0", "dft_s1a", "idft_0", "dft_s1b", "idft_1"))
            spectrum_hi(0)
            split_after(s0)
            spectrum_hi(1)
            spectrum_hi(2)
            split_after(s0 + 1)
            spectrum_hi(3)
            split_after(s1a)
            skip(0)
            skip(1)
            split_after(i0)
            spectrum_hi(4)
            spectrum_hi(5)
            split_after(i0 + 1)
            hyena_out_hi(0)
            spectrum_hi(6)
            split_after(s1b)
            spectrum_hi(7)
            split_after(i1)
            hyena_out_hi(1)
            split_after(i1 + 1)
            tail("hy_out", "norm_ffn_2", 0, 4, 4)
            root(6)
            for g in range(3):
                ffn_up(f"up2_{g}", FFN_GROUPS[g], 8 * g, 1)
                if g < 2:
                    ffn_down(f"down2_{g}")
            tail("down2_2", None, None, 5, None, unroll=True)
            root(7)
            for q in range(4):
                act.wait_ge(out_made, 2 * q + 2)
                act.dma_start(a["out"][:, 2 * q:2 * q + 2, :], h[:, 2 * q:2 * q + 2, :]).then_inc(stored, 16)
            act.wait_ge(stored, 64)

        @block.vector
        def _(dve):
            V = nc.vector
            S = Steps(dve, vstep)

            def split_lo(m, p):
                dve.wait_ge(hi_ready, 2 * m + (p + 1))
                V.tensor_tensor(w_lo[:, p, :], raw[:, p, :], w_hi[:, p, :].bitcast(F32), ALU.subtract).then_inc(lo_ready, 1)

            def split_after(g):
                if g + 2 < PAIRS:
                    split_lo((g + 2) // 2, g % 2)

            def product(c):
                dve.wait_ge(chunk_done, c + 1)

            def evac(c, out, scale=None, width=T, bank=None):
                product(c)
                bank = c % 4 if bank is None else bank
                if scale is None:
                    return V.tensor_tensor(out, ps[:, bank, 0:width], rstd[:, 0:width], ALU.mult).then_inc(bank_read, 1)
                return V.scalar_tensor_tensor(out, ps[:, bank, 0:width], scale, rstd[:, 0:width], ALU.mult,
                                              ALU.mult).then_inc(bank_read, 1)

            def misc(j):
                dve.wait_ge(misc_done, j + 1)
                return ps[:, 6 + j % 2, :]

            def finish_norm(i, src, width=T):
                V.tensor_scalar(mean[:, 0:width], src, 1.0 / D, EPS, ALU.mult, ALU.add).then_inc(norm_mean, 1)
                dve.wait_ge(norm_root, i + 1)
                V.reciprocal(rstd[:, 0:width], mean[:, 0:width]).then_inc(norm_rstd, 1)
                dve.wait_ge(norm_rstd, i + 1)

            def lo_part(out, src, hi):
                return V.tensor_tensor(out, src, hi.bitcast(F32), ALU.subtract)

            V.memset(ones[:], 1.0).then_inc(made_ones, 1)
            S.link(V.memset(acc[:], 0.0))
            dve.wait_ge(vecs_in, 32)
            for k in range(KT):
                dve.wait_ge(next_hi, k + 1)
                V.scalar_tensor_tensor(op_lo[0][:, k, :], h[:, k, :], vec("g_mix", k), op_hi[0][:, k, :].bitcast(F32),
                                       ALU.mult, ALU.subtract).then_inc(next_lo, 1)
                if k == 1:
                    split_lo(0, 0)
            for k in range(KT):
                if k == 2:
                    split_lo(0, 1)
                dve.wait_ge(squared, k + 1)
                V.tensor_tensor(acc[:], acc[:], sq[:, k % 2, :], ALU.add).then_inc(summed, 1)
                dve.wait_ge(summed, k + 1)
            dve.wait_ge(small_in, 96)
            V.tensor_tensor(gate_w[:], gate_w[:], vec("g_mix", 0, 8).unsqueeze(2).to_broadcast([P, KT, 4]),
                            ALU.mult).then_inc(gate_folded, 1)
            bank = misc(0)
            V.tensor_scalar(mean[:], bank, 1.0 / D, EPS, ALU.mult, ALU.add).then_inc(norm_mean, 1)
            dve.wait_ge(norm_mean, 1)
            V.engine_nop().then_inc(misc_read, 1)
            dve.wait_ge(norm_root, 1)
            V.reciprocal(rstd[:], mean[:]).then_inc(norm_rstd, 1)
            dve.wait_ge(norm_rstd, 1)
            bank = misc(1)
            V.tensor_scalar(rstd_tok[:], bank[:, 16:20], 1.0 / D, EPS, ALU.mult, ALU.add).then_inc(gate_z, 1)
            S.link(V.tensor_copy(gate_tmp[:, 0, :], bank[:, 0:16]))
            V.engine_nop().then_inc(misc_read, 1)
            for j in range(2):
                evac(j, qk[:, j, :], -0.125)
            split_after(0)

            def reduce_turns(out, x, k, offset=0.0):
                if offset:
                    S.link(V.tensor_scalar(k, x, INV_2PI, offset, ALU.mult, ALU.add))
                    S.link(V.tensor_scalar(k, k, MAGIC, None, ALU.add))
                else:
                    S.link(V.tensor_scalar(k, x, INV_2PI, MAGIC, ALU.mult, ALU.add))
                S.link(V.tensor_scalar(k, k, MAGIC, None, ALU.subtract))
                S.link(V.scalar_tensor_tensor(out, k, -C1, x, ALU.mult, ALU.add))
                S.link(V.scalar_tensor_tensor(out, k, -C2, out, ALU.mult, ALU.add))
                S.link(V.scalar_tensor_tensor(out, k, -C3, out, ALU.mult, ALU.add))

            def mlp_args(layer):
                for d in range(2):
                    bank = misc(MLP_JOB[layer] + d)
                    x = mlp_x[:, d, :]
                    if layer > 0:
                        dve.wait_ge(mlp_sin, 2 * layer)
                    V.tensor_scalar(x, bank[0:64, :], mlp_b[:, layer:layer + 1], mlp_b[:, 3:4], ALU.add,
                                    ALU.mult).then_inc(misc_read, 1)
                    dve.wait_ge(misc_read, MLP_JOB[layer] + d + 1)
                    reduce_turns(x, x, mlp_k[:])
                    V.tensor_scalar(x, x, PI_IN, -PI_IN, ALU.min, ALU.max).then_inc(mlp_arg, 1)

            mlp_args(0)
            for j in range(2):
                evac(2 + j, qk[:, 2 + j, :])
            split_after(1)
            S.link(V.tensor_copy(ang[:], pos[:]))
            S.link(V.tensor_scalar(ang[:], ang[:], vec("inv_freq"), None, ALU.mult))
            reduce_turns(turns[:], ang[:], rope_tmp[:, 0, :])
            V.tensor_scalar(turns[:], turns[:], PI_IN, -PI_IN, ALU.min, ALU.max).then_inc(rope_arg, 1)
            reduce_turns(ang[:], ang[:], rope_tmp[:, 0, :], 0.25)
            S.link(V.tensor_scalar(ang[:], ang[:], HALF_PI, None, ALU.add))
            V.tensor_scalar(ang[:], ang[:], PI_IN, -PI_IN, ALU.min, ALU.max).then_inc(rope_arg, 1)
            dve.wait_ge(gate_root, 1)
            S.link(V.reciprocal(rstd_tok[:], rstd_tok[:]))
            for i in range(NT):
                last = V.scalar_tensor_tensor(gate_tmp[:, 0, 4 * i:4 * i + 4], gate_tmp[:, 0, 4 * i:4 * i + 4],
                                              rstd_tok[:, i:i + 1], vec("b_forget", 4 * i, 4), ALU.mult, ALU.add)
            S.link(last)
            V.scalar_tensor_tensor(gate_tmp[:, 1, :], gate_tmp[:, 0, :], -1.0, gate_tmp[:, 0, :], ALU.mult, ALU.max).then_inc(gate_z, 1)
            for j in range(2):
                evac(4 + j, v_raw[:, j, :])
            split_after(2)

            def rope(first_tile, job):
                dve.wait_ge(rope_sin, 2)
                for j in range(2):
                    t = qk[:, first_tile + j, :]
                    bank = misc(job + j)
                    V.tensor_tensor(rope_tmp[:, j, :], bank, sin_t[:], ALU.mult).then_inc(misc_read, 1)
                    dve.wait_ge(misc_read, job + j + 1)
                    S.link(V.tensor_tensor(t, t, cos_t[:], ALU.mult))
                    V.tensor_tensor(t, t, rope_tmp[:, j, :], ALU.add).then_inc(roped, 1)

            rope(0, 4)
            S.link(V.memset(acc[:], 0.0))
            for r in range(4):
                dve.wait_ge(mem_sq, r + 1)
                V.tensor_tensor(acc[:], acc[:], sq[:, r % 2, :], ALU.add).then_inc(mem_sum, 1)
                dve.wait_ge(mem_sum, r + 1)
            V.tensor_tensor(acc[:, 0:M], acc[:, 0:M], acc[:, M:2 * M], ALU.add).then_inc(mem_sum, 1)
            dve.wait_ge(gate_log, 1)
            V.scalar_tensor_tensor(log_f[:].rearrange("p i h -> p (i h)"), gate_tmp[:, 0, :], 0.0, gate_tmp[:, 2, :], ALU.min,
                                   ALU.subtract).then_inc(gate_ready, 1)
            rope(2, 6)
            for j in range(2):
                evac(6 + j, qk[:, 4 + j, :], -0.125)
            split_after(3)
            mlp_args(1)

            def v_tokens(m, job):
                for b in range(2):
                    bank = misc(job + b)
                    V.tensor_copy(v_tok[:, 2 * b:2 * b + 2, M * m:M * m + M], bank.rearrange("p (i f) -> p i f", i=2)
                                  ).then_inc(misc_read, 1)

            v_tokens(0, 10)
            for j in range(2):
                evac(8 + j, qk[:, 6 + j, :])
            split_after(4)
            mlp_args(2)
            bank = misc(14)
            V.tensor_copy(c_tok[:].rearrange("p i h -> p (i h)"), bank[:, 0:16]).then_inc(misc_read, 1)
            bank = misc(15)
            V.tensor_copy(c_row[:], bank[0:4, :]).then_inc(misc_read, 1)
            for j in range(2):
                evac(10 + j, v_raw[:, j, :])
            split_after(5)
            for k in range(KT):
                dve.wait_ge(mem_hi, k + 1)
                V.scalar_tensor_tensor(mg_lo[:, k, :], mem_raw[:, k, :], vec("g_mem", k), mg_hi[:, k, :].bitcast(F32),
                                       ALU.mult, ALU.subtract).then_inc(mem_lo, 1)
            v_tokens(1, 16)
            V.memset(pool_x[:, :, 0:16], 0.0)
            V.memset(pool_a[:, :, 0:16], 0.0)
            S.link(V.memset(pool_b[:, :, 0:16], 0.0))
            for j in range(2):
                evac(12 + j, pool_x[:, j, 16:16 + T])
            split_after(6)
            dve.wait_ge(bank_read, 14)
            S.link(V.tensor_tensor(pool_a[:, :, 1:], pool_x[:, :, 1:], pool_x[:, :, 0:527], ALU.add))
            S.link(V.tensor_tensor(pool_b[:, :, 3:], pool_a[:, :, 3:], pool_a[:, :, 1:526], ALU.add))
            S.link(V.tensor_copy(pool_a[64:128, 0, 16:], pool_b[64:128, 0, 16:]))
            S.link(V.tensor_tensor(pool_a[:, 1, 7:], pool_b[:, 1, 7:], pool_b[:, 1, 3:524], ALU.add))
            S.link(V.tensor_tensor(pool_b[64:128, 1, 15:], pool_a[64:128, 1, 15:], pool_a[64:128, 1, 7:520], ALU.add))
            S.link(V.tensor_copy(pool_a[64:128, 1, 16:], pool_b[64:128, 1, 16:]))
            for j in range(2):
                S.link(V.tensor_tensor(pool_b[:, j, 0:16], pool_a[:, j, 16:32], vec("pool_edge", 16 * j, 16), ALU.mult))
                S.link(V.scalar_tensor_tensor(pool_a[:, j, 16:], pool_a[:, j, 16:], vec("pool_inv", j), pool_x[:, j, 16:],
                                              ALU.mult, ALU.subtract))
                V.tensor_tensor(pool_a[:, j, 16:32], pool_b[:, j, 0:16], pool_x[:, j, 16:32], ALU.subtract).then_inc(pooled, 1)
            V.memset(sc_m[:, :, 0:2], 0.0)
            for t in range(2):
                evac(14 + 2 * t, sc_c[:])
                evac(15 + 2 * t, sc_m[:, t, 2:2 + T])
                dve.wait_ge(bank_read, 16 + 2 * t)
                V.tensor_tensor(sc_m[:, t, 2:2 + T], sc_m[:, t, 2:2 + T], sc_c[:], ALU.mult).then_inc(sc_mul, 1)
                dve.wait_ge(sc_mul, t + 1)
                split_after(7 + t)
                if t == 0:
                    for u in range(2):
                        bank = misc(18 + u)
                        dve.wait_ge(mix_hi, u + 1)
                        V.scalar_tensor_tensor(op_lo[1][:, 6 + u, :], bank, vec("pool_scale", u),
                                               op_hi[1][:, 6 + u, :].bitcast(F32), ALU.mult, ALU.subtract).then_inc(mix_lo, 1)
                        dve.wait_ge(mix_lo, u + 1)
                        V.engine_nop().then_inc(misc_read, 1)
            for t in range(2):
                dve.wait_ge(sc_tap, t + 1)
                S.link(V.scalar_tensor_tensor(sc_y[:, t, :], sc_m[:, t, 1:1 + T], vec("sconv", 2 + t), sc_y[:, t, :],
                                              ALU.mult, ALU.add))
                S.link(V.scalar_tensor_tensor(sc_y[:, t, :], sc_m[:, t, 0:T], vec("sconv", t), sc_y[:, t, :],
                                              ALU.mult, ALU.add))
            for t in range(2):
                S.link(V.tensor_tensor(sc_y[:, t, :], sc_y[:, t, :], rstd[:], ALU.mult))
                product(18 + t)
                S.link(V.tensor_tensor(sc_y[:, t, :], sc_y[:, t, :], ps[:, (18 + t) % 4, :], ALU.mult))
                V.engine_nop().then_inc(sc_out, 1)
                dve.wait_ge(sc_out, t + 1)
                V.engine_nop().then_inc(bank_read, 1)
            split_after(9)
            for t in range(2):
                dve.wait_ge(mix_hi, 3 + t)
                lo_part(op_lo[1][:, t, :], sc_y[:, t, :], op_hi[1][:, t, :]).then_inc(mix_lo, 1)
            bank = misc(20)
            finish_norm(1, bank[:, 0:M], M)
            V.engine_nop().then_inc(misc_read, 1)
            dve.wait_ge(late_in, 32)
            V.scalar_tensor_tensor(decay[:], decay[:], -1.0, decay[:], ALU.mult, ALU.max).then_inc(decay_abs, 1)

            def mask_unit(u):
                s, i = UNITS[u]
                n = (i + 1) * P
                strip = mask[:, (3 - i) * P:T]
                if s >= 4:
                    if i == 0:
                        dve.wait_ge(bcast_done, s - 3)
                        V.tensor_copy(c_keys[:], ps[:, 3, :]).then_inc(bcast_read, 1)
                        dve.wait_ge(bcast_read, s - 3)
                    if u == 16:
                        dve.wait_ge(mask_in, 32)
                    if u > 16:
                        dve.wait_ge(masked, u)
                    S.link(V.scalar_tensor_tensor(bias[:, 0:n], c_keys[:, 0:n], c_tok[:, i, s - 4:s - 3], strip,
                                                  ALU.subtract, ALU.add))
                    strip = bias[:, 0:n]
                if u == 0:
                    dve.wait_ge(mask_in, 16)
                dve.wait_ge(qk_done, u + 1)
                if u >= 4:
                    dve.wait_ge(transposed, u - 3)
                V.tensor_tensor_reduce(unit_scores(u), ps[:, 4 + u % 2, 0:n], strip, 1.0, 3e38, ALU.add, ALU.min,
                                       low[:, u:u + 1]).then_inc(masked, 1)

            def normalise(u, v):
                dve.wait_ge(exped, u + 1)
                S.link(V.reciprocal(inv_total[:, v:v + 1], total[:, v:v + 1]))
                V.tensor_scalar(unit_scores(u), unit_scores(u), inv_total[:, v:v + 1], None, ALU.mult).then_inc(probs_ready, 1)

            mask_unit(0)
            for u, (s, i) in enumerate(UNITS):
                half, n = s // 4, s % 4
                g = (FIRST["k_mem"] if s < 4 else FIRST["v_mem"] - 4) + s
                if u + 1 < len(UNITS) and u != 15:
                    mask_unit(u + 1)
                normalise(u, u)
                if i == 0:
                    dve.wait_ge(gen_done, s + 1)
                    for d in range(2):
                        dve.wait_ge(gen_exp, 2 * s + d + 1)
                        S.link(V.tensor_tensor(gen[:, 2 * d + 1, :], ps[:, 2 + d, :], gen[:, 2 * d, :], ALU.mult))
                        if d == 1 and n == 0:
                            S.link(V.memset(gen[0:1, 3, :], 0.0))
                    V.engine_nop().then_inc(gen_taps, 1)
                if i == 1 and n:
                    split_after(g - 1)
                if i % 2 == 1:
                    c = 2 * g + i // 2
                    dst = k_mem[:, 2 * s + i // 2, :] if s < 4 else v_stage[:, i // 2, :]
                    if s > 4:
                        dve.wait_ge(vt_done, s - 4)
                    evac(c, dst, None, M, bank=c % 2)
                if i == 3:
                    for d in range(2):
                        dve.wait_ge(gen_hi, 2 * s + d + 1)
                        lo_part(op_lo[0][:, 4 * d + n, :], gen[:, 2 * d, :], op_hi[0][:, 4 * d + n, :]).then_inc(gen_lo, 1)
                    dve.wait_ge(gen_lo, 2 * s + 2)
                if u in (9, 17, 25, 31):
                    t = 2 + (u - 7) // 8
                    dve.wait_ge(pv_hi, t - 1)
                    lo_part(op_lo[1][:, t, :], ps[:, 7, :], op_hi[1][:, t, :]).then_inc(pv_lo, 1)
                if i == 3 and s >= 4:
                    dve.wait_ge(vt_done, s - 3)
                    V.tensor_copy(v_mem[:, :, (s - 4) * M:(s - 3) * M], ps[:, 2, :].rearrange("p (b f) -> p b f", b=2)
                                  ).then_inc(vt_read, 1)
                if i == 3 and n == 3:
                    dve.wait_ge(fnorm_done, half + 1)
                    V.reciprocal(filter_norm[:, 4 * half:4 * half + 4], ps[:, 3, 0:4]).then_inc(fnorm_read, 1)
                    if half == 0:
                        dve.wait_ge(late_in, 64)
                        V.scalar_tensor_tensor(decay[:], decay[:], -1.0, decay[:], ALU.mult, ALU.max).then_inc(decay_abs, 1)
                    for j in range(4):
                        c = 2 * FIRST[f"dft_g{half}"] + j
                        if j == 0:
                            split_after(FIRST[f"dft_g{half}"] - 1)
                        product(c)
                        if j >= 2:
                            dve.wait_ge(g_out[j % 2], 32 * half + 16)
                        for r in range(2):
                            last = V.tensor_copy(gen[:, 2 * (j % 2) + r, :], ps[:, 2 * (j % 2) + r, :])
                            if r == 0:
                                S.link(last)
                        last.then_inc(g_staged, 1)
                        dve.wait_ge(g_staged, 4 * half + j + 1)
                        V.engine_nop().then_inc(bank_read, 1)
                        if j % 2:
                            split_after(FIRST[f"dft_g{half}"] + j // 2)
                if u == 15:
                    mask_unit(16)

            def tail(first, gname, dst, isq, iop, bias_name=None, unroll=False):
                S.link(V.memset(acc[:], 0.0))
                if gname == "gvec_first":
                    S.link(V.memset(acc_next[:], 0.0))

                def one(m, p, d, n):
                    for j in range(2):
                        product(4 * m + (2 * p + j))
                        hd = h[:, bass.ds(d + j, 1), :].rearrange("p a t -> p (a t)")
                        if iop == 4:
                            dve.wait_ge(h2_made, KT)
                        if bias_name:
                            V.scalar_tensor_tensor(hd, ps[:, 2 * p + j, :], vecs[:, bass.ds(d + (VEC[bias_name] + j), 1)], hd,
                                                   ALU.add, ALU.add).then_inc(bank_read, 1)
                        else:
                            V.tensor_tensor(hd, ps[:, 2 * p + j, :], hd, ALU.add).then_inc(bank_read, 1)
                        if j == 1 and p == 0 and not (unroll and 2 * m + 2 >= PAIRS):
                            split_lo(m + 1, p)
                        if gname:
                            g = (gvec_first[:, bass.ds(d + j, 1)] if gname == "gvec_first" else
                                 vecs[:, bass.ds(d + (VEC[gname] + j), 1)])
                            dve.wait_ge(next_hi, n + (8 * iop + j + 1))
                            V.scalar_tensor_tensor(op_lo[dst][:, bass.ds(d + j, 1), :].rearrange("p a t -> p (a t)"), hd, g,
                                                   op_hi[dst][:, bass.ds(d + j, 1), :].rearrange("p a t -> p (a t)").bitcast(F32),
                                                   ALU.mult, ALU.subtract).then_inc(next_lo, 1)
                        dve.wait_ge(squared, n + (8 * isq + j + 1))
                        V.tensor_tensor(acc[:], acc[:], sq[:, j, :], ALU.add).then_inc(summed, 1)
                        dve.wait_ge(summed, n + (8 * isq + j + 1))
                        if gname == "gvec_first":
                            dve.wait_ge(squared_next, n + (j + 1))
                            V.tensor_tensor(acc_next[:], acc_next[:], sq_next[:, j, :], ALU.add).then_inc(summed_next, 1)
                            dve.wait_ge(summed_next, n + (j + 1))
                if unroll:
                    for q in range(4):
                        one((FIRST[first] + q) // 2, q % 2, 2 * q, 2 * q)
                        if q % 2:
                            split_after(FIRST[first] + q)
                else:
                    with dve.Fori(0, 2) as i:
                        for p in range(2):
                            m = FIRST[first] // 2 + i
                            one(m, p, 4 * i + 2 * p, 4 * i + 2 * p)
                            if p:
                                split_lo(m + 1, p)

            def norm(i):
                dve.wait_ge(norm_sum, i - 1)
                finish_norm(i, ps[:, 7, :])

            dve.wait_ge(x_again, 16)
            tail("w_out", "g_xa", 0, 1, 1)
            norm(2)
            def evac_xq(q):
                for j in range(2):
                    evac(2 * (FIRST["xq"] + q) + j, xq[:, 2 * q + j, :], -1.0 / 16.0)
                split_after(FIRST["xq"] + q)

            def lowest(u):
                dve.wait_ge(qk_done, 32 + u + 1)
                V.tensor_reduce(low[:, u:u + 1], ps[:, 4 + u % 2, 0:M], AX.X, ALU.min).then_inc(masked, 1)

            evac_xq(0)
            evac_xq(1)
            lowest(0)
            for u in range(18):
                if u + 1 < 16:
                    lowest(u + 1)
                if u < 16:
                    normalise(32 + u, u)
                if u >= 2:
                    v = u - 2
                    dve.wait_ge(pv_hi, 4 + v + 1)
                    lo_part(op_lo[1][:, 2 * (v // 4):2 * (v // 4) + 2, (v % 4) * P:(v % 4 + 1) * P],
                            ps[:, 7, 0:M].rearrange("p (a t) -> p a t", a=2),
                            op_hi[1][:, 2 * (v // 4):2 * (v // 4) + 2, (v % 4) * P:(v % 4 + 1) * P]).then_inc(pv_lo, 1)
                if u in (3, 7):
                    evac_xq(2 + u // 4)
            tail("xo", "g_ffn", 0, 2, 2)
            norm(3)
            V.memset(z_pad[:, :, :, 0:2], 0.0)
            S.link(V.tensor_tensor(gvec_first[:], vec("g_final", 0, 8), vec("norm_mix_2", 0, 8), ALU.mult))

            def conv_up(section, count, base_tiles):
                with dve.Fori(0, count // 2) as i:
                    S.start(i, 6)
                    for p in range(2):
                        m = FIRST[section] // 2 + i
                        n = 2 * i + (base_tiles + p)
                        for j in range(2):
                            product(4 * m + (2 * p + j))
                            V.tensor_tensor(z_pad[:, p, j, 2:2 + T], ps[:, 2 * p + j, :], rstd[:], ALU.mult).then_inc(bank_read, 1)
                        split_lo(m + 1, p)
                        dve.wait_ge(bank_read, 4 * m + (2 * p + 2))
                        for j in (1, 0):
                            dve.wait_ge(tapped, 4 * i + (2 * base_tiles + 2 * p + 2))
                            for tap in (1, 0):
                                ins = V.scalar_tensor_tensor(
                                    conv[:, p, j, :], z_pad[:, p, j, tap:tap + T],
                                    vecs[:, bass.ds(2 * i + (VEC["ffconv"] + tap * 2 * FT + j * FT + base_tiles + p), 1)],
                                    conv[:, p, j, :], ALU.mult, ALU.add)
                                if j == 1 and tap == 0:
                                    ins.then_inc(conved, 1)
                                else:
                                    S.link(ins)
                        dve.wait_ge(gated, n + 1)
                        V.tensor_tensor(conv[:, p, 0, :], conv[:, p, 0, :], conv[:, p, 1, :], ALU.mult).then_inc(act_prod, 1)
                        dve.wait_ge(act_hi, n + 1)
                        lo_part(op_lo[1][:, bass.ds(2 * i + p, 1), :].rearrange("p a t -> p (a t)"), conv[:, p, 0, :],
                                op_hi[1][:, bass.ds(2 * i + p, 1), :].rearrange("p a t -> p (a t)")).then_inc(act_lo, 1)
                    S.end(count // 2)

            def down(section):
                with dve.Fori(0, 2) as i:
                    for p in range(2):
                        m = FIRST[section] // 2 + i
                        for j in range(2):
                            product(4 * m + (2 * p + j))
                            hd = h[:, bass.ds(4 * i + (2 * p + j), 1), :].rearrange("p a t -> p (a t)")
                            V.tensor_tensor(hd, ps[:, 2 * p + j, :], hd, ALU.add).then_inc(bank_read, 1)
                        split_lo(m + 1, p)
                dve.wait_ge(bank_read, 2 * FIRST[section] + 8)

            for g in range(3):
                conv_up(f"up1_{g}", FFN_GROUPS[g], 8 * g)
                if g < 2:
                    down(f"down1_{g}")
            tail("down1_2", "gvec_first", 0, 3, 3)
            norm(4)
            dve.wait_ge(norm_sum, 4)
            S.link(V.tensor_tensor(mean[:], ps[:, 6, :], rstd[:], ALU.mult))
            S.link(V.tensor_tensor(mean[:], mean[:], rstd[:], ALU.mult))
            V.tensor_scalar(mean[:], mean[:], 1.0 / D, EPS, ALU.mult, ALU.add).then_inc(norm_mean, 1)
            S.link(V.tensor_copy(acc_next[:], rstd[:]))
            V.engine_nop().then_inc(first_rstd, 1)
            dve.wait_ge(norm_root, 6)
            S.link(V.reciprocal(mean[:], mean[:]))
            V.tensor_tensor(rstd[:], rstd[:], mean[:], ALU.mult).then_inc(norm_rstd, 1)
            dve.wait_ge(norm_rstd, 6)

            V.memset(z_pad[:, :, :, 0:1], 0.0)
            S.link(V.memset(z_pad[:, :, :, 1 + T:2 + T], 0.0))
            hy_pairs = FIRST["hy_in"]

            def hy_conv(i, p, finish):
                m = hy_pairs // 2 + i
                for j in range(2):
                    product(4 * m + (2 * p + j))
                    V.tensor_tensor(z_pad[:, p, j, 1:1 + T], ps[:, 2 * p + j, :], rstd[:], ALU.mult).then_inc(bank_read, 1)
                split_lo(m + 1, p)
                for j in range(2):
                    f = 4 * i + (2 * p + j)
                    dve.wait_ge(hz_tap, f + 1)
                    S.link(V.scalar_tensor_tensor(conv[:, p, j, :], z_pad[:, p, j, 0:T],
                                                  vecs[:, bass.ds(f + VEC["hy_conv"], 1)], conv[:, p, j, :], ALU.mult, ALU.add))
                    finish(j, V.scalar_tensor_tensor, z_pad[:, p, j, 2:2 + T], vecs[:, bass.ds(f + (VEC["hy_conv"] + 48), 1)],
                           conv[:, p, j, :])

            with dve.Fori(0, 4) as i:
                S.start(i, 8)
                for p in range(2):
                    def into_s(j, stt, z, w, c):
                        S.link(stt(c, z, w, c, ALU.mult, ALU.add))
                        if j == 1:
                            V.tensor_tensor(s_feat[:, bass.ds(2 * i + p, 1), :].rearrange("p a t -> p (a t)"), conv[:, p, 0, :],
                                            conv[:, p, 1, :], ALU.mult).then_inc(hz_done, 1)
                    hy_conv(i, p, into_s)
                S.end(4)
            for q in range(4):
                def into_x0(j, stt, z, w, c):
                    stt(x0_feat[:, 2 * q + j, :], z, w, c, ALU.mult, ALU.add).then_inc(hz_done, 1)
                hy_conv(4 + q // 2, q % 2, into_x0)
                for n in (2 * q, 2 * q + 1):
                    dve.wait_ge(st_hi, n + 1)
                    lo_part(op_lo[1][:, n, :], ps[:, 4 + n % 4, :], op_hi[1][:, n, :]).then_inc(st_lo, 1)
            def spectrum_products(n):
                b = 2 * (n % 2)
                c = S_CHUNK[n]
                product(c)
                dve.wait_ge(g_back[n % 2], 16 * (n // 2 + 1))
                if n >= 2:
                    dve.wait_ge(y_hi, 2 * n - 2)
                    dve.wait_ge(y_lo, 2 * n - 2)
                gr, gi, t = g_spec[:, n % 2, 0, :], g_spec[:, n % 2, 1, :], spec[:, n % 2]
                V.tensor_tensor(t[:, 0, :], ps[:, b, :], gr, ALU.mult)
                V.tensor_tensor(t[:, 1, :], ps[:, b + 1, :], gi, ALU.mult)
                V.tensor_tensor(t[:, 2, :], ps[:, b, :], gi, ALU.mult)
                V.tensor_tensor(t[:, 3, :], ps[:, b + 1, :], gr, ALU.mult).then_inc(bank_read, 1)
                dve.wait_ge(bank_read, c + 1)
                if n % 4 == 0:
                    S.link(V.tensor_copy(t[0:1, 2, :], t[0:1, 1, :]))
                    V.memset(t[0:1, 3, :], 0.0)
                    S.link(V.memset(t[0:1, 1, :], 0.0))
                V.engine_nop().then_inc(spec_mul, 1)

            def spectrum_lo(n):
                for r in range(2):
                    dve.wait_ge(y_hi, 2 * n + r + 1)
                    lo_part(op_lo[0][:, 2 * (n % 4) + r, :], spec[:, n % 2, 2 * r, :], op_hi[0][:, 2 * (n % 4) + r, :]
                            ).then_inc(y_lo, 1)

            def hyena_out(half):
                dve.wait_ge(chunk_done, 2 * FIRST[f"idft_{half}"] + 4)

                def low_of(c):
                    dve.wait_ge(u_hi, c + 1)
                    lo_part(op_lo[1][:, c, :], hy_tmp[:, c % 2, 1, :], op_hi[1][:, c, :]).then_inc(u_lo, 1)
                    dve.wait_ge(u_lo, c + 1)

                for t in range(4):
                    c = 4 * half + t
                    dve.wait_ge(skip_s, c + 1)
                    y = hy_tmp[:, c % 2, 1, :]
                    V.scalar_tensor_tensor(y, ps[:, 4 + t, :], filter_norm[:, c:c + 1], hy_tmp[:, c % 2, 0, :], ALU.mult,
                                           ALU.add).then_inc(bank_read, 1)
                    dve.wait_ge(bank_read, 2 * FIRST[f"idft_{half}"] + t + 1)
                    V.tensor_tensor(y, y, x0_feat[:, c, :], ALU.mult).then_inc(hy_val, 1)
                    if t:
                        low_of(c - 1)
                low_of(4 * half + 3)

            s0, s1a, i0, s1b, i1 = (FIRST[name] for name in ("dft_s0", "dft_s1a", "idft_0", "dft_s1b", "idft_1"))
            spectrum_products(0)
            spectrum_products(1)
            spectrum_lo(0)
            split_after(s0)
            spectrum_lo(1)
            spectrum_products(2)
            spectrum_products(3)
            spectrum_lo(2)
            split_after(s0 + 1)
            spectrum_lo(3)
            spectrum_products(4)
            spectrum_products(5)
            split_after(s1a)
            split_after(i0)
            dve.wait_ge(chunk_done, 2 * i0 + 4)
            spectrum_lo(4)
            spectrum_lo(5)
            split_after(i0 + 1)
            hyena_out(0)
            spectrum_products(6)
            spectrum_products(7)
            spectrum_lo(6)
            split_after(s1b)
            spectrum_lo(7)
            split_after(i1)
            hyena_out(1)
            split_after(i1 + 1)
            tail("hy_out", "norm_ffn_2", 0, 4, 4, bias_name="hy_b_out")
            norm(6)

            def gate_up(section, count, base_tiles):
                with dve.Fori(0, count // 2) as i:
                    for p in range(2):
                        m = FIRST[section] // 2 + i
                        n = 2 * i + (base_tiles + p)
                        for j in range(2):
                            product(4 * m + (2 * p + j))
                            V.tensor_tensor(z_pad[:, p, j, 0:T], ps[:, 2 * p + j, :], rstd[:], ALU.mult).then_inc(bank_read, 1)
                        split_lo(m + 1, p)
                        dve.wait_ge(bank_read, 4 * m + (2 * p + 2))
                        dve.wait_ge(gated, n + (FT + 1))
                        V.tensor_tensor(conv[:, p, 1, :], conv[:, p, 0, :], z_pad[:, p, 1, 0:T], ALU.mult).then_inc(act_prod, 1)
                        dve.wait_ge(act_hi, n + (FT + 1))
                        lo_part(op_lo[1][:, bass.ds(2 * i + p, 1), :].rearrange("p a t -> p (a t)"), conv[:, p, 1, :],
                                op_hi[1][:, bass.ds(2 * i + p, 1), :].rearrange("p a t -> p (a t)")).then_inc(act_lo, 1)

            for g in range(3):
                gate_up(f"up2_{g}", FFN_GROUPS[g], 8 * g)
                if g < 2:
                    down(f"down2_{g}")
            tail("down2_2", None, None, 5, None, unroll=True)
            norm(7)
            for k in range(KT):
                V.scalar_tensor_tensor(h[:, k, :], h[:, k, :], vec("norm_final_2", k), rstd[:], ALU.mult,
                                       ALU.mult).then_inc(out_made, 1)

        @block.tensor
        def _(pe):
            W = nc.tensor

            def weight(part, p, j, k):
                return part[:, p, j * CHUNK + k * P:j * CHUNK + (k + 1) * P]

            def passes(out, w, x, start, stop):
                W.matmul(out, w[0], x[0], start=start, stop=False)
                W.matmul(out, w[0], x[1], start=False, stop=False)
                return W.matmul(out, w[1], x[0], start=False, stop=stop)

            def pair_ready(g):
                pe.wait_ge(lo_ready, g + 1)

            def chunk(p, j, x, out, ks=range(KT), n_k=KT, operand=None, count=0):
                for k in ks:
                    if operand is not None:
                        pe.wait_ge(operand, count + k + 1)
                    last = passes(out, (weight(w_hi, p, j, k), weight(w_lo, p, j, k)), (x[0][:, k, :], x[1][:, k, :]),
                                  k == 0, k == n_k - 1)
                return last

            def gemm(section, x, n_k=KT, operand=None, count=0, norms=(), wide=2, late=2, pairs=None, free=None):

                def chunk_norms(at_chunk):
                    for c, which in norms:
                        if c == at_chunk:
                            norm_matmul(which)

                m = FIRST[section] // 2
                early = n_k - late
                for part in (range(early), range(early, n_k)):
                    for c in range(wide):
                        p, j = c // 2, c % 2
                        if part[0] == 0:
                            if j == 0:
                                pe.wait_ge(lo_ready, 2 * m + p + 1)
                            pe.wait_ge(bank_read, 4 * m + c - 3 if free is None else free)
                        last = chunk(p, j, x, ps[:, c, :], part, n_k, operand if c == 0 else None, count)
                        if part[0]:
                            last.then_inc(chunk_done, 1)
                            chunk_norms(c)
                for c in range(wide, 4):
                    p, j = c // 2, c % 2
                    if j == 0:
                        pe.wait_ge(lo_ready, 2 * m + p + 1)
                    pe.wait_ge(bank_read, 4 * m + c - 3)
                    chunk(p, j, x, ps[:, c, :], range(n_k), n_k).then_inc(chunk_done, 1)
                    chunk_norms(c)
                with pe.Fori(1, (dict(SECTIONS)[section] if pairs is None else pairs) // 2) as i:
                    m = FIRST[section] // 2 + i
                    for p in range(2):
                        pe.wait_ge(lo_ready, 2 * m + (p + 1))
                        for j in range(2):
                            pe.wait_ge(bank_read, 4 * m + (2 * p + j - 3))
                            chunk(p, j, x, ps[:, 2 * p + j, :], range(n_k), n_k).then_inc(chunk_done, 1)

            X = [(op_hi[0], op_lo[0]), (op_hi[1], op_lo[1])]

            def norm_matmul(isq, bank=7):
                pe.wait_ge(summed, 8 * isq + 8)
                W.matmul(ps[:, bank, :], ones[:], acc[:], start=True, stop=True).then_inc(norm_sum, 1)
                if isq == 3:
                    pe.wait_ge(summed_next, 8)
                    W.matmul(ps[:, 6, :], ones[:], acc_next[:], start=True, stop=True).then_inc(norm_sum, 1)

            def misc(j, ready=None):
                if j >= 2:
                    pe.wait_ge(misc_read, j - 1)
                return ps[:, 6 + j % 2, :]

            def in_pair(q, j):
                c = 2 * q + j
                if j == 0:
                    pair_ready(q)
                if c >= 4:
                    pe.wait_ge(bank_read, c - 3)
                chunk(q % 2, j, X[0], ps[:, c % 4, :], operand=next_lo if c == 0 else None).then_inc(chunk_done, 1)

            def mlp(layer):
                for d in range(2):
                    j = MLP_JOB[layer] + d
                    out = misc(j)
                    if layer == 0:
                        W.matmul(out[0:64, :], mlp_w[0:33, 0, :], feat[:, d * T:(d + 1) * T], start=True,
                                 stop=True).then_inc(misc_done, 1)
                    else:
                        pe.wait_ge(mlp_sin, 2 * layer)
                        W.matmul(out[0:64, :], mlp_w[:, layer, :], mlp_h[layer - 1][:, d, :], start=True,
                                 stop=True).then_inc(misc_done, 1)

            in_pair(0, 0)
            pe.wait_ge(made_ones, 1)
            pe.wait_ge(summed, KT)
            W.matmul(misc(0), ones[:], acc[:], start=True, stop=True).then_inc(misc_done, 1)
            in_pair(0, 1)
            pe.wait_ge(gate_folded, 1)
            bank = misc(1)
            for i in range(NT):
                for k in range(KT):
                    W.matmul(bank[:, 4 * i:4 * i + 4], h[:, k, i * P:(i + 1) * P], gate_w[:, k, :], start=(k == 0),
                             stop=(k == KT - 1))
                last = W.matmul(bank[:, 16 + i:17 + i], acc[:, i * P:(i + 1) * P], ones[:, 0:1], start=True, stop=True)
            last.then_inc(misc_done, 1)
            pe.wait_ge(small_in, 96)
            mlp(0)
            for j in range(2):
                in_pair(1, j)

            def rotate(tile, job):
                for j in range(2):
                    out = misc(job + j)
                    pe.wait_ge(bank_read, tile + j + 1)
                    W.matmul(out, rot[:], qk[:, tile + j, :], start=True, stop=True).then_inc(misc_done, 1)

            rotate(0, 4)
            for j in range(2):
                in_pair(2, j)
            rotate(2, 6)
            mlp(1)
            for j in range(2):
                in_pair(3, j)

            def transpose_v(c, job):
                for b in range(2):
                    out = misc(job + b)
                    pe.wait_ge(bank_read, c + 2)
                    for i in range(2):
                        for j in range(2):
                            last = W.transpose(out[:, i * M + j * P:i * M + (j + 1) * P],
                                               v_raw[:, j, (2 * b + i) * P:(2 * b + i + 1) * P], ident[:])
                    last.then_inc(misc_done, 1)

            transpose_v(4, 10)
            for j in range(2):
                in_pair(4, j)
            mlp(2)
            out = misc(14)
            pe.wait_ge(gate_ready, 1)
            pe.wait_ge(tri_in, 16)
            for i in range(NT):
                for s in range(i + 1):
                    last = W.matmul(out[:, 4 * i:4 * i + 4], tri[:, 0:P] if s == i else ones[:], log_f[:, s, :],
                                    start=(s == 0), stop=(s == i))
            last.then_inc(misc_done, 1)
            out = misc(15)
            for s in range(NT):
                last = W.matmul(out[0:4, s * P:T], log_f[:, s, :], tri[:, 0:T - s * P], start=(s == 0), stop=(s == NT - 1),
                                skip_group_check=True)
            last.then_inc(misc_done, 1)
            for j in range(2):
                in_pair(5, j)
            for j in range(2):
                in_pair(6, j)
            transpose_v(10, 16)
            for j in range(2):
                in_pair(7, j)
            pe.wait_ge(pool_in, 16)
            for j in range(2):
                out = misc(18 + j)
                pe.wait_ge(pooled, j + 1)
                W.matmul(out, pool_w[:, j, :], pool_a[:, j, 16:16 + T], start=True, stop=True).then_inc(misc_done, 1)
            for j in range(2):
                in_pair(8, j)
            for j in range(2):
                in_pair(9, j)
            out = misc(20)
            pe.wait_ge(mem_sum, 5)
            W.matmul(out[:, 0:M], ones[:], acc[:, 0:M], start=True, stop=True).then_inc(misc_done, 1)

            def qk_unit(u):
                s, i = UNITS[u]
                b = 64 * (s % 2)
                tile = 4 * (s // 4) + (s % 4) // 2
                n = (i + 1) * P
                if u >= 2:
                    pe.wait_ge(masked, u - 1)
                W.matmul(ps[:, 4 + u % 2, 0:n], qk[b:b + 64, tile, i * P:(i + 1) * P], qk[b:b + 64, tile + 2, 0:n],
                         start=True, stop=True).then_inc(qk_done, 1)

            def transpose_unit(u, n_blocks):
                pe.wait_ge(probs_ready, u + 1)
                if u:
                    pe.wait_ge(pt_ready, u)
                for kb in range(n_blocks):
                    last = W.transpose(ps[:, 6, kb * P:(kb + 1) * P], unit_scores(u)[:, kb * P:(kb + 1) * P], ident[:])
                last.then_inc(transposed, 1)

            def pv_unit(u):
                s, i = UNITS[u]
                b = 64 * (s % 2)
                pe.wait_ge(pt_ready, u + 1)
                if u % 8 == 0 and u > 0:
                    pe.wait_ge(pv_lo, u // 8)
                for kb in range(i + 1):
                    last = W.matmul(ps[b:b + 64, 7, i * P:(i + 1) * P], v_tok[:, kb, HD * s:HD * s + HD],
                                    probs_t[:, u % 2, kb * P:(kb + 1) * P], start=(kb == 0), stop=(kb == i))
                last.then_inc(pv_done, 1)

            def keys_broadcast(s):
                pe.wait_ge(gen_taps, s)
                if s == 4:
                    pe.wait_ge(bank_read, 2 * FIRST["dft_g0"] + 4)
                W.matmul(ps[:, 3, :], ident[0:4, s - 4:s - 3].to_broadcast([4, P]), c_row[:], start=True, stop=True).then_inc(bcast_done, 1)

            def transform(tiles, chunks, x, before):
                for j, c in zip(tiles, chunks):
                    g = c // 2
                    if j % 2 == 0:
                        pair_ready(g)
                    pe.wait_ge(bank_read, c - before + 1)
                    for r in range(2):
                        for n in range(NT):
                            last = passes(ps[:, 2 * (j % 2) + r, :],
                                          (weight(w_hi, g % 2, j % 2, 4 * r + n), weight(w_lo, g % 2, j % 2, 4 * r + n)),
                                          x(j, n), n == 0, n == NT - 1)
                    last.then_inc(chunk_done, 1)

            pe.wait_ge(roped, 4)
            pe.wait_ge(bank_read, 20)
            pe.wait_ge(misc_read, 21)
            qk_unit(0)
            qk_unit(1)
            pe.wait_ge(mem_lo, KT)
            for u, (s, i) in enumerate(UNITS):
                half, n = s // 4, s % 4
                g = (FIRST["k_mem"] if s < 4 else FIRST["v_mem"] - 4) + s
                c = 2 * g + i // 2
                if i == 0:
                    if s >= 4:
                        pe.wait_ge(bcast_read, s - 3)
                    if s >= 5:
                        pe.wait_ge(vt_read, s - 4)
                    if s == 0:
                        pe.wait_ge(late_in, 32)
                    elif s == 4:
                        pe.wait_ge(late_in, 64)
                    if s in (1, 2, 3):
                        pe.wait_ge(gen_taps, s)
                    for d in range(2):
                        last = W.matmul(ps[:, 2 + d, :], mlp_h[2][:, d, n * P:(n + 1) * P], f_out[:, d, :], start=True, stop=True)
                    last.then_inc(gen_done, 1)
                    pair_ready(g)
                if i == 2 and 4 <= s < 7:
                    keys_broadcast(s + 1)
                if u + 2 < len(UNITS):
                    qk_unit(u + 2)
                if i % 2 == 0:
                    pe.wait_ge(bank_read, c - 1)
                last = chunk(g % 2, i // 2, (mg_hi, mg_lo), ps[:, c % 2, 0:M], range(4 * (i % 2), 4 * (i % 2) + 4))
                if i % 2 == 1:
                    last.then_inc(chunk_done, 1)
                if u:
                    transpose_unit(u - 1, (u - 1) % 4 + 1)
                if u >= 2:
                    pv_unit(u - 2)
                if u == 31:
                    transpose_unit(31, NT)
                    pv_unit(30)
                    pv_unit(31)
                if i == 3 and s >= 4:
                    pe.wait_ge(bank_read, c + 1)
                    pe.wait_ge(gen_taps, s + 1)
                    for b in range(2):
                        for j in range(2):
                            last = W.transpose(ps[:, 2, b * M + j * P:b * M + (j + 1) * P],
                                               v_stage[:, j, b * P:(b + 1) * P], ident[:])
                    last.then_inc(vt_done, 1)
                if i == 3 and n == 3:
                    pe.wait_ge(gen_lo, 8 * half + 8)
                    if half:
                        pe.wait_ge(bcast_read, 4)
                        pe.wait_ge(vt_read, 4)
                    for t in range(4):
                        last = W.matmul(ps[:, 3, t:t + 1], acc[:, t * P:(t + 1) * P], ones[:, 0:1], start=True, stop=True)
                    last.then_inc(fnorm_done, 1)
                    pe.wait_ge(fnorm_read, half + 1)
                    first = 2 * FIRST[f"dft_g{half}"]
                    transform(range(4), range(first, first + 4),
                              lambda j, n: (op_hi[0][:, 4 * (j // 2) + n, :], op_lo[0][:, 4 * (j // 2) + n, :]), 2)
                    if half == 0:
                        keys_broadcast(4)

            pe.wait_ge(mix_lo, 4)
            pe.wait_ge(pv_lo, 4)
            pe.wait_ge(bank_read, 2 * FIRST["w_out"])
            gemm("w_out", X[1])

            def xq_half(n):
                q, j, part = n // 4, n % 4 // 2, n % 2
                g = FIRST["xq"] + q
                c = 2 * g + j
                if n % 4 == 0:
                    pair_ready(g)
                if part == 0:
                    pe.wait_ge(bank_read, c - 3)
                if n == 0:
                    pe.wait_ge(next_lo, 16)
                last = chunk(g % 2, j, X[0], ps[:, c % 4, :], range(4 * part, 4 * part + 4))
                if part:
                    last.then_inc(chunk_done, 1)
                if n == 1:
                    norm_matmul(1)

            def x_qk(u):
                hd, i = u // 4, u % 4
                if u >= 2:
                    pe.wait_ge(exped, 32 + u - 1)
                if i == 0:
                    pe.wait_ge(bank_read, 2 * (FIRST["xq"] + hd) + 2)
                for k in range(2):
                    last = W.matmul(ps[:, 4 + u % 2, 0:M], xq[:, 2 * hd + k, i * P:(i + 1) * P], k_mem[:, 2 * hd + k, :],
                                    start=(k == 0), stop=(k == 1))
                last.then_inc(qk_done, 1)

            def x_pv(u):
                hd = u // 4
                pe.wait_ge(pt_ready, 32 + u + 1)
                if u:
                    pe.wait_ge(pv_lo, 4 + u)
                else:
                    pe.wait_ge(norm_mean, 3)
                for d in range(2):
                    for kb in range(2):
                        last = W.matmul(ps[:, 7, d * P:(d + 1) * P], v_mem[:, kb, hd * M + d * P:hd * M + (d + 1) * P],
                                        probs_t[:, u % 2, kb * P:(kb + 1) * P], start=(kb == 0), stop=(kb == 1))
                last.then_inc(pv_done, 1)

            for n in range(8):
                xq_half(n)
            x_qk(0)
            x_qk(1)
            for u in range(18):
                if u < 8:
                    xq_half(8 + u)
                if u + 2 < 16:
                    x_qk(u + 2)
                if 1 <= u <= 16:
                    transpose_unit(32 + u - 1, 2)
                if u >= 2:
                    x_pv(u - 2)
            pe.wait_ge(pv_lo, 20)
            gemm("xo", X[1])

            for g in range(3):
                gemm(f"up1_{g}", X[0], operand=next_lo if g == 0 else None, count=16, norms=[(0, 2)] if g == 0 else ())
                gemm(f"down1_{g}", X[1], n_k=FFN_GROUPS[g], operand=act_lo, count=8 * g, wide=4)

            gemm("hy_in", X[0], operand=next_lo, count=24, norms=[(0, 3)], pairs=8)
            for q in range(4):
                g = FIRST["hy_in"] + 8 + q
                pair_ready(g)
                for j in range(2):
                    c = 2 * g + j
                    pe.wait_ge(bank_read, c - 3)
                    chunk(g % 2, j, X[0], ps[:, c % 4, :]).then_inc(chunk_done, 1)
                    n = 2 * q + j
                    half, t = n // 4, n % 4
                    pe.wait_ge(norm_rstd, 6)
                    if n >= 4:
                        pe.wait_ge(st_lo, n - 3)
                    pe.wait_ge(hz_done, 4 * half + 4)
                    for c in range(4):
                        last = W.transpose(ps[:, 4 + n % 4, c * P:(c + 1) * P], s_feat[:, 4 * half + c, t * P:(t + 1) * P],
                                           ident[:])
                    last.then_inc(st_done, 1)

            def forward_s(half, tiles, before):
                if tiles[0] == 0:
                    pe.wait_ge(st_lo, 4 * half + 4)
                transform(tiles, [S_CHUNK[4 * half + j] for j in tiles],
                          lambda j, n: (op_hi[1][:, 4 * half + n, :], op_lo[1][:, 4 * half + n, :]), before)

            def inverse(half):
                if half:
                    pe.wait_ge(bank_read, 2 * FIRST["idft_0"] + 4)
                else:
                    pe.wait_ge(st_lo, 8)
                for q in range(4):
                    g = FIRST[f"idft_{half}"] + q // 2
                    if q % 2 == 0:
                        pair_ready(g)
                    pe.wait_ge(y_lo, 8 * half + 2 * q + 2)
                    for f in range(2):
                        at_f = slice((q % 2) * CHUNK + f * T, (q % 2) * CHUNK + (f + 1) * T)
                        for c in range(4):
                            cs = slice(c * P, (c + 1) * P)
                            last = passes(ps[:, 4 + c, :], (op_hi[0][:, 2 * q + f, cs], op_lo[0][:, 2 * q + f, cs]),
                                          (w_hi[:, g % 2, at_f], w_lo[:, g % 2, at_f]), q == f == 0, q == 3 and f == 1)
                    last.then_inc(chunk_done, 1)

            forward_s(0, (0, 1, 2, 3), 2)
            forward_s(1, (0, 1), 2)
            inverse(0)
            forward_s(1, (2, 3), 6)
            inverse(1)
            gemm("hy_out", X[1], operand=u_lo, wide=4, late=4, free=S_CHUNK[7] + 1)

            for g in range(3):
                gemm(f"up2_{g}", X[0], operand=next_lo if g == 0 else None, count=32, norms=[(0, 4)] if g == 0 else ())
                gemm(f"down2_{g}", X[1], n_k=FFN_GROUPS[g], operand=act_lo, count=FT + 8 * g, wide=4)
            norm_matmul(5)


def constants():
    f64 = np.float64
    pos = np.arange(T)
    n_fft = 2 * T
    freqs = np.concatenate([2 * np.arange(T // 2), 2 * np.arange(T // 2) + 1])
    angle = 2 * np.pi * ((freqs[:, None] * pos[None, :]) % n_fft) / n_fft
    re, im = np.cos(angle), -np.sin(angle)
    im[0] = np.cos(np.pi * pos)
    inv_re, inv_im = 2 * re / n_fft, 2 * im / n_fft
    inv_re[0] /= 2
    inv_im[0] /= 2
    t = np.linspace(0.0, 1.0, T, dtype=np.float32)
    w = (np.float32(2 * np.pi) * pos.astype(np.float32) / np.float32(T)).astype(np.float32)
    bands = np.linspace(1e-4, 15, 16, dtype=np.float32)
    arg = (bands[None, :] * w[:, None]).astype(np.float32).astype(f64)
    feat = np.concatenate([t[:, None].astype(f64), np.cos(arg), -np.sin(arg)], axis=1).astype(np.float32)
    back = np.where(pos > 0, T - pos, 0)
    feat = np.concatenate([feat, feat[back]], axis=0).T
    delta = np.arange(P)[:, None] - np.arange(T)[None, :] + 3 * P
    uses = (delta <= 128).astype(int) + ((delta % 4 == 0) & (delta <= 512)) + (delta % 16 == 0)
    uses = np.where(delta >= 0, uses, 0)
    dilated = np.where(uses > 0, -np.log(np.maximum(uses, 1).astype(f64)), BIG)
    causal = np.where(delta >= 0, 0.0, BIG)
    rot = np.zeros((P, P))
    inv_freq = np.zeros(P)
    theta = 500000.0 ** (-np.arange(0, 16, 2, dtype=f64) / 16)
    for base in (0, 64):
        for r in range(8):
            rot[base + 8 + r, base + r] = -1
            rot[base + r, base + 8 + r] = 1
            inv_freq[base + r] = inv_freq[base + 8 + r] = theta[r]
    tokens = np.arange(P)[:, None] + P * np.arange(NT)[None, :]
    neg_t = -np.concatenate([t[tokens], t[back[tokens]]], axis=1)
    edge = np.zeros((P, 2, 16))
    inv_window = np.zeros((P, 2))
    for tile in range(2):
        for part in range(2):
            window = (2, 4, 8, 16)[2 * tile + part]
            edge[64 * part:64 * part + 64, tile] = 1.0 / np.minimum(np.arange(16) + 1, window)
            inv_window[64 * part:64 * part + 64, tile] = 1.0 / window
    f32 = lambda x: np.ascontiguousarray(x, dtype=np.float32)
    return {"re": f32(re.T), "im": f32(im.T), "inv_re": f32(inv_re), "inv_im": f32(inv_im), "feat": f32(feat),
            "masks": f32(np.stack([dilated, causal])), "rot": f32(rot), "inv_freq": f32(inv_freq[:, None]),
            "neg_t": f32(neg_t), "edge": f32(edge.reshape(P, 32)), "inv_window": f32(inv_window),
            "tri": f32(np.arange(P)[:, None] <= np.arange(T)[None, :]), "ident": f32(np.eye(P))}


def by_tile(v):
    return v.reshape(-1, P).T


def chunk_of(w, tile, n_k=KT):
    out = np.zeros((P, KT, P), w.dtype)
    out[:, :n_k] = w[:, tile * P:(tile + 1) * P].reshape(n_k, P, P).transpose(1, 0, 2)
    return out.reshape(P, CHUNK)


def kernel(**inputs):
    import concourse.bacc as bacc
    from concourse.bass_utils import run_bass_kernel_spmd as run

    v = {k: np.asarray(x) for k, x in inputs.items()}
    const = constants()
    chunks = []

    def take(w, tiles, n_k=KT):
        chunks.extend(chunk_of(w, i, n_k) for i in tiles)

    def forward(tiles=range(4)):
        for j in tiles:
            both = [const[part][:, j * P:(j + 1) * P].reshape(NT, P, P).transpose(1, 0, 2).reshape(P, NT * P) for part in ("re", "im")]
            chunks.append(np.concatenate(both, axis=1))

    def inverse():
        for j in range(4):
            chunks.append(np.concatenate([const[part][j * P:(j + 1) * P] for part in ("inv_re", "inv_im")], axis=1))

    w_in = v["w_in"][0]
    gates = w_in[:, 18 * P:18 * P + 4]
    w_main = np.concatenate([w_in[:, :18 * P], w_in[:, 18 * P + 4:]], axis=1)
    take(w_main, [6, 7, 8, 9, 10, 11, 12, 13, 14, 15, 16, 17, 18, 19, 4, 0, 5, 1, 2, 3])
    take(v["w_xkv"][0], range(8))
    forward()
    take(v["w_xkv"][0], range(8, 16))
    forward()
    take(v["w_out"][0], range(8))
    take(v["w_xq"][0], range(8))
    take(v["w_xo"][0], range(8))

    def ffn(left, right, down):
        for g in range(3):
            for i in range(8 * g, 8 * g + FFN_GROUPS[g]):
                take(left, [i])
                take(right, [i])
            take(down[8 * g * P:(8 * g + FFN_GROUPS[g]) * P], range(8), FFN_GROUPS[g])

    ffn(v["w_up"][0][:, :FF], v["w_up"][0][:, FF:], v["w_down"][0])
    hy_order = [t for i in range(8) for t in (16 + i, 8 + i)] + list(range(8))
    take(v["hy_w_in_2"][0], hy_order)
    forward()
    forward((0, 1))
    inverse()
    forward((2, 3))
    inverse()
    take(v["hy_w_out_2"][0], range(8))
    ffn(v["ffn_w_gate_2"][0], v["ffn_w_up_2"][0], v["ffn_w_down_2"][0])
    weights = np.stack(chunks).reshape(PAIRS, 2, P, CHUNK).transpose(0, 2, 1, 3).reshape(PAIRS, P, 2 * CHUNK)

    hy_cols = lambda x: by_tile(x)[:, hy_order]
    cols = {name: by_tile(v[name][0]) for name in ("g_mix", "g_xa", "g_mem", "g_ffn", "norm_mix_2", "norm_ffn_2", "pool_scale")}
    cols["g_final"] = by_tile(v["g_final"])
    cols["norm_final_2"] = by_tile(v["norm_final_2"])
    cols["sconv"] = np.concatenate([by_tile(x) for x in v["w_sconv"][0]], axis=1)
    cols["ffconv"] = np.concatenate([by_tile(x) for x in v["w_ffconv"][0]], axis=1)
    cols["hy_conv"] = np.concatenate([hy_cols(x) for x in v["hy_conv_w_2"][0]], axis=1)
    cols["hy_conv_b"] = hy_cols(v["hy_conv_b_2"][0])
    cols["hy_b_in"] = hy_cols(v["hy_b_in_2"][0])
    cols["hy_skip"] = by_tile(v["hy_skip_2"][0])
    cols["hy_b_out"] = by_tile(v["hy_b_out_2"][0])
    cols["b_forget"] = np.broadcast_to(np.tile(v["b_forget"][0], 4), (P, 16))
    for name, key in (("inv_freq", "inv_freq"), ("pool_inv", "inv_window"), ("pool_edge", "edge"), ("neg_t", "neg_t")):
        cols[name] = const[key]
    vecs = np.concatenate([cols[name] for name in VEC], axis=1)
    pool_w = np.zeros((P, 2, P), np.float32)
    for i in range(4):
        at = 64 * (i % 2)
        pool_w[at:at + 64, i // 2, at:at + 64] = v["w_pool"][0][i]
    mlp_w = np.zeros((64, 3, 64), np.float32)
    mlp_w[:33, 0] = v["hy_f_w1_2"][0]
    mlp_w[:, 1] = v["hy_f_w2_2"][0]
    mlp_w[:, 2] = v["hy_f_w3_2"][0]
    arrays = {
        "weights": weights, "vecs": vecs, "ident": const["ident"],
        "x_t": v["x"][0].T.reshape(KT, P, T).transpose(1, 0, 2), "mem_t": v["mem"][0].T.reshape(KT, P, M).transpose(1, 0, 2),
        "positions": np.broadcast_to(v["positions"], (P, T)), "gate_w": gates.reshape(KT, P, 4).transpose(1, 0, 2),
        "mlp_w": mlp_w, "mlp_b": np.stack([v[k][0] for k in ("hy_f_b1_2", "hy_f_b2_2", "hy_f_b3_2", "hy_f_freq_2")], axis=1),
        "feat": const["feat"], "rot": const["rot"], "tri": const["tri"], "masks": const["masks"], "pool_w": pool_w,
        "f_out": v["hy_f_wout_2"][0].reshape(64, 2, D), "decay": np.broadcast_to(v["hy_decay_2"][0], (P, 2, D)),
    }
    nc = bacc.Bacc("TRN2", target_bir_lowering=False, num_devices=1)
    a = {}
    feeds = {}
    for name, x in arrays.items():
        feeds[f"{name}_dram"] = np.ascontiguousarray(x)
        a[name] = nc.dram_tensor(f"{name}_dram", x.shape, mybir.dt.from_np(x.dtype), kind="ExternalInput").ap()
    a["out"] = nc.dram_tensor("out_dram", (P, KT, T), F32, kind="ExternalOutput").ap()
    program(nc, a)
    r = run(nc, [feeds], core_ids=[0])
    return np.ascontiguousarray(r.results[0]["out_dram"].transpose(2, 1, 0)).reshape(1, T, D)
```

```python
from contextlib import ExitStack

import concourse.bass as bass
import numpy as np
from concourse import mybir

F32 = mybir.dt.float32
F32R = mybir.dt.float32r
I32 = mybir.dt.int32
ACT = mybir.ActivationFunctionType
ALU = mybir.AluOpType
AX = mybir.AxisListType

P = 128
D = 1024
T = 512
M = 256
KT = D // P
NT = T // P
HD = 64
FF = 2816
FT = FF // P
FFN_GROUPS = (8, 8, 6)
CHUNK = KT * P
EPS = 1e-6
BIG = 1e30
MAGIC = 12582912.0
INV_2PI = float(np.float32(1.0 / (2.0 * np.pi)))
C1 = 6.28125
C2 = float(np.float32(np.round((2.0 * np.pi - C1) * 2.0 ** 20) / 2.0 ** 20))
C3 = float(np.float32(2.0 * np.pi - C1 - C2))
PI_IN = 3.1415925
HALF_PI = float(np.float32(np.pi / 2))

SECTIONS = [("w_in", 10), ("k_mem", 4), ("dft_g0", 2), ("v_mem", 4), ("dft_g1", 2), ("w_out", 4), ("xq", 4), ("xo", 4)]
for g in range(3):
    SECTIONS += [(f"up1_{g}", FFN_GROUPS[g]), (f"down1_{g}", 4)]
SECTIONS += [("hy_in", 12), ("dft_s0", 2), ("dft_s1a", 1), ("idft_0", 2), ("dft_s1b", 1), ("idft_1", 2),
             ("hy_out", 4)]
for g in range(3):
    SECTIONS += [(f"up2_{g}", FFN_GROUPS[g]), (f"down2_{g}", 4)]
FIRST = {}
n_pairs = 0
for name, pairs in SECTIONS:
    FIRST[name] = n_pairs
    n_pairs += pairs
PAIRS = n_pairs

VEC = {}
n_cols = 0
for name, cols in [("g_mix", 8), ("g_xa", 8), ("g_mem", 8), ("g_ffn", 8), ("g_final", 8), ("norm_mix_2", 8), ("norm_ffn_2", 8),
                   ("norm_final_2", 8), ("sconv", 6), ("pool_scale", 2), ("ffconv", 3 * 2 * FT), ("hy_conv", 72),
                   ("hy_conv_b", 24), ("hy_b_in", 24), ("hy_skip", 8), ("hy_b_out", 8), ("inv_freq", 1), ("pool_inv", 2),
                   ("pool_edge", 32), ("b_forget", 16), ("neg_t", 8)]:
    VEC[name] = n_cols
    n_cols += cols
VECS = n_cols

MLP_JOB = (2, 8, 12)


def program(nc, a):
    with ExitStack() as ctx:
        base = 16512

        def at(name, shape, dt, offset):
            return nc.alloc_sbuf_tensor_at(name, shape, dt, offset=base + offset)

        def sem(name):
            return ctx.enter_context(nc.semaphore(name))

        KB = 1024
        h = at("h", [P, KT, T], F32, 0)
        op_hi = [at("opA_hi", [P, KT, T], F32R, 16 * KB), at("opB_hi", [P, KT, T], F32R, 48 * KB)]
        op_lo = [at("opA_lo", [P, KT, T], F32R, 32 * KB), at("opB_lo", [P, KT, T], F32R, 64 * KB)]
        raw = at("raw", [P, 2, 2 * CHUNK], F32, 80 * KB)
        w_hi = at("w_hi", [P, 2, 2 * CHUNK], F32R, 96 * KB)
        w_lo = at("w_lo", [P, 2, 2 * CHUNK], F32R, 112 * KB)
        o = 128 * KB
        vecs = at("vecs", [P, VECS], F32, o); o += 4 * ((VECS + 7) // 8 * 8)
        ident = at("ident", [P, P], F32, o); o += 512
        ones = at("ones", [P, P], F32, o); o += 512
        rstd = at("rstd", [P, T], F32, o); o += 2048
        acc = at("acc", [P, T], F32, o); o += 2048
        sq = at("sq", [P, 2, T], F32, o)
        scores = at("scores", [P, 3 * T], F32, o); o += 4096
        mean = at("mean", [P, T], F32, o); o += 2048
        low = at("low", [P, 32], F32, o); o += 128
        total = at("total", [P, 32], F32, o); o += 128
        inv_total = at("inv_total", [P, 32], F32, o); o += 128
        gate_w = at("gate_w", [P, KT, 4], F32, o); o += 128
        rstd_tok = at("rstd_tok", [P, 4], F32, o); o += 32
        log_f = at("log_f", [P, 4, 4], F32, o); o += 64
        gate_tmp = at("gate_tmp", [P, 4, 16], F32, o); o += 256
        c_tok = at("c_tok", [P, 4, 4], F32, o); o += 64
        filter_norm = at("filter_norm", [P, 8], F32, o); o += 32
        gvec_first = at("gvec_first", [P, KT], F32, o); o += 32
        c1 = (o + 31) // 32 * 32
        qk = at("qk", [P, 8, T], F32, c1)
        v_mem = at("v_mem", [P, 2, D], F32, c1)
        v_tok = at("v_tok", [P, NT, T], F32, c1 + 16 * KB)
        mg_hi = at("mg_hi", [P, KT, M], F32R, c1 + 24 * KB)
        mg_lo = at("mg_lo", [P, KT, M], F32R, c1 + 32 * KB)
        xq = at("xq", [P, KT, T], F32, c1 + 24 * KB)
        k_mem = at("k_mem", [P, KT, M], F32, c1 + 40 * KB)
        mem_raw = at("mem_raw", [P, KT, M], F32, 48 * KB + 4 * KB)
        e0 = c1 + 40 * KB
        c2 = c1 + 48 * KB
        feat = at("feat", [33, 2 * T], F32, c1 + 24 * KB)
        mlp_h = [at("mlp_h0", [64, 2, T], F32, c1 + 28 * KB), at("mlp_h1", [64, 2, T], F32, c1 + 32 * KB),
                 at("mlp_h2", [64, 2, T], F32, 0)]
        mlp_x = at("mlp_x", [64, 2, T], F32, c1 + 36 * KB)
        mlp_k = at("mlp_k", [64, T], F32, e0 + 22 * KB)
        mlp_w = at("mlp_w", [64, 3, 64], F32, e0 + 24 * KB)
        mlp_b = at("mlp_b", [64, 4], F32, e0 + 24 * KB + 768)
        cos_t = at("cos_t", [P, T], F32, e0)
        sin_t = at("sin_t", [P, T], F32, e0 + 2 * KB)
        rope_tmp = at("rope_tmp", [P, 2, T], F32, e0 + 4 * KB)
        v_raw = at("v_raw", [P, 2, T], F32, e0 + 8 * KB)
        pos = at("pos", [P, T], I32, e0 + 12 * KB)
        ang = at("ang", [P, T], F32, e0 + 14 * KB)
        turns = at("turns", [P, T], F32, e0 + 16 * KB)
        rot = at("rot", [P, P], F32, e0 + 18 * KB)
        pool_x = at("pool_x", [P, 2, 528], F32, e0 + 8 * KB)
        pool_a = at("pool_a", [P, 2, 528], F32, e0 + 8 * KB + 4224)
        pool_b = at("pool_b", [P, 2, 528], F32, e0 + 8 * KB + 8448)
        sc_m = at("sc_m", [P, 2, 516], F32, e0)
        sc_y = at("sc_y", [P, 2, T], F32, e0 + 8 * KB)
        sc_c = at("sc_c", [P, T], F32, e0 + 4128)
        tri = at("tri", [P, T], F32, 12 * KB)
        c_row = at("c_row", [4, T], F32, 14 * KB)
        v_stage = at("v_stage", [P, 2, M], F32, 12 * KB)
        probs_t = at("probs_t", [P, 2, T], F32, c2)
        mask = at("mask", [P, T], F32, c2 + 4 * KB)
        c_keys = [at("c_keys0", [P, T], F32, c2 + 6 * KB), at("c_keys1", [P, T], F32, 14 * KB)]
        bias = at("bias", [P, T], F32, c2 + 8 * KB)
        gen = at("gen", [P, 4, T], F32, c2 + 10 * KB)
        pool_w = at("pool_w", [P, 2, P], F32, e0 + 21 * KB)
        f_out = at("f_out", [64, 2, T], F32, 4 * KB)
        decay = at("decay", [P, 2, T], F32, 8 * KB)
        z_pad = at("z_pad", [P, 2, 2, 520], F32, c1)
        conv = at("conv", [P, 2, 2, T], F32, c1 + 9 * KB)
        s_feat = at("s_feat", [P, KT, T], F32, c1 + 18 * KB)
        x0_feat = at("x0_feat", [P, KT, T], F32, c1 + 34 * KB)
        g_spec = [scores[:, 0:2 * T].rearrange("p (a t) -> p a t", a=2), at("g_spec1", [P, 2, T], F32, c1 + 13 * KB)[:]]
        spec = at("spec", [P, 2, 4, T], F32, c1 + 50 * KB)
        hy_val_feat = at("hy_val_feat", [P, 4, T], F32, c1)
        sq_next = at("sq_next", [P, 2, T], F32, c1 + 50 * KB)
        acc_next = at("acc_next", [P, T], F32, c1 + 54 * KB)

        ps = ctx.enter_context(nc.psum_tensor("ps", [P, 8, T], F32))
        g_dram = nc.dram_tensor("g_dram", [2, 4, P, 2 * T], F32, kind="Internal").ap()

        c_dram = nc.dram_tensor("c_dram", [4, T], F32, kind="Internal").ap()

        x_in = [sem(f"x_in{i}") for i in range(4)]
        raw_in = [sem("raw_in0"), sem("raw_in1")]
        vecs_in, small_in, mem_in = sem("vecs_in"), sem("small_in"), sem("mem_in")
        tri_in, pool_in, late_in, mask_in, x_again = (sem(n) for n in (
            "tri_in", "pool_in", "late_in", "mask_in", "x_again"))
        g_out = [sem("g_out0"), sem("g_out1")]
        g_back = [sem("g_back0"), sem("g_back1")]
        hi_ready, lo_ready, hi_quarter = sem("hi_ready"), sem("lo_ready"), sem("hi_quarter")
        chunk_done, bank_read = sem("chunk_done"), sem("bank_read")
        made_ones = sem("made_ones")
        next_hi, next_lo, squared, summed = sem("next_hi"), sem("next_lo"), sem("squared"), sem("summed")
        norm_sum, norm_mean, norm_root, norm_rstd = sem("norm_sum"), sem("norm_mean"), sem("norm_root"), sem("norm_rstd")
        misc_done, misc_read = sem("misc_done"), sem("misc_read")
        vstep, gate_root = sem("vector_step"), sem("gate_root")
        gate_folded = sem("gate_folded")
        mlp_arg, mlp_sin = sem("mlp_arg"), sem("mlp_sin")
        rope_arg, rope_sin, roped = sem("rope_arg"), sem("rope_sin"), sem("roped")
        gate_z, gate_exp, gate_log, gate_ready = (sem(n) for n in ("gate_z", "gate_exp", "gate_log", "gate_ready"))
        sc_mul, sc_tap, sc_out, pooled = sem("sc_mul"), sem("sc_tap"), sem("sc_out"), sem("pooled")
        mix_hi, mix_lo = sem("mix_hi"), sem("mix_lo")
        mem_hi, mem_lo, mem_sq, mem_sum = sem("mem_hi"), sem("mem_lo"), sem("mem_sq"), sem("mem_sum")
        qk_done, masked, exped, probs_ready, transposed, pt_ready, pv_done, pv_hi, pv_lo = (sem(n) for n in (
            "qk_done", "masked", "exped", "probs_ready", "transposed", "pt_ready", "pv_done", "pv_hi", "pv_lo"))
        c_stored, c_keys_in = sem("c_stored"), [sem("c_keys_in0"), sem("c_keys_in1")]
        vt_done, vt_read = sem("vt_done"), sem("vt_read")
        gen_done, gen_exp, gen_taps, gen_abs, gen_fold, gen_hi, gen_lo = (sem(n) for n in (
            "gen_done", "gen_exp", "gen_taps", "gen_abs", "gen_fold", "gen_hi", "gen_lo"))
        decay_abs, fnorm_done, fnorm_read, g_staged = (sem(n) for n in ("decay_abs", "fnorm_done", "fnorm_read", "g_staged"))
        tapped, conved, gated, act_prod, act_hi, act_lo = (sem(n) for n in (
            "tapped", "conved", "gated", "act_prod", "act_hi", "act_lo"))
        hz_bias, hz_tap, hz_done = sem("hz_bias"), sem("hz_tap"), sem("hz_done")
        st_done, st_hi, st_lo = sem("st_done"), sem("st_hi"), sem("st_lo")
        spec_mul, spec_sum, y_hi, y_lo = sem("spec_mul"), sem("spec_sum"), sem("y_hi"), sem("y_lo")
        squared_next, summed_next, gen_acc, acc_zero = sem("squared_next"), sem("summed_next"), sem("gen_acc"), sem("acc_zero")
        skip_s, hy_val, u_hi, u_lo = sem("skip_s"), sem("hy_val"), sem("u_hi"), sem("u_lo")
        first_rstd, h2_scaled = sem("first_rstd"), sem("h2_scaled")
        h2_made, out_made, stored = sem("h2_made"), sem("out_made"), sem("stored")

        block = ctx.enter_context(nc.Block())

        def vec(name, i=0, n=1):
            return vecs[:, VEC[name] + i:VEC[name] + i + n]

        S_CHUNK = [2 * FIRST["dft_s0"] + j for j in range(4)] + [2 * FIRST[name] + j for name in ("dft_s1a", "dft_s1b") for j in range(2)]

        UNITS = [(s, i) for s in range(8) for i in range(NT)]
        SCORE_AT = [0, P, 3 * P, 6 * P]
        QUARTERS = ((0,), (1, 2), (3,), ())
        TAPS_AT = [0] * 4 + [1] * 4

        def unit_scores(u):
            start, tiles = (SCORE_AT[u % 4], u % 4 + 1) if u < 32 else (M * (u % 4), M // P)
            return scores[:, start:start + tiles * P]

        class Steps:

            def __init__(self, eng, counter):
                self.eng, self.counter, self.n, self.origin = eng, counter, 0, None

            def link(self, ins):
                ins.then_inc(self.counter, 1)
                self.n += 1
                self.eng.wait_ge(self.counter, self.n if self.origin is None else self.origin + self.n)

            def start(self, i, per):
                self.origin, self.per, self.before = i * per, per, self.n

            def end(self, count):
                assert self.n - self.before == self.per, (self.n - self.before, self.per)
                self.origin, self.n = None, self.before + count * self.per

        @block.sync
        def _(sp):
            sp.dma_start(raw[:, 0, :], a["weights"][0]).then_inc(raw_in[0], 16)
            for i in range(4):
                sp.dma_start(h[:, 2 * i:2 * i + 2, :], a["x_t"][:, 2 * i:2 * i + 2, :]).then_inc(x_in[i], 16)
            sp.dma_start(raw[:, 1, :], a["weights"][1]).then_inc(raw_in[1], 16)
            with sp.Fori(1, PAIRS // 2) as m:
                for p in range(2):
                    sp.wait_ge(lo_ready, 2 * m + (p - 1))
                    sp.dma_start(raw[:, p, :], a["weights"][bass.ds(2 * m + p, 1)].rearrange("o p n -> p (o n)")
                                 ).then_inc(raw_in[p], 16)

        @block.gpsimd
        def _(pool):
            pool.dma_start(gate_w[:], a["gate_w"]).then_inc(small_in, 16)
            pool.dma_start(mlp_w[:], a["mlp_w"]).then_inc(small_in, 16)
            pool.dma_start(mlp_b[:], a["mlp_b"]).then_inc(small_in, 16)
            pool.dma_start(feat[:], a["feat"]).then_inc(small_in, 16)
            pool.dma_start(pos[:], a["positions"]).then_inc(small_in, 16)
            pool.dma_start(rot[:], a["rot"]).then_inc(small_in, 16)
            pool.dma_start(ident[:], a["ident"]).then_inc(small_in, 16)
            pool.dma_start(mem_raw[:], a["mem_t"]).then_inc(mem_in, 16)
            pool.wait_ge(misc_done, 2)
            pool.wait_ge(next_lo, KT)
            pool.wait_ge(squared, KT)
            pool.dma_start(tri[:], a["tri"]).then_inc(tri_in, 16)
            pool.dma_start(pool_w[:], a["pool_w"]).then_inc(pool_in, 16)
            pool.dma_start(f_out[:], a["f_out"][:, :, 0:T]).then_inc(late_in, 16)
            pool.dma_start(decay[:], a["decay"][:, :, 0:T]).then_inc(late_in, 16)
            def load_keys(head):
                pool.dma_start(c_keys[head % 2][:], c_dram[head:head + 1, :].to_broadcast([P, T])).then_inc(c_keys_in[head % 2], 16)

            pool.wait_ge(misc_read, 16)
            pool.dma_start(c_dram, c_row[:]).then_inc(c_stored, 16)
            pool.wait_ge(pooled, 2)
            pool.wait_ge(misc_done, 20)
            pool.dma_start(mask[:], a["masks"][0]).then_inc(mask_in, 16)
            pool.wait_ge(c_stored, 16)
            load_keys(0)
            load_keys(1)
            for step in range(8):
                half = step // 4
                if step % 4 == 0:
                    pool.wait_ge(norm_mean, 2)
                    if half:
                        pool.wait_ge(fnorm_read, 1)
                    nc.gpsimd.memset(acc[:], 0.0).then_inc(acc_zero, 1)
                    pool.wait_ge(acc_zero, half + 1)
                if step in (5, 6):
                    pool.wait_ge(masked, 4 * step)
                    load_keys(step - 3)
                for d in range(2):
                    pool.wait_ge(gen_abs, 2 * step + d + 1)
                    nc.gpsimd.tensor_tensor(acc[:], acc[:], gen[:, 2 * d, :], ALU.add).then_inc(gen_acc, 1)
                    pool.wait_ge(gen_acc, 2 * step + d + 1)
                nc.gpsimd.tensor_tensor(gen[:, 0, :], gen[:, 1, :], gen[:, 3, :], ALU.add).then_inc(gen_fold, 1)
                nc.gpsimd.tensor_tensor(gen[:, 2, :], gen[:, 1, :], gen[:, 3, :], ALU.subtract).then_inc(gen_fold, 1)
                if step == 3:
                    pool.wait_ge(gen_exp, 8)
                    pool.wait_ge(gen_done, 4)
                    pool.dma_start(f_out[:], a["f_out"][:, :, T:2 * T]).then_inc(late_in, 16)
                    pool.dma_start(decay[:], a["decay"][:, :, T:2 * T]).then_inc(late_in, 16)
                    pool.wait_ge(masked, 16)
                    pool.dma_start(mask[:], a["masks"][1]).then_inc(mask_in, 16)
                if step % 4 == 3:
                    for j in range(4):
                        pool.wait_ge(g_staged, 4 * half + j + 1)
                        pool.dma_start(g_dram[half, j], gen[:, 2 * (j % 2):2 * (j % 2) + 2, :].rearrange("p a t -> p (a t)")
                                       ).then_inc(g_out[j % 2], 16)
            pool.wait_ge(gen_exp, 16)
            pool.wait_ge(gen_done, 8)
            pool.wait_ge(masked, 32)
            pool.wait_ge(vt_done, 4)
            pool.dma_start(h[:], a["x_t"]).then_inc(x_again, 16)
            pool.wait_ge(pv_done, 48)
            nc.gpsimd.memset(acc_next[:], 0.0).then_inc(summed_next, 2)
            pool.wait_ge(summed_next, 2)
            for k in range(KT):
                pool.wait_ge(squared_next, k + 1)
                nc.gpsimd.tensor_tensor(acc_next[:], acc_next[:], sq_next[:, k % 2, :], ALU.add).then_inc(summed_next, 1)
                pool.wait_ge(summed_next, k + 3)
            pool.wait_ge(first_rstd, 1)
            for k in range(KT):
                nc.gpsimd.tensor_tensor(h[:, k, :], h[:, k, :], acc_next[:], ALU.mult).then_inc(h2_scaled, 1)
            pool.wait_ge(h2_scaled, KT)
            for k in range(KT):
                nc.gpsimd.tensor_tensor(h[:, k, :], h[:, k, :], vec("g_final", k).to_broadcast([P, T]), ALU.mult
                                        ).then_inc(h2_made, 1)
            pool.wait_ge(h2_made, KT)
            pool.wait_ge(summed, 32)
            for p in range(2):
                pool.wait_ge(g_out[p], 64)

            def load_spectrum(n):
                pool.dma_start(g_spec[n % 2].rearrange("p a t -> p (a t)"), g_dram[n // 4, n % 4]).then_inc(g_back[n % 2], 16)

            load_spectrum(0)
            pool.wait_ge(hz_done, 16)
            load_spectrum(1)
            for n in range(8):
                t = spec[:, n % 2]
                pool.wait_ge(spec_mul, n + 1)
                if n + 2 < 8:
                    load_spectrum(n + 2)
                nc.gpsimd.tensor_tensor(t[:, 0, :], t[:, 0, :], t[:, 1, :], ALU.subtract).then_inc(spec_sum, 1)
                nc.gpsimd.tensor_tensor(t[:, 2, :], t[:, 2, :], t[:, 3, :], ALU.add).then_inc(spec_sum, 1)

        @block.scalar
        def _(act):
            A = nc.scalar

            def split_hi(m, p, first=False):
                act.wait_ge(raw_in[p], 16 * m + 16)
                if not first:
                    act.wait_ge(chunk_done, 4 * m + (2 * p - 2))
                A.copy(w_hi[:, p, :], raw[:, p, :]).then_inc(hi_ready, 1)

            def split_after(g):
                if g + 2 < PAIRS:
                    split_hi((g + 2) // 2, g % 2)

            def quarter_hi(g, q):
                if q == 0:
                    act.wait_ge(raw_in[g % 2], 16 * (g // 2 + 1) + 16)
                    act.wait_ge(chunk_done, 2 * g + 2)
                cols = slice(q * T, (q + 1) * T)
                A.copy(w_hi[:, g % 2, cols], raw[:, g % 2, cols]).then_inc(hi_ready if q == 3 else hi_quarter, 1)

            def root(i, width=T):
                act.wait_ge(norm_mean, i + 1 - (i > 5))
                A.activation(mean[:, 0:width], mean[:, 0:width], ACT.Sqrt).then_inc(norm_root, 1)

            act.dma_start(vecs[:], a["vecs"]).then_inc(vecs_in, 16)
            split_hi(0, 0, first=True)
            act.wait_ge(vecs_in, 16)
            for k in range(KT):
                act.wait_ge(x_in[k // 2], 16)
                A.activation(op_hi[0][:, k, :], h[:, k, :], ACT.Copy, scale=vec("g_mix", k)).then_inc(next_hi, 1)
            for k in range(KT):
                if k >= 2:
                    act.wait_ge(summed, k - 1)
                A.activation(sq[:, k % 2, :], h[:, k, :], ACT.Square).then_inc(squared, 1)
                if k == 1:
                    split_hi(0, 1, first=True)
            root(0)
            for r, table in enumerate((sin_t, cos_t)):
                act.wait_ge(rope_arg, r + 1)
                A.activation(table[:], ang[:] if r else turns[:], ACT.Sin).then_inc(rope_sin, 1)
            act.wait_ge(gate_z, 1)
            A.activation(rstd_tok[:], rstd_tok[:], ACT.Sqrt).then_inc(gate_root, 1)

            def mlp_sins(layer):
                for d in range(2):
                    act.wait_ge(mlp_arg, 2 * layer + d + 1)
                    A.activation(mlp_h[layer][:, d, :], mlp_x[:, d, :], ACT.Sin).then_inc(mlp_sin, 1)

            split_after(0)
            act.wait_ge(gate_z, 2)
            A.activation(gate_tmp[:, 1, :], gate_tmp[:, 1, :], ACT.Exp, scale=-1.0).then_inc(gate_exp, 1)
            act.wait_ge(gate_exp, 1)
            A.activation(gate_tmp[:, 2, :], gate_tmp[:, 1, :], ACT.Ln, bias=1.0).then_inc(gate_log, 1)
            mlp_sins(0)
            split_after(1)
            split_after(2)
            act.wait_ge(mem_in, 16)
            act.wait_ge(summed, KT)
            for r in range(4):
                if r >= 2:
                    act.wait_ge(mem_sum, r - 1)
                A.activation(sq[:, r % 2, :], mem_raw[:, 2 * r:2 * r + 2, :].rearrange("p k t -> p (k t)"),
                             ACT.Square).then_inc(mem_sq, 1)
            mlp_sins(1)
            split_after(3)
            mlp_sins(2)
            split_after(4)
            act.wait_ge(misc_done, 14)
            act.wait_ge(mlp_sin, 6)
            for k in range(KT):
                A.activation(mg_hi[:, k, :], mem_raw[:, k, :], ACT.Copy, scale=vec("g_mem", k)).then_inc(mem_hi, 1)
            split_after(5)
            split_after(6)
            for t in range(2):
                act.wait_ge(sc_mul, t + 1)
                A.activation(sc_y[:, t, :], sc_m[:, t, 2:2 + T], ACT.Copy, scale=vec("sconv", 2 * 2 + t)).then_inc(sc_tap, 1)
                split_after(7 + t)
                if t == 0:
                    for u in range(2):
                        act.wait_ge(misc_done, 19 + u)
                        A.activation(op_hi[1][:, 6 + u, :], ps[:, 6 + u % 2, :], ACT.Copy, scale=vec("pool_scale", u)
                                     ).then_inc(mix_hi, 1)

            def exp_unit(u):
                act.wait_ge(masked, u + 1)
                A.activation(unit_scores(u), unit_scores(u), ACT.Exp, scale=-1.0,
                             bias=low[:, u:u + 1], accum_out=total[:, u:u + 1]).then_inc(exped, 1)

            def copy_transposed(u, width):
                act.wait_ge(transposed, u + 1)
                if u >= 2:
                    act.wait_ge(pv_done, u - 1)
                A.copy(probs_t[:, u % 2, 0:width], ps[:, 6, 0:width]).then_inc(pt_ready, 1)

            def out_tile(t):
                act.wait_ge(pv_done, 8 * (t - 1))
                A.copy(op_hi[1][:, t, :], ps[:, 7, :]).then_inc(pv_hi, 1)

            def taps_hi(s):
                for d in range(2):
                    act.wait_ge(gen_fold, 2 * s + d + 1)
                    if s == 4:
                        act.wait_ge(chunk_done, 2 * FIRST["dft_g0"] + 4)
                    A.copy(op_hi[0][:, 4 * d + s % 4, :], gen[:, 2 * d, :]).then_inc(gen_hi, 1)

            exp_unit(0)
            for u, (s, i) in enumerate(UNITS):
                half, n = s // 4, s % 4
                g = (FIRST["k_mem"] if s < 4 else FIRST["v_mem"] - 4) + s
                if u + 1 < len(UNITS) and u != 15:
                    exp_unit(u + 1)
                if u == 0:
                    for t in range(2):
                        act.wait_ge(sc_out, t + 1)
                        A.copy(op_hi[1][:, t, :], sc_y[:, t, :]).then_inc(mix_hi, 1)
                    root(1, M)
                if u:
                    copy_transposed(u - 1, ((u - 1) % 4 + 1) * P)
                if i == 0 and s > 4:
                    taps_hi(s - 1)
                if i == TAPS_AT[s]:
                    act.wait_ge(decay_abs, half + 1)
                    if s > 0:
                        act.wait_ge(gen_lo, 2 * s)
                    if s == 4:
                        for p in range(2):
                            act.wait_ge(g_out[p], 32)
                    for d in range(2):
                        A.activation(gen[:, 2 * d, :], decay[:, d, :], ACT.Exp, scale=vec("neg_t", 4 * d + n)).then_inc(gen_exp, 1)
                if s != 4:
                    for q in QUARTERS[i]:
                        quarter_hi(g - 1, q)
                if i == TAPS_AT[s] + 1:
                    act.wait_ge(gen_taps, s + 1)
                    for d in range(2):
                        A.activation(gen[:, 2 * d, :], gen[:, 2 * d + 1, :], ACT.Abs).then_inc(gen_abs, 1)
                if i == 3 and s < 4:
                    taps_hi(s)
                if u in (9, 17, 25):
                    out_tile(2 + (u - 9) // 8)
                if u == 31:
                    copy_transposed(31, T)
                    out_tile(5)
                    taps_hi(7)
                if u % 16 == 15:
                    split_after(g)
                    if u == 15:
                        exp_unit(16)
                    split_after(g + 1)
                    split_after(g + 2)

            def tail(first, gname, dst, isq, iop):
                for k in range(KT):
                    g = FIRST[first] + k // 2
                    if k % 2 == 1 and k < 6:
                        split_after(g)
                    act.wait_ge(bank_read, 2 * FIRST[first] + k + 1)
                    act.wait_ge(summed, 8 * isq + k - 1)
                    if gname:
                        scale = gvec_first[:, k:k + 1] if gname == "gvec_first" else vec(gname, k)
                        A.activation(op_hi[dst][:, k, :], h[:, k, :], ACT.Copy, scale=scale).then_inc(next_hi, 1)
                    A.activation(sq[:, k % 2, :], h[:, k, :], ACT.Square).then_inc(squared, 1)
                    if gname == "gvec_first":
                        act.wait_ge(summed_next, k + 1)
                        A.activation(sq_next[:, k % 2, :], h[:, k, :], ACT.Square, scale=vec("g_final", k)).then_inc(squared_next, 1)
                split_after(FIRST[first] + 3)

            tail("w_out", "g_xa", 0, 1, 1)
            root(2)

            def exp_x(u):
                act.wait_ge(masked, 32 + u + 1)
                A.activation(unit_scores(32 + u), ps[:, 4 + u % 2, 0:M], ACT.Exp, scale=-1.0,
                             bias=low[:, u:u + 1], accum_out=total[:, u:u + 1]).then_inc(exped, 1)

            split_after(FIRST["xq"])
            split_after(FIRST["xq"] + 1)
            exp_x(0)
            for u in range(18):
                if u + 1 < 16:
                    exp_x(u + 1)
                if 1 <= u <= 16:
                    copy_transposed(32 + u - 1, M)
                if u >= 2:
                    v = u - 2
                    act.wait_ge(pv_done, 32 + v + 1)
                    A.copy(op_hi[1][:, 2 * (v // 4):2 * (v // 4) + 2, (v % 4) * P:(v % 4 + 1) * P],
                           ps[:, 7, 0:M].rearrange("p (a t) -> p a t", a=2)).then_inc(pv_hi, 1)
                if u in (3, 7):
                    split_after(FIRST["xq"] + 2 + u // 4)

            tail("xo", "g_ffn", 0, 2, 2)
            root(3)

            def ffn_up(section, count, base_tiles, gated_only):
                with act.Fori(0, count // 2) as i:
                    for p in range(2):
                        m = FIRST[section] // 2 + i
                        n = 2 * i + (base_tiles + p)
                        if not gated_only:
                            split_hi(m + 1, p)
                            for j in range(2):
                                act.wait_ge(bank_read, 4 * m + (2 * p + j + 1))
                                A.activation(conv[:, p, j, :], z_pad[:, p, j, 2:2 + T], ACT.Copy,
                                             scale=vecs[:, bass.ds(2 * i + (VEC["ffconv"] + 2 * 2 * FT + j * FT + base_tiles + p), 1)]
                                             ).then_inc(tapped, 1)
                            act.wait_ge(conved, n + 1)
                            A.activation(conv[:, p, 1, :], conv[:, p, 1, :], ACT.Silu).then_inc(gated, 1)
                        else:
                            act.wait_ge(bank_read, 4 * m + (2 * p + 1))
                            A.activation(conv[:, p, 0, :], z_pad[:, p, 0, 0:T], ACT.Silu).then_inc(gated, 1)
                            split_hi(m + 1, p)
                        act.wait_ge(act_prod, n + (FT * gated_only + 1))
                        A.copy(op_hi[1][:, bass.ds(2 * i + p, 1), :].rearrange("p a t -> p (a t)"),
                               conv[:, p, 0, :] if not gated_only else conv[:, p, 1, :]).then_inc(act_hi, 1)

            def ffn_down(section):
                with act.Fori(0, 2) as i:
                    for p in range(2):
                        split_hi(FIRST[section] // 2 + i + 1, p)

            for g in range(3):
                ffn_up(f"up1_{g}", FFN_GROUPS[g], 8 * g, 0)
                if g < 2:
                    ffn_down(f"down1_{g}")
            tail("down1_2", "gvec_first", 0, 3, 3)
            root(4)

            def hy_taps(i, p):
                m = FIRST["hy_in"] // 2 + i
                split_hi(m + 1, p)
                for j in range(2):
                    f = 4 * i + (2 * p + j)
                    act.wait_ge(bank_read, 4 * m + (2 * p + j + 1))
                    A.activation(z_pad[:, p, j, 1:1 + T], z_pad[:, p, j, 1:1 + T], ACT.Identity,
                                 bias=vecs[:, bass.ds(f + VEC["hy_b_in"], 1)]).then_inc(hz_bias, 1)
                    act.wait_ge(hz_bias, f + 1)
                    A.activation(conv[:, p, j, :], z_pad[:, p, j, 1:1 + T], ACT.Identity,
                                 scale=vecs[:, bass.ds(f + (VEC["hy_conv"] + 24), 1)],
                                 bias=vecs[:, bass.ds(f + VEC["hy_conv_b"], 1)]).then_inc(hz_tap, 1)

            with act.Fori(0, 4) as i:
                for p in range(2):
                    hy_taps(i, p)
            A.activation(acc_next[:], acc_next[:], ACT.Sqrt).then_inc(norm_root, 1)
            for q in range(4):
                hy_taps(4 + q // 2, q % 2)
                for n in (2 * q, 2 * q + 1):
                    act.wait_ge(st_done, n + 1)
                    A.copy(op_hi[1][:, n, :], ps[:, 4 + n % 4, :]).then_inc(st_hi, 1)
            def spectrum_hi(n):
                if n == 4:
                    act.wait_ge(chunk_done, 2 * FIRST["idft_0"] + 4)
                for r in range(2):
                    act.wait_ge(spec_sum, 2 * n + r + 1)
                    A.copy(op_hi[0][:, 2 * (n % 4) + r, :], spec[:, n % 2, 2 * r, :]).then_inc(y_hi, 1)

            def skips(half):
                for c in range(4 * half, 4 * half + 4):
                    if half:
                        act.wait_ge(u_lo, c - 3)
                    A.activation(hy_val_feat[:, c % 4, :], s_feat[:, c, :], ACT.Copy, scale=vec("hy_skip", c)).then_inc(skip_s, 1)

            def hyena_out_hi(half):
                for c in range(4 * half, 4 * half + 4):
                    act.wait_ge(hy_val, c + 1)
                    A.copy(op_hi[1][:, c, :], hy_val_feat[:, c % 4, :]).then_inc(u_hi, 1)

            s0, s1a, i0, s1b, i1 = (FIRST[name] for name in ("dft_s0", "dft_s1a", "idft_0", "dft_s1b", "idft_1"))
            spectrum_hi(0)
            split_after(s0)
            spectrum_hi(1)
            spectrum_hi(2)
            split_after(s0 + 1)
            spectrum_hi(3)
            split_after(s1a)
            skips(0)
            split_after(i0)
            spectrum_hi(4)
            spectrum_hi(5)
            split_after(i0 + 1)
            spectrum_hi(6)
            hyena_out_hi(0)
            split_after(s1b)
            spectrum_hi(7)
            skips(1)
            split_after(i1)
            split_after(i1 + 1)
            hyena_out_hi(1)
            tail("hy_out", "norm_ffn_2", 0, 4, 4)
            root(6)
            for g in range(3):
                ffn_up(f"up2_{g}", FFN_GROUPS[g], 8 * g, 1)
                if g < 2:
                    ffn_down(f"down2_{g}")
            act.wait_ge(norm_rstd, 6)
            A.activation(mean[:, 0:1], mean[:, 0:1], ACT.Sqrt)
            tail("down2_2", None, None, 5, None)
            root(7)
            for q in range(4):
                act.wait_ge(out_made, 2 * q + 2)
                act.dma_start(a["out"][:, 2 * q:2 * q + 2, :], h[:, 2 * q:2 * q + 2, :]).then_inc(stored, 16)
            act.wait_ge(stored, 64)

        @block.vector
        def _(dve):
            V = nc.vector
            S = Steps(dve, vstep)

            def split_lo(m, p):
                dve.wait_ge(hi_ready, 2 * m + (p + 1))
                V.tensor_tensor(w_lo[:, p, :], raw[:, p, :], w_hi[:, p, :].bitcast(F32), ALU.subtract).then_inc(lo_ready, 1)

            def split_after(g):
                if g + 2 < PAIRS:
                    split_lo((g + 2) // 2, g % 2)

            def quarter_lo(g, q, done):
                if q == 3:
                    dve.wait_ge(hi_ready, g + 3)
                else:
                    dve.wait_ge(hi_quarter, 3 * done + q + 1)
                cols = slice(q * T, (q + 1) * T)
                ins = V.tensor_tensor(w_lo[:, g % 2, cols], raw[:, g % 2, cols], w_hi[:, g % 2, cols].bitcast(F32), ALU.subtract)
                if q == 3:
                    ins.then_inc(lo_ready, 1)

            def product(c):
                dve.wait_ge(chunk_done, c + 1)

            def evac(c, out, scale=None, width=T, bank=None):
                product(c)
                bank = c % 4 if bank is None else bank
                if scale is None:
                    return V.tensor_tensor(out, ps[:, bank, 0:width], rstd[:, 0:width], ALU.mult).then_inc(bank_read, 1)
                return V.scalar_tensor_tensor(out, ps[:, bank, 0:width], scale, rstd[:, 0:width], ALU.mult,
                                              ALU.mult).then_inc(bank_read, 1)

            def misc(j):
                dve.wait_ge(misc_done, j + 1)
                return ps[:, 6 + j % 2, :]

            def finish_norm(i, src, width=T):
                V.tensor_scalar(mean[:, 0:width], src, 1.0 / D, EPS, ALU.mult, ALU.add).then_inc(norm_mean, 1)
                dve.wait_ge(norm_root, i + 1)
                V.reciprocal(rstd[:, 0:width], mean[:, 0:width]).then_inc(norm_rstd, 1)
                dve.wait_ge(norm_rstd, i + 1 - (i > 5))

            def lo_part(out, src, hi):
                return V.tensor_tensor(out, src, hi.bitcast(F32), ALU.subtract)

            V.memset(ones[:], 1.0).then_inc(made_ones, 1)
            S.link(V.memset(acc[:], 0.0))
            split_lo(0, 0)
            dve.wait_ge(vecs_in, 16)
            for k in range(KT):
                dve.wait_ge(next_hi, k + 1)
                V.scalar_tensor_tensor(op_lo[0][:, k, :], h[:, k, :], vec("g_mix", k), op_hi[0][:, k, :].bitcast(F32),
                                       ALU.mult, ALU.subtract).then_inc(next_lo, 1)
            for k in range(KT):
                if k == 2:
                    split_lo(0, 1)
                dve.wait_ge(squared, k + 1)
                V.tensor_tensor(acc[:], acc[:], sq[:, k % 2, :], ALU.add).then_inc(summed, 1)
                dve.wait_ge(summed, k + 1)
            dve.wait_ge(small_in, 112)
            V.tensor_tensor(gate_w[:], gate_w[:], vec("g_mix", 0, 8).unsqueeze(2).to_broadcast([P, KT, 4]),
                            ALU.mult).then_inc(gate_folded, 1)
            bank = misc(0)
            V.tensor_scalar(mean[:], bank, 1.0 / D, EPS, ALU.mult, ALU.add).then_inc(norm_mean, 1)
            dve.wait_ge(norm_mean, 1)
            V.engine_nop().then_inc(misc_read, 1)
            dve.wait_ge(norm_root, 1)
            V.reciprocal(rstd[:], mean[:]).then_inc(norm_rstd, 1)
            dve.wait_ge(norm_rstd, 1)

            def reduce_turns(out, x, k, offset=0.0):
                if offset:
                    S.link(V.tensor_scalar(k, x, INV_2PI, offset, ALU.mult, ALU.add))
                    S.link(V.tensor_scalar(k, k, MAGIC, None, ALU.add))
                else:
                    S.link(V.tensor_scalar(k, x, INV_2PI, MAGIC, ALU.mult, ALU.add))
                S.link(V.tensor_scalar(k, k, MAGIC, None, ALU.subtract))
                S.link(V.scalar_tensor_tensor(out, k, -C1, x, ALU.mult, ALU.add))
                S.link(V.scalar_tensor_tensor(out, k, -C2, out, ALU.mult, ALU.add))
                S.link(V.scalar_tensor_tensor(out, k, -C3, out, ALU.mult, ALU.add))

            S.link(V.tensor_copy(ang[:], pos[:]))
            S.link(V.tensor_scalar(ang[:], ang[:], vec("inv_freq"), None, ALU.mult))
            reduce_turns(turns[:], ang[:], rope_tmp[:, 0, :])
            V.tensor_scalar(turns[:], turns[:], PI_IN, -PI_IN, ALU.min, ALU.max).then_inc(rope_arg, 1)
            reduce_turns(ang[:], ang[:], rope_tmp[:, 0, :], 0.25)
            S.link(V.tensor_scalar(ang[:], ang[:], HALF_PI, None, ALU.add))
            V.tensor_scalar(ang[:], ang[:], PI_IN, -PI_IN, ALU.min, ALU.max).then_inc(rope_arg, 1)
            bank = misc(1)
            V.tensor_scalar(rstd_tok[:], bank[:, 16:20], 1.0 / D, EPS, ALU.mult, ALU.add).then_inc(gate_z, 1)
            S.link(V.tensor_copy(gate_tmp[:, 0, :], bank[:, 0:16]))
            V.engine_nop().then_inc(misc_read, 1)
            for j in range(2):
                evac(j, qk[:, j, :], -0.125)
            split_after(0)
            dve.wait_ge(gate_root, 1)
            S.link(V.reciprocal(rstd_tok[:], rstd_tok[:]))
            for i in range(NT):
                last = V.scalar_tensor_tensor(gate_tmp[:, 0, 4 * i:4 * i + 4], gate_tmp[:, 0, 4 * i:4 * i + 4],
                                              rstd_tok[:, i:i + 1], vec("b_forget", 4 * i, 4), ALU.mult, ALU.add)
            S.link(last)
            V.scalar_tensor_tensor(gate_tmp[:, 1, :], gate_tmp[:, 0, :], -1.0, gate_tmp[:, 0, :], ALU.mult, ALU.max).then_inc(gate_z, 1)

            def mlp_args(layer):
                for d in range(2):
                    bank = misc(MLP_JOB[layer] + d)
                    x = mlp_x[:, d, :]
                    if layer > 0:
                        dve.wait_ge(mlp_sin, 2 * layer)
                    V.tensor_scalar(x, bank[0:64, :], mlp_b[:, layer:layer + 1], mlp_b[:, 3:4], ALU.add,
                                    ALU.mult).then_inc(misc_read, 1)
                    dve.wait_ge(misc_read, MLP_JOB[layer] + d + 1)
                    reduce_turns(x, x, mlp_k[:])
                    V.tensor_scalar(x, x, PI_IN, -PI_IN, ALU.min, ALU.max).then_inc(mlp_arg, 1)

            mlp_args(0)
            for j in range(2):
                evac(2 + j, qk[:, 2 + j, :])
            split_after(1)
            def rope(first_tile, job):
                dve.wait_ge(rope_sin, 2)
                for j in range(2):
                    t = qk[:, first_tile + j, :]
                    bank = misc(job + j)
                    V.tensor_tensor(rope_tmp[:, j, :], bank, sin_t[:], ALU.mult).then_inc(misc_read, 1)
                    dve.wait_ge(misc_read, job + j + 1)
                    S.link(V.tensor_tensor(t, t, cos_t[:], ALU.mult))
                    V.tensor_tensor(t, t, rope_tmp[:, j, :], ALU.add).then_inc(roped, 1)

            rope(0, 4)
            for j in range(2):
                evac(4 + j, v_raw[:, j, :])
            split_after(2)

            dve.wait_ge(gate_log, 1)
            V.scalar_tensor_tensor(log_f[:].rearrange("p i h -> p (i h)"), gate_tmp[:, 0, :], 0.0, gate_tmp[:, 2, :], ALU.min,
                                   ALU.subtract).then_inc(gate_ready, 1)
            rope(2, 6)
            S.link(V.memset(acc[:], 0.0))
            for r in range(4):
                dve.wait_ge(mem_sq, r + 1)
                V.tensor_tensor(acc[:], acc[:], sq[:, r % 2, :], ALU.add).then_inc(mem_sum, 1)
                dve.wait_ge(mem_sum, r + 1)
            V.tensor_tensor(acc[:, 0:M], acc[:, 0:M], acc[:, M:2 * M], ALU.add).then_inc(mem_sum, 1)
            mlp_args(1)
            for j in range(2):
                evac(6 + j, qk[:, 4 + j, :], -0.125)

            def v_tokens(m, job):
                for b in range(2):
                    bank = misc(job + b)
                    V.tensor_copy(v_tok[:, 2 * b:2 * b + 2, M * m:M * m + M], bank.rearrange("p (i f) -> p i f", i=2)
                                  ).then_inc(misc_read, 1)

            v_tokens(0, 10)
            split_after(3)

            mlp_args(2)
            for j in range(2):
                evac(8 + j, qk[:, 6 + j, :])
            split_after(4)
            bank = misc(14)
            V.tensor_copy(c_tok[:].rearrange("p i h -> p (i h)"), bank[:, 0:16]).then_inc(misc_read, 1)
            bank = misc(15)
            V.tensor_copy(c_row[:], bank[0:4, :]).then_inc(misc_read, 1)
            for j in range(2):
                evac(10 + j, v_raw[:, j, :])
            split_after(5)
            for k in range(KT):
                dve.wait_ge(mem_hi, k + 1)
                V.scalar_tensor_tensor(mg_lo[:, k, :], mem_raw[:, k, :], vec("g_mem", k), mg_hi[:, k, :].bitcast(F32),
                                       ALU.mult, ALU.subtract).then_inc(mem_lo, 1)
            v_tokens(1, 16)
            V.memset(pool_x[:, :, 0:16], 0.0)
            V.memset(pool_a[:, :, 0:16], 0.0)
            S.link(V.memset(pool_b[:, :, 0:16], 0.0))
            for j in range(2):
                evac(12 + j, pool_x[:, j, 16:16 + T])
            split_after(6)
            dve.wait_ge(bank_read, 14)
            S.link(V.tensor_tensor(pool_a[:, :, 1:], pool_x[:, :, 1:], pool_x[:, :, 0:527], ALU.add))
            S.link(V.tensor_tensor(pool_b[:, :, 3:], pool_a[:, :, 3:], pool_a[:, :, 1:526], ALU.add))
            S.link(V.tensor_copy(pool_a[64:128, 0, 16:], pool_b[64:128, 0, 16:]))
            S.link(V.tensor_tensor(pool_a[:, 1, 7:], pool_b[:, 1, 7:], pool_b[:, 1, 3:524], ALU.add))
            S.link(V.tensor_tensor(pool_b[64:128, 1, 15:], pool_a[64:128, 1, 15:], pool_a[64:128, 1, 7:520], ALU.add))
            S.link(V.tensor_copy(pool_a[64:128, 1, 16:], pool_b[64:128, 1, 16:]))
            for j in range(2):
                S.link(V.tensor_tensor(pool_b[:, j, 0:16], pool_a[:, j, 16:32], vec("pool_edge", 16 * j, 16), ALU.mult))
                S.link(V.scalar_tensor_tensor(pool_a[:, j, 16:], pool_a[:, j, 16:], vec("pool_inv", j), pool_x[:, j, 16:],
                                              ALU.mult, ALU.subtract))
                V.tensor_tensor(pool_a[:, j, 16:32], pool_b[:, j, 0:16], pool_x[:, j, 16:32], ALU.subtract).then_inc(pooled, 1)
            V.memset(sc_m[:, :, 0:2], 0.0)
            for t in range(2):
                evac(14 + 2 * t, sc_c[:])
                evac(15 + 2 * t, sc_m[:, t, 2:2 + T])
                dve.wait_ge(bank_read, 16 + 2 * t)
                V.tensor_tensor(sc_m[:, t, 2:2 + T], sc_m[:, t, 2:2 + T], sc_c[:], ALU.mult).then_inc(sc_mul, 1)
                dve.wait_ge(sc_mul, t + 1)
                split_after(7 + t)
                if t == 0:
                    for u in range(2):
                        bank = misc(18 + u)
                        dve.wait_ge(mix_hi, u + 1)
                        V.scalar_tensor_tensor(op_lo[1][:, 6 + u, :], bank, vec("pool_scale", u),
                                               op_hi[1][:, 6 + u, :].bitcast(F32), ALU.mult, ALU.subtract).then_inc(mix_lo, 1)
                        dve.wait_ge(mix_lo, u + 1)
                        V.engine_nop().then_inc(misc_read, 1)
                    dve.wait_ge(late_in, 32)
                    V.scalar_tensor_tensor(decay[:], decay[:], -1.0, decay[:], ALU.mult, ALU.max).then_inc(decay_abs, 1)
            for t in range(2):
                dve.wait_ge(sc_tap, t + 1)
                S.link(V.scalar_tensor_tensor(sc_y[:, t, :], sc_m[:, t, 1:1 + T], vec("sconv", 2 + t), sc_y[:, t, :],
                                              ALU.mult, ALU.add))
                S.link(V.scalar_tensor_tensor(sc_y[:, t, :], sc_m[:, t, 0:T], vec("sconv", t), sc_y[:, t, :],
                                              ALU.mult, ALU.add))
                S.link(V.tensor_tensor(sc_y[:, t, :], sc_y[:, t, :], rstd[:], ALU.mult))
                product(18 + t)
                S.link(V.tensor_tensor(sc_y[:, t, :], sc_y[:, t, :], ps[:, (18 + t) % 4, :], ALU.mult))
                V.engine_nop().then_inc(sc_out, 1)
                dve.wait_ge(sc_out, t + 1)
                V.engine_nop().then_inc(bank_read, 1)

            def finish_inputs():
                for t in range(2):
                    dve.wait_ge(mix_hi, 3 + t)
                    lo_part(op_lo[1][:, t, :], sc_y[:, t, :], op_hi[1][:, t, :]).then_inc(mix_lo, 1)
                bank = misc(20)
                finish_norm(1, bank[:, 0:M], M)
                V.engine_nop().then_inc(misc_read, 1)

            def mask_unit(u):
                s, i = UNITS[u]
                n = (i + 1) * P
                strip = mask[:, (3 - i) * P:T]
                if s >= 4:
                    if i == 0:
                        dve.wait_ge(c_keys_in[s % 2], 16 * ((s - 4) // 2 + 1))
                    if u == 16:
                        dve.wait_ge(mask_in, 32)
                    if u > 16:
                        dve.wait_ge(masked, u)
                    S.link(V.scalar_tensor_tensor(bias[:, 0:n], c_keys[s % 2][:, 0:n], c_tok[:, i, s - 4:s - 3], strip,
                                                  ALU.subtract, ALU.add))
                    strip = bias[:, 0:n]
                if u == 0:
                    dve.wait_ge(mask_in, 16)
                dve.wait_ge(qk_done, u + 1)
                if u >= 4:
                    dve.wait_ge(transposed, u - 3)
                V.tensor_tensor_reduce(unit_scores(u), ps[:, 4 + u % 2, 0:n], strip, 1.0, 3e38, ALU.add, ALU.min,
                                       low[:, u:u + 1]).then_inc(masked, 1)

            def normalise(u, v):
                dve.wait_ge(exped, u + 1)
                S.link(V.reciprocal(inv_total[:, v:v + 1], total[:, v:v + 1]))
                V.tensor_scalar(unit_scores(u), unit_scores(u), inv_total[:, v:v + 1], None, ALU.mult).then_inc(probs_ready, 1)

            def taps_lo(s):
                for d in range(2):
                    dve.wait_ge(gen_hi, 2 * s + d + 1)
                    lo_part(op_lo[0][:, 4 * d + s % 4, :], gen[:, 2 * d, :], op_hi[0][:, 4 * d + s % 4, :]).then_inc(gen_lo, 1)
                dve.wait_ge(gen_lo, 2 * s + 2)

            def mem_values(hd):
                dve.wait_ge(vt_done, hd + 1)
                V.tensor_copy(v_mem[:, :, hd * M:(hd + 1) * M], ps[:, 2, :].rearrange("p (b f) -> p b f", b=2)).then_inc(vt_read, 1)

            mask_unit(0)
            for u, (s, i) in enumerate(UNITS):
                half, n = s // 4, s % 4
                g = (FIRST["k_mem"] if s < 4 else FIRST["v_mem"] - 4) + s
                if u + 1 < len(UNITS) and u != 15:
                    mask_unit(u + 1)
                normalise(u, u)
                if u == 0:
                    finish_inputs()
                if i == 0 and s > 4:
                    mem_values(s - 5)
                if i == 0 and s > 4:
                    taps_lo(s - 1)
                if i == TAPS_AT[s]:
                    dve.wait_ge(gen_done, s + 1)
                    for d in range(2):
                        dve.wait_ge(gen_exp, 2 * s + d + 1)
                        S.link(V.tensor_tensor(gen[:, 2 * d + 1, :], ps[:, 2 + d, :], gen[:, 2 * d, :], ALU.mult))
                        if d == 1 and n == 0:
                            S.link(V.memset(gen[0:1, 3, :], 0.0))
                    V.engine_nop().then_inc(gen_taps, 1)
                if s != 4:
                    for q in QUARTERS[i]:
                        quarter_lo(g - 1, q, s - half)
                if i % 2 == 1:
                    c = 2 * g + i // 2
                    dst = k_mem[:, 2 * s + i // 2, :] if s < 4 else v_stage[:, i // 2, :]
                    if s > 4:
                        dve.wait_ge(vt_done, s - 4)
                    evac(c, dst, None, M, bank=c % 2)
                if i == 3 and (s < 4 or s == 7):
                    taps_lo(s)
                if u in (9, 17, 25, 31):
                    t = 2 + (u - 7) // 8
                    dve.wait_ge(pv_hi, t - 1)
                    lo_part(op_lo[1][:, t, :], ps[:, 7, :], op_hi[1][:, t, :]).then_inc(pv_lo, 1)
                if u == 31:
                    mem_values(3)
                if i == 3 and n == 3:
                    dve.wait_ge(fnorm_done, half + 1)
                    V.reciprocal(filter_norm[:, 4 * half:4 * half + 4], ps[:, 3, 0:4]).then_inc(fnorm_read, 1)
                    if half == 0:
                        dve.wait_ge(late_in, 64)
                        V.scalar_tensor_tensor(decay[:], decay[:], -1.0, decay[:], ALU.mult, ALU.max).then_inc(decay_abs, 1)
                    for j in range(4):
                        c = 2 * FIRST[f"dft_g{half}"] + j
                        if j == 0:
                            split_after(FIRST[f"dft_g{half}"] - 1)
                        product(c)
                        if j >= 2:
                            dve.wait_ge(g_out[j % 2], 32 * half + 16)
                        for r in range(2):
                            last = V.tensor_copy(gen[:, 2 * (j % 2) + r, :], ps[:, 2 * (j % 2) + r, :])
                            if r == 0:
                                S.link(last)
                        last.then_inc(g_staged, 1)
                        dve.wait_ge(g_staged, 4 * half + j + 1)
                        V.engine_nop().then_inc(bank_read, 1)
                        if j == 1 and half == 0:
                            mask_unit(16)
                        if j % 2:
                            split_after(FIRST[f"dft_g{half}"] + j // 2)

            def tail(first, gname, dst, isq, iop, bias_name=None):
                S.link(V.memset(acc[:], 0.0))
                if iop == 4:
                    dve.wait_ge(h2_made, KT)
                for k in range(KT):
                    c = 2 * FIRST[first] + k
                    product(c)
                    if bias_name:
                        V.scalar_tensor_tensor(h[:, k, :], ps[:, c % 4, :], vec(bias_name, k), h[:, k, :], ALU.add,
                                               ALU.add).then_inc(bank_read, 1)
                    else:
                        V.tensor_tensor(h[:, k, :], ps[:, c % 4, :], h[:, k, :], ALU.add).then_inc(bank_read, 1)
                    if k % 2 == 1 and k < 6:
                        split_after(c // 2)
                    if gname:
                        scale = gvec_first[:, k:k + 1] if gname == "gvec_first" else vec(gname, k)
                        dve.wait_ge(next_hi, 8 * iop + k + 1)
                        V.scalar_tensor_tensor(op_lo[dst][:, k, :], h[:, k, :], scale, op_hi[dst][:, k, :].bitcast(F32), ALU.mult,
                                               ALU.subtract).then_inc(next_lo, 1)
                    dve.wait_ge(squared, 8 * isq + k + 1)
                    V.tensor_tensor(acc[:], acc[:], sq[:, k % 2, :], ALU.add).then_inc(summed, 1)
                    dve.wait_ge(summed, 8 * isq + k + 1)
                split_after(FIRST[first] + 3)

            def norm(i):
                dve.wait_ge(norm_sum, i - 1)
                finish_norm(i, ps[:, 7, :])

            dve.wait_ge(x_again, 16)
            tail("w_out", "g_xa", 0, 1, 1)
            norm(2)
            def evac_xq(q):
                for j in range(2):
                    evac(2 * (FIRST["xq"] + q) + j, xq[:, 2 * q + j, :], -1.0 / 16.0)
                split_after(FIRST["xq"] + q)

            def lowest(u):
                dve.wait_ge(qk_done, 32 + u + 1)
                V.tensor_reduce(low[:, u:u + 1], ps[:, 4 + u % 2, 0:M], AX.X, ALU.min).then_inc(masked, 1)

            evac_xq(0)
            evac_xq(1)
            lowest(0)
            for u in range(18):
                if u + 1 < 16:
                    lowest(u + 1)
                if u < 16:
                    normalise(32 + u, u)
                if u >= 2:
                    v = u - 2
                    dve.wait_ge(pv_hi, 4 + v + 1)
                    lo_part(op_lo[1][:, 2 * (v // 4):2 * (v // 4) + 2, (v % 4) * P:(v % 4 + 1) * P],
                            ps[:, 7, 0:M].rearrange("p (a t) -> p a t", a=2),
                            op_hi[1][:, 2 * (v // 4):2 * (v // 4) + 2, (v % 4) * P:(v % 4 + 1) * P]).then_inc(pv_lo, 1)
                if u in (3, 7):
                    evac_xq(2 + u // 4)
            tail("xo", "g_ffn", 0, 2, 2)
            norm(3)
            V.memset(z_pad[:, :, :, 0:2], 0.0)
            S.link(V.tensor_tensor(gvec_first[:], vec("g_final", 0, 8), vec("norm_mix_2", 0, 8), ALU.mult))

            def conv_up(section, count, base_tiles):
                with dve.Fori(0, count // 2) as i:
                    S.start(i, 6)
                    for p in range(2):
                        m = FIRST[section] // 2 + i
                        n = 2 * i + (base_tiles + p)
                        for j in range(2):
                            product(4 * m + (2 * p + j))
                            V.tensor_tensor(z_pad[:, p, j, 2:2 + T], ps[:, 2 * p + j, :], rstd[:], ALU.mult).then_inc(bank_read, 1)
                        split_lo(m + 1, p)
                        dve.wait_ge(bank_read, 4 * m + (2 * p + 2))
                        for j in (1, 0):
                            dve.wait_ge(tapped, 4 * i + (2 * base_tiles + 2 * p + 2))
                            for tap in (1, 0):
                                ins = V.scalar_tensor_tensor(
                                    conv[:, p, j, :], z_pad[:, p, j, tap:tap + T],
                                    vecs[:, bass.ds(2 * i + (VEC["ffconv"] + tap * 2 * FT + j * FT + base_tiles + p), 1)],
                                    conv[:, p, j, :], ALU.mult, ALU.add)
                                if j == 1 and tap == 0:
                                    ins.then_inc(conved, 1)
                                else:
                                    S.link(ins)
                        dve.wait_ge(gated, n + 1)
                        V.tensor_tensor(conv[:, p, 0, :], conv[:, p, 0, :], conv[:, p, 1, :], ALU.mult).then_inc(act_prod, 1)
                        dve.wait_ge(act_hi, n + 1)
                        lo_part(op_lo[1][:, bass.ds(2 * i + p, 1), :].rearrange("p a t -> p (a t)"), conv[:, p, 0, :],
                                op_hi[1][:, bass.ds(2 * i + p, 1), :].rearrange("p a t -> p (a t)")).then_inc(act_lo, 1)
                    S.end(count // 2)

            def down(section):
                with dve.Fori(0, 2) as i:
                    for p in range(2):
                        m = FIRST[section] // 2 + i
                        for j in range(2):
                            product(4 * m + (2 * p + j))
                            hd = h[:, bass.ds(4 * i + (2 * p + j), 1), :].rearrange("p a t -> p (a t)")
                            V.tensor_tensor(hd, ps[:, 2 * p + j, :], hd, ALU.add).then_inc(bank_read, 1)
                        split_lo(m + 1, p)
                dve.wait_ge(bank_read, 2 * FIRST[section] + 8)

            for g in range(3):
                conv_up(f"up1_{g}", FFN_GROUPS[g], 8 * g)
                if g < 2:
                    down(f"down1_{g}")
            tail("down1_2", "gvec_first", 0, 3, 3)
            dve.wait_ge(norm_sum, 4)
            S.link(V.tensor_scalar(acc_next[:], ps[:, 7, :], 1.0 / D, EPS, ALU.mult, ALU.add))
            S.link(V.tensor_scalar(mean[:], acc_next[:], EPS, None, ALU.mult))
            V.scalar_tensor_tensor(mean[:], ps[:, 6, :], 1.0 / D, mean[:], ALU.mult, ALU.add).then_inc(norm_mean, 1)
            dve.wait_ge(norm_root, 5)
            V.reciprocal(rstd[:], mean[:]).then_inc(norm_rstd, 1)
            dve.wait_ge(norm_rstd, 5)

            V.memset(z_pad[:, :, :, 0:1], 0.0)
            S.link(V.memset(z_pad[:, :, :, 1 + T:2 + T], 0.0))
            hy_pairs = FIRST["hy_in"]

            def hy_conv(i, p, finish):
                m = hy_pairs // 2 + i
                for j in range(2):
                    product(4 * m + (2 * p + j))
                    V.tensor_tensor(z_pad[:, p, j, 1:1 + T], ps[:, 2 * p + j, :], rstd[:], ALU.mult).then_inc(bank_read, 1)
                split_lo(m + 1, p)
                for j in range(2):
                    f = 4 * i + (2 * p + j)
                    dve.wait_ge(hz_tap, f + 1)
                    S.link(V.scalar_tensor_tensor(conv[:, p, j, :], z_pad[:, p, j, 0:T],
                                                  vecs[:, bass.ds(f + VEC["hy_conv"], 1)], conv[:, p, j, :], ALU.mult, ALU.add))
                    finish(j, V.scalar_tensor_tensor, z_pad[:, p, j, 2:2 + T], vecs[:, bass.ds(f + (VEC["hy_conv"] + 48), 1)],
                           conv[:, p, j, :])

            with dve.Fori(0, 4) as i:
                S.start(i, 8)
                for p in range(2):
                    def into_s(j, stt, z, w, c):
                        S.link(stt(c, z, w, c, ALU.mult, ALU.add))
                        if j == 1:
                            V.tensor_tensor(s_feat[:, bass.ds(2 * i + p, 1), :].rearrange("p a t -> p (a t)"), conv[:, p, 0, :],
                                            conv[:, p, 1, :], ALU.mult).then_inc(hz_done, 1)
                    hy_conv(i, p, into_s)
                S.end(4)
            dve.wait_ge(norm_root, 6)
            V.reciprocal(acc_next[:], acc_next[:]).then_inc(first_rstd, 1)
            for q in range(4):
                def into_x0(j, stt, z, w, c):
                    stt(x0_feat[:, 2 * q + j, :], z, w, c, ALU.mult, ALU.add).then_inc(hz_done, 1)
                hy_conv(4 + q // 2, q % 2, into_x0)
                for n in (2 * q, 2 * q + 1):
                    dve.wait_ge(st_hi, n + 1)
                    lo_part(op_lo[1][:, n, :], ps[:, 4 + n % 4, :], op_hi[1][:, n, :]).then_inc(st_lo, 1)
            def spectrum_products(n):
                b = 2 * (n % 2)
                c = S_CHUNK[n]
                product(c)
                dve.wait_ge(g_back[n % 2], 16 * (n // 2 + 1))
                if n >= 2:
                    dve.wait_ge(y_hi, 2 * n - 2)
                    dve.wait_ge(y_lo, 2 * n - 2)
                gr, gi, t = g_spec[n % 2][:, 0, :], g_spec[n % 2][:, 1, :], spec[:, n % 2]
                V.tensor_tensor(t[:, 0, :], ps[:, b, :], gr, ALU.mult)
                V.tensor_tensor(t[:, 1, :], ps[:, b + 1, :], gi, ALU.mult)
                V.tensor_tensor(t[:, 2, :], ps[:, b, :], gi, ALU.mult)
                V.tensor_tensor(t[:, 3, :], ps[:, b + 1, :], gr, ALU.mult).then_inc(bank_read, 1)
                dve.wait_ge(bank_read, c + 1)
                if n % 4 == 0:
                    S.link(V.tensor_copy(t[0:1, 2, :], t[0:1, 1, :]))
                    V.memset(t[0:1, 3, :], 0.0)
                    S.link(V.memset(t[0:1, 1, :], 0.0))
                V.engine_nop().then_inc(spec_mul, 1)

            def spectrum_lo(n):
                for r in range(2):
                    dve.wait_ge(y_hi, 2 * n + r + 1)
                    lo_part(op_lo[0][:, 2 * (n % 4) + r, :], spec[:, n % 2, 2 * r, :], op_hi[0][:, 2 * (n % 4) + r, :]
                            ).then_inc(y_lo, 1)

            def hyena_sums(half):
                dve.wait_ge(chunk_done, 2 * FIRST[f"idft_{half}"] + 4)
                dve.wait_ge(skip_s, 4 * half + 4)
                for t in range(4):
                    y = hy_val_feat[:, t, :]
                    V.scalar_tensor_tensor(y, ps[:, 4 + t, :], filter_norm[:, 4 * half + t:4 * half + t + 1], y, ALU.mult,
                                           ALU.add).then_inc(bank_read, 1)

            def hyena_products(half):
                dve.wait_ge(bank_read, 2 * FIRST[f"idft_{half}"] + 4)
                for t in range(4):
                    y = hy_val_feat[:, t, :]
                    V.tensor_tensor(y, y, x0_feat[:, 4 * half + t, :], ALU.mult).then_inc(hy_val, 1)

            def hyena_out_lo(half):
                for c in range(4 * half, 4 * half + 4):
                    dve.wait_ge(u_hi, c + 1)
                    lo_part(op_lo[1][:, c, :], hy_val_feat[:, c % 4, :], op_hi[1][:, c, :]).then_inc(u_lo, 1)

            s0, s1a, i0, s1b, i1 = (FIRST[name] for name in ("dft_s0", "dft_s1a", "idft_0", "dft_s1b", "idft_1"))
            spectrum_products(0)
            spectrum_products(1)
            spectrum_lo(0)
            split_after(s0)
            spectrum_products(2)
            spectrum_lo(1)
            spectrum_products(3)
            spectrum_lo(2)
            split_after(s0 + 1)
            spectrum_lo(3)
            spectrum_products(4)
            spectrum_products(5)
            split_after(s1a)
            split_after(i0)
            hyena_sums(0)
            spectrum_lo(4)
            spectrum_lo(5)
            split_after(i0 + 1)
            spectrum_products(6)
            hyena_products(0)
            spectrum_lo(6)
            spectrum_products(7)
            hyena_out_lo(0)
            split_after(s1b)
            spectrum_lo(7)
            split_after(i1)
            hyena_sums(1)
            split_after(i1 + 1)
            hyena_products(1)
            hyena_out_lo(1)
            tail("hy_out", "norm_ffn_2", 0, 4, 4, bias_name="hy_b_out")
            norm(6)

            def gate_up(section, count, base_tiles):
                with dve.Fori(0, count // 2) as i:
                    for p in range(2):
                        m = FIRST[section] // 2 + i
                        n = 2 * i + (base_tiles + p)
                        for j in range(2):
                            product(4 * m + (2 * p + j))
                            V.tensor_tensor(z_pad[:, p, j, 0:T], ps[:, 2 * p + j, :], rstd[:], ALU.mult).then_inc(bank_read, 1)
                        split_lo(m + 1, p)
                        dve.wait_ge(bank_read, 4 * m + (2 * p + 2))
                        dve.wait_ge(gated, n + (FT + 1))
                        V.tensor_tensor(conv[:, p, 1, :], conv[:, p, 0, :], z_pad[:, p, 1, 0:T], ALU.mult).then_inc(act_prod, 1)
                        dve.wait_ge(act_hi, n + (FT + 1))
                        lo_part(op_lo[1][:, bass.ds(2 * i + p, 1), :].rearrange("p a t -> p (a t)"), conv[:, p, 1, :],
                                op_hi[1][:, bass.ds(2 * i + p, 1), :].rearrange("p a t -> p (a t)")).then_inc(act_lo, 1)

            for g in range(3):
                gate_up(f"up2_{g}", FFN_GROUPS[g], 8 * g)
                if g < 2:
                    down(f"down2_{g}")
            tail("down2_2", None, None, 5, None)
            norm(7)
            for k in range(KT):
                V.scalar_tensor_tensor(h[:, k, :], h[:, k, :], vec("norm_final_2", k), rstd[:], ALU.mult,
                                       ALU.mult).then_inc(out_made, 1)

        @block.tensor
        def _(pe):
            W = nc.tensor

            def weight(part, p, j, k):
                return part[:, p, j * CHUNK + k * P:j * CHUNK + (k + 1) * P]

            def passes(out, w, x, start, stop):
                W.matmul(out, w[0], x[0], start=start, stop=False)
                W.matmul(out, w[0], x[1], start=False, stop=False)
                return W.matmul(out, w[1], x[0], start=False, stop=stop)

            def pair_ready(g):
                pe.wait_ge(lo_ready, g + 1)

            def chunk(p, j, x, out, ks=range(KT), n_k=KT, operand=None, count=0):
                for k in ks:
                    if operand is not None:
                        pe.wait_ge(operand, count + k + 1)
                    last = passes(out, (weight(w_hi, p, j, k), weight(w_lo, p, j, k)), (x[0][:, k, :], x[1][:, k, :]),
                                  k == 0, k == n_k - 1)
                return last

            def gemm(section, x, n_k=KT, operand=None, count=0, norms=(), wide=2, late=2, pairs=None, free=None):

                def chunk_norms(at_chunk):
                    for c, which in norms:
                        if c == at_chunk:
                            norm_matmul(which)

                m = FIRST[section] // 2
                early = n_k - late
                for part in (range(early), range(early, n_k)):
                    for c in range(wide):
                        p, j = c // 2, c % 2
                        if part[0] == 0:
                            if j == 0:
                                pe.wait_ge(lo_ready, 2 * m + p + 1)
                            pe.wait_ge(bank_read, 4 * m + c - 3 if free is None else free)
                        last = chunk(p, j, x, ps[:, c, :], part, n_k, operand if c == 0 else None, count)
                        if part[0]:
                            last.then_inc(chunk_done, 1)
                            chunk_norms(c)
                for c in range(wide, 4):
                    p, j = c // 2, c % 2
                    if j == 0:
                        pe.wait_ge(lo_ready, 2 * m + p + 1)
                    pe.wait_ge(bank_read, 4 * m + c - 3)
                    chunk(p, j, x, ps[:, c, :], range(n_k), n_k).then_inc(chunk_done, 1)
                    chunk_norms(c)
                with pe.Fori(1, (dict(SECTIONS)[section] if pairs is None else pairs) // 2) as i:
                    m = FIRST[section] // 2 + i
                    for p in range(2):
                        pe.wait_ge(lo_ready, 2 * m + (p + 1))
                        for j in range(2):
                            pe.wait_ge(bank_read, 4 * m + (2 * p + j - 3))
                            chunk(p, j, x, ps[:, 2 * p + j, :], range(n_k), n_k).then_inc(chunk_done, 1)

            X = [(op_hi[0], op_lo[0]), (op_hi[1], op_lo[1])]

            def norm_matmul(isq, bank=7):
                pe.wait_ge(summed, 8 * isq + 8)
                W.matmul(ps[:, bank, :], ones[:], acc[:], start=True, stop=True).then_inc(norm_sum, 1)
                if isq == 3:
                    pe.wait_ge(summed_next, KT + 2)
                    W.matmul(ps[:, 6, :], ones[:], acc_next[:], start=True, stop=True).then_inc(norm_sum, 1)

            def misc(j):
                if j >= 2:
                    pe.wait_ge(misc_read, j - 1)
                return ps[:, 6 + j % 2, :]

            def in_pair(q, j):
                c = 2 * q + j
                if j == 0:
                    pair_ready(q)
                if c >= 4:
                    pe.wait_ge(bank_read, c - 3)
                chunk(q % 2, j, X[0], ps[:, c % 4, :], operand=next_lo if c == 0 else None).then_inc(chunk_done, 1)

            def mlp(layer):
                for d in range(2):
                    j = MLP_JOB[layer] + d
                    out = misc(j)
                    if layer == 0:
                        W.matmul(out[0:64, :], mlp_w[0:33, 0, :], feat[:, d * T:(d + 1) * T], start=True,
                                 stop=True).then_inc(misc_done, 1)
                    else:
                        pe.wait_ge(mlp_sin, 2 * layer)
                        W.matmul(out[0:64, :], mlp_w[:, layer, :], mlp_h[layer - 1][:, d, :], start=True,
                                 stop=True).then_inc(misc_done, 1)

            in_pair(0, 0)
            in_pair(0, 1)
            pe.wait_ge(made_ones, 1)
            pe.wait_ge(summed, KT)
            W.matmul(misc(0), ones[:], acc[:], start=True, stop=True).then_inc(misc_done, 1)
            pe.wait_ge(gate_folded, 1)
            bank = misc(1)
            for i in range(NT):
                for k in range(KT):
                    W.matmul(bank[:, 4 * i:4 * i + 4], h[:, k, i * P:(i + 1) * P], gate_w[:, k, :], start=(k == 0),
                             stop=(k == KT - 1))
                last = W.matmul(bank[:, 16 + i:17 + i], acc[:, i * P:(i + 1) * P], ones[:, 0:1], start=True, stop=True)
            last.then_inc(misc_done, 1)
            pe.wait_ge(small_in, 112)
            mlp(0)
            for j in range(2):
                in_pair(1, j)

            def rotate(tile, job):
                for j in range(2):
                    out = misc(job + j)
                    pe.wait_ge(bank_read, tile + j + 1)
                    W.matmul(out, rot[:], qk[:, tile + j, :], start=True, stop=True).then_inc(misc_done, 1)

            rotate(0, 4)
            for j in range(2):
                in_pair(2, j)
            rotate(2, 6)
            mlp(1)
            for j in range(2):
                in_pair(3, j)

            def transpose_v(c, job):
                for b in range(2):
                    out = misc(job + b)
                    pe.wait_ge(bank_read, c + 2)
                    for i in range(2):
                        for j in range(2):
                            last = W.transpose(out[:, i * M + j * P:i * M + (j + 1) * P],
                                               v_raw[:, j, (2 * b + i) * P:(2 * b + i + 1) * P], ident[:])
                    last.then_inc(misc_done, 1)

            transpose_v(4, 10)
            mlp(2)
            for j in range(2):
                in_pair(4, j)
            out = misc(14)
            pe.wait_ge(gate_ready, 1)
            pe.wait_ge(tri_in, 16)
            for i in range(NT):
                for s in range(i + 1):
                    last = W.matmul(out[:, 4 * i:4 * i + 4], tri[:, 0:P] if s == i else ones[:], log_f[:, s, :],
                                    start=(s == 0), stop=(s == i))
            last.then_inc(misc_done, 1)
            out = misc(15)
            for s in range(NT):
                last = W.matmul(out[0:4, s * P:T], log_f[:, s, :], tri[:, 0:T - s * P], start=(s == 0), stop=(s == NT - 1),
                                skip_group_check=True)
            last.then_inc(misc_done, 1)
            for j in range(2):
                in_pair(5, j)
            for j in range(2):
                in_pair(6, j)
            transpose_v(10, 16)
            for j in range(2):
                in_pair(7, j)
            pe.wait_ge(pool_in, 16)
            for j in range(2):
                out = misc(18 + j)
                pe.wait_ge(pooled, j + 1)
                W.matmul(out, pool_w[:, j, :], pool_a[:, j, 16:16 + T], start=True, stop=True).then_inc(misc_done, 1)
            for j in range(2):
                in_pair(8, j)
            in_pair(9, 0)
            out = misc(20)
            pe.wait_ge(mem_sum, 5)
            W.matmul(out[:, 0:M], ones[:], acc[:, 0:M], start=True, stop=True).then_inc(misc_done, 1)

            def qk_unit(u):
                s, i = UNITS[u]
                b = 64 * (s % 2)
                tile = 4 * (s // 4) + (s % 4) // 2
                n = (i + 1) * P
                if u >= 2:
                    pe.wait_ge(masked, u - 1)
                W.matmul(ps[:, 4 + u % 2, 0:n], qk[b:b + 64, tile, i * P:(i + 1) * P], qk[b:b + 64, tile + 2, 0:n],
                         start=True, stop=True).then_inc(qk_done, 1)

            def transpose_unit(u, n_blocks):
                pe.wait_ge(probs_ready, u + 1)
                if u:
                    pe.wait_ge(pt_ready, u)
                for kb in range(n_blocks):
                    last = W.transpose(ps[:, 6, kb * P:(kb + 1) * P], unit_scores(u)[:, kb * P:(kb + 1) * P], ident[:])
                last.then_inc(transposed, 1)

            def pv_unit(u):
                s, i = UNITS[u]
                b = 64 * (s % 2)
                pe.wait_ge(pt_ready, u + 1)
                if u % 8 == 0 and u > 0:
                    pe.wait_ge(pv_lo, u // 8)
                for kb in range(i + 1):
                    last = W.matmul(ps[b:b + 64, 7, i * P:(i + 1) * P], v_tok[:, kb, HD * s:HD * s + HD],
                                    probs_t[:, u % 2, kb * P:(kb + 1) * P], start=(kb == 0), stop=(kb == i))
                last.then_inc(pv_done, 1)

            def transform(tiles, chunks, x, before):
                for j, c in zip(tiles, chunks):
                    g = c // 2
                    if j % 2 == 0:
                        pair_ready(g)
                    pe.wait_ge(bank_read, c - before + 1)
                    for r in range(2):
                        for n in range(NT):
                            last = passes(ps[:, 2 * (j % 2) + r, :],
                                          (weight(w_hi, g % 2, j % 2, 4 * r + n), weight(w_lo, g % 2, j % 2, 4 * r + n)),
                                          x(j, n), n == 0, n == NT - 1)
                    last.then_inc(chunk_done, 1)

            def filter_taps(s):
                if s == 0:
                    pe.wait_ge(bank_read, 20)
                if s % 4 == 0:
                    pe.wait_ge(late_in, 32 + 8 * s)
                if s in (1, 2, 3):
                    pe.wait_ge(gen_taps, s)
                if s == 4:
                    pe.wait_ge(bank_read, 2 * FIRST["dft_g0"] + 4)
                if s >= 5:
                    pe.wait_ge(vt_read, s - 4)
                for d in range(2):
                    last = W.matmul(ps[:, 2 + d, :], mlp_h[2][:, d, s % 4 * P:(s % 4 + 1) * P], f_out[:, d, :], start=True,
                                    stop=True)
                last.then_inc(gen_done, 1)

            pe.wait_ge(roped, 4)
            qk_unit(0)
            qk_unit(1)
            in_pair(9, 1)
            pe.wait_ge(mem_lo, KT)
            for u, (s, i) in enumerate(UNITS):
                half, n = s // 4, s % 4
                g = (FIRST["k_mem"] if s < 4 else FIRST["v_mem"] - 4) + s
                c = 2 * g + i // 2
                if i == 0:
                    pair_ready(g)
                if u + 2 < len(UNITS):
                    qk_unit(u + 2)
                if u == 0:
                    filter_taps(0)
                if i % 2 == 0:
                    pe.wait_ge(bank_read, c - 1)
                last = chunk(g % 2, i // 2, (mg_hi, mg_lo), ps[:, c % 2, 0:M], range(4 * (i % 2), 4 * (i % 2) + 4))
                if i % 2 == 1:
                    last.then_inc(chunk_done, 1)
                if u == 1:
                    pe.wait_ge(misc_read, 21)
                if u:
                    transpose_unit(u - 1, (u - 1) % 4 + 1)
                if u >= 2:
                    pv_unit(u - 2)
                if i == 0 and s >= 4:
                    filter_taps(s)
                if i == 3 and s < 3:
                    filter_taps(s + 1)
                if u == 31:
                    transpose_unit(31, NT)
                    pv_unit(30)
                    pv_unit(31)
                if i == 3 and s >= 4:
                    pe.wait_ge(bank_read, c + 1)
                    pe.wait_ge(gen_taps, s + 1)
                    for b in range(2):
                        for j in range(2):
                            last = W.transpose(ps[:, 2, b * M + j * P:b * M + (j + 1) * P],
                                               v_stage[:, j, b * P:(b + 1) * P], ident[:])
                    last.then_inc(vt_done, 1)
                if i == 3 and n == 3:
                    pe.wait_ge(gen_acc, 8 * half + 8)
                    for t in range(4):
                        last = W.matmul(ps[:, 3, t:t + 1], acc[:, t * P:(t + 1) * P], ones[:, 0:1], start=True, stop=True)
                    last.then_inc(fnorm_done, 1)
                    pe.wait_ge(gen_lo, 8 * half + 8)
                    first = 2 * FIRST[f"dft_g{half}"]
                    for tiles in ((0,), (1, 2, 3)):
                        if tiles[0]:
                            pe.wait_ge(fnorm_read, half + 1)
                            if half:
                                pe.wait_ge(vt_read, 4)
                        transform(tiles, [first + j for j in tiles],
                                  lambda j, n: (op_hi[0][:, 4 * (j // 2) + n, :], op_lo[0][:, 4 * (j // 2) + n, :]), 2)

            pe.wait_ge(mix_lo, 4)
            pe.wait_ge(pv_lo, 4)
            pe.wait_ge(bank_read, 2 * FIRST["w_out"])
            gemm("w_out", X[1])

            def xq_half(n):
                q, j, part = n // 4, n % 4 // 2, n % 2
                g = FIRST["xq"] + q
                c = 2 * g + j
                if n % 4 == 0:
                    pair_ready(g)
                if part == 0:
                    pe.wait_ge(bank_read, c - 3)
                last = chunk(g % 2, j, X[0], ps[:, c % 4, :], range(4 * part, 4 * part + 4), operand=next_lo if n < 4 else None,
                             count=8)
                if part:
                    last.then_inc(chunk_done, 1)
                if n == 3:
                    norm_matmul(1)

            def x_qk(u):
                hd, i = u // 4, u % 4
                if u >= 2:
                    pe.wait_ge(exped, 32 + u - 1)
                if i == 0:
                    pe.wait_ge(bank_read, 2 * (FIRST["xq"] + hd) + 2)
                for k in range(2):
                    last = W.matmul(ps[:, 4 + u % 2, 0:M], xq[:, 2 * hd + k, i * P:(i + 1) * P], k_mem[:, 2 * hd + k, :],
                                    start=(k == 0), stop=(k == 1))
                last.then_inc(qk_done, 1)

            def x_pv(u):
                hd = u // 4
                pe.wait_ge(pt_ready, 32 + u + 1)
                if u:
                    pe.wait_ge(pv_lo, 4 + u)
                else:
                    pe.wait_ge(norm_mean, 3)
                for d in range(2):
                    for kb in range(2):
                        last = W.matmul(ps[:, 7, d * P:(d + 1) * P], v_mem[:, kb, hd * M + d * P:hd * M + (d + 1) * P],
                                        probs_t[:, u % 2, kb * P:(kb + 1) * P], start=(kb == 0), stop=(kb == 1))
                last.then_inc(pv_done, 1)

            for n in (0, 2, 1, 3, 4, 5, 6, 7):
                xq_half(n)
            x_qk(0)
            x_qk(1)
            for u in range(18):
                if u < 8:
                    xq_half(8 + u)
                if u + 2 < 16:
                    x_qk(u + 2)
                if 1 <= u <= 16:
                    transpose_unit(32 + u - 1, 2)
                if u >= 2:
                    x_pv(u - 2)
            pe.wait_ge(pv_lo, 20)
            gemm("xo", X[1])

            for g in range(3):
                gemm(f"up1_{g}", X[0], operand=next_lo if g == 0 else None, count=16, norms=[(0, 2)] if g == 0 else ())
                gemm(f"down1_{g}", X[1], n_k=FFN_GROUPS[g], operand=act_lo, count=8 * g, wide=3, late=2 if g < 2 else 1)

            gemm("hy_in", X[0], operand=next_lo, count=24, norms=[(0, 3)], pairs=8)
            for q in range(4):
                g = FIRST["hy_in"] + 8 + q
                pair_ready(g)
                for j in range(2):
                    c = 2 * g + j
                    pe.wait_ge(bank_read, c - 3)
                    chunk(g % 2, j, X[0], ps[:, c % 4, :]).then_inc(chunk_done, 1)
                    n = 2 * q + j
                    half, t = n // 4, n % 4
                    pe.wait_ge(norm_rstd, 5)
                    if n >= 4:
                        pe.wait_ge(st_lo, n - 3)
                    pe.wait_ge(hz_done, 4 * half + 4)
                    for c in range(4):
                        last = W.transpose(ps[:, 4 + n % 4, c * P:(c + 1) * P], s_feat[:, 4 * half + c, t * P:(t + 1) * P],
                                           ident[:])
                    last.then_inc(st_done, 1)

            def forward_s(half, tiles, before):
                if tiles[0] == 0:
                    pe.wait_ge(st_lo, 4 * half + 4)
                transform(tiles, [S_CHUNK[4 * half + j] for j in tiles],
                          lambda j, n: (op_hi[1][:, 4 * half + n, :], op_lo[1][:, 4 * half + n, :]), before)

            def inverse(half):
                if half:
                    pe.wait_ge(bank_read, 2 * FIRST["idft_0"] + 4)
                else:
                    pe.wait_ge(st_lo, 8)
                for q in range(4):
                    g = FIRST[f"idft_{half}"] + q // 2
                    if q % 2 == 0:
                        pair_ready(g)
                    pe.wait_ge(y_lo, 8 * half + 2 * q + 2)
                    for f in range(2):
                        at_f = slice((q % 2) * CHUNK + f * T, (q % 2) * CHUNK + (f + 1) * T)
                        for c in range(4):
                            cs = slice(c * P, (c + 1) * P)
                            last = passes(ps[:, 4 + c, :], (op_hi[0][:, 2 * q + f, cs], op_lo[0][:, 2 * q + f, cs]),
                                          (w_hi[:, g % 2, at_f], w_lo[:, g % 2, at_f]), q == f == 0, q == 3 and f == 1)
                    last.then_inc(chunk_done, 1)

            forward_s(0, (0, 1, 2, 3), 2)
            forward_s(1, (0, 1), 2)
            inverse(0)
            forward_s(1, (2, 3), 6)
            inverse(1)
            gemm("hy_out", X[1], operand=u_lo, wide=4, late=4, free=S_CHUNK[7] + 1)

            for g in range(3):
                gemm(f"up2_{g}", X[0], operand=next_lo if g == 0 else None, count=32, norms=[(0, 4)] if g == 0 else ())
                gemm(f"down2_{g}", X[1], n_k=FFN_GROUPS[g], operand=act_lo, count=FT + 8 * g, wide=3)
            norm_matmul(5)


def constants():
    f64 = np.float64
    pos = np.arange(T)
    n_fft = 2 * T
    freqs = np.concatenate([2 * np.arange(T // 2), 2 * np.arange(T // 2) + 1])
    angle = 2 * np.pi * ((freqs[:, None] * pos[None, :]) % n_fft) / n_fft
    re, im = np.cos(angle), -np.sin(angle)
    im[0] = np.cos(np.pi * pos)
    inv_re, inv_im = 2 * re / n_fft, 2 * im / n_fft
    inv_re[0] /= 2
    inv_im[0] /= 2
    t = np.linspace(0.0, 1.0, T, dtype=np.float32)
    w = (np.float32(2 * np.pi) * pos.astype(np.float32) / np.float32(T)).astype(np.float32)
    bands = np.linspace(1e-4, 15, 16, dtype=np.float32)
    arg = (bands[None, :] * w[:, None]).astype(np.float32).astype(f64)
    feat = np.concatenate([t[:, None].astype(f64), np.cos(arg), -np.sin(arg)], axis=1).astype(np.float32)
    back = np.where(pos > 0, T - pos, 0)
    feat = np.concatenate([feat, feat[back]], axis=0).T
    delta = np.arange(P)[:, None] - np.arange(T)[None, :] + 3 * P
    uses = (delta <= 128).astype(int) + ((delta % 4 == 0) & (delta <= 512)) + (delta % 16 == 0)
    uses = np.where(delta >= 0, uses, 0)
    dilated = np.where(uses > 0, -np.log(np.maximum(uses, 1).astype(f64)), BIG)
    causal = np.where(delta >= 0, 0.0, BIG)
    rot = np.zeros((P, P))
    inv_freq = np.zeros(P)
    theta = 500000.0 ** (-np.arange(0, 16, 2, dtype=f64) / 16)
    for base in (0, 64):
        for r in range(8):
            rot[base + 8 + r, base + r] = -1
            rot[base + r, base + 8 + r] = 1
            inv_freq[base + r] = inv_freq[base + 8 + r] = theta[r]
    tokens = np.arange(P)[:, None] + P * np.arange(NT)[None, :]
    neg_t = -np.concatenate([t[tokens], t[back[tokens]]], axis=1)
    edge = np.zeros((P, 2, 16))
    inv_window = np.zeros((P, 2))
    for tile in range(2):
        for part in range(2):
            window = (2, 4, 8, 16)[2 * tile + part]
            edge[64 * part:64 * part + 64, tile] = 1.0 / np.minimum(np.arange(16) + 1, window)
            inv_window[64 * part:64 * part + 64, tile] = 1.0 / window
    f32 = lambda x: np.ascontiguousarray(x, dtype=np.float32)
    return {"re": f32(re.T), "im": f32(im.T), "inv_re": f32(inv_re), "inv_im": f32(inv_im), "feat": f32(feat),
            "masks": f32(np.stack([dilated, causal])), "rot": f32(rot), "inv_freq": f32(inv_freq[:, None]),
            "neg_t": f32(neg_t), "edge": f32(edge.reshape(P, 32)), "inv_window": f32(inv_window),
            "tri": f32(np.arange(P)[:, None] <= np.arange(T)[None, :]), "ident": f32(np.eye(P))}


def by_tile(v):
    return v.reshape(-1, P).T


def chunk_of(w, tile, n_k=KT):
    out = np.zeros((P, KT, P), w.dtype)
    out[:, :n_k] = w[:, tile * P:(tile + 1) * P].reshape(n_k, P, P).transpose(1, 0, 2)
    return out.reshape(P, CHUNK)


def kernel(**inputs):
    import concourse.bacc as bacc
    from concourse.bass_utils import run_bass_kernel_spmd as run

    v = {k: np.asarray(x) for k, x in inputs.items()}
    const = constants()
    chunks = []

    def take(w, tiles, n_k=KT):
        chunks.extend(chunk_of(w, i, n_k) for i in tiles)

    def forward(tiles=range(4)):
        for j in tiles:
            both = [const[part][:, j * P:(j + 1) * P].reshape(NT, P, P).transpose(1, 0, 2).reshape(P, NT * P) for part in ("re", "im")]
            chunks.append(np.concatenate(both, axis=1))

    def inverse():
        for j in range(4):
            chunks.append(np.concatenate([const[part][j * P:(j + 1) * P] for part in ("inv_re", "inv_im")], axis=1))

    w_in = v["w_in"][0]
    gates = w_in[:, 18 * P:18 * P + 4]
    w_main = np.concatenate([w_in[:, :18 * P], w_in[:, 18 * P + 4:]], axis=1)
    take(w_main, [6, 7, 8, 9, 10, 11, 12, 13, 14, 15, 16, 17, 18, 19, 4, 0, 5, 1, 2, 3])
    take(v["w_xkv"][0], range(8))
    forward()
    take(v["w_xkv"][0], range(8, 16))
    forward()
    take(v["w_out"][0], range(8))
    take(v["w_xq"][0], range(8))
    take(v["w_xo"][0], range(8))

    def ffn(left, right, down):
        for g in range(3):
            for i in range(8 * g, 8 * g + FFN_GROUPS[g]):
                take(left, [i])
                take(right, [i])
            take(down[8 * g * P:(8 * g + FFN_GROUPS[g]) * P], range(8), FFN_GROUPS[g])

    ffn(v["w_up"][0][:, :FF], v["w_up"][0][:, FF:], v["w_down"][0])
    hy_order = [t for i in range(8) for t in (16 + i, 8 + i)] + list(range(8))
    take(v["hy_w_in_2"][0], hy_order)
    forward()
    forward((0, 1))
    inverse()
    forward((2, 3))
    inverse()
    take(v["hy_w_out_2"][0], range(8))
    ffn(v["ffn_w_gate_2"][0], v["ffn_w_up_2"][0], v["ffn_w_down_2"][0])
    weights = np.stack(chunks).reshape(PAIRS, 2, P, CHUNK).transpose(0, 2, 1, 3).reshape(PAIRS, P, 2 * CHUNK)

    hy_cols = lambda x: by_tile(x)[:, hy_order]
    cols = {name: by_tile(v[name][0]) for name in ("g_mix", "g_xa", "g_mem", "g_ffn", "norm_mix_2", "norm_ffn_2", "pool_scale")}
    cols["g_final"] = by_tile(v["g_final"])
    cols["norm_final_2"] = by_tile(v["norm_final_2"])
    cols["sconv"] = np.concatenate([by_tile(x) for x in v["w_sconv"][0]], axis=1)
    cols["ffconv"] = np.concatenate([by_tile(x) for x in v["w_ffconv"][0]], axis=1)
    cols["hy_conv"] = np.concatenate([hy_cols(x) for x in v["hy_conv_w_2"][0]], axis=1)
    cols["hy_conv_b"] = hy_cols(v["hy_conv_b_2"][0])
    cols["hy_b_in"] = hy_cols(v["hy_b_in_2"][0])
    cols["hy_skip"] = by_tile(v["hy_skip_2"][0])
    cols["hy_b_out"] = by_tile(v["hy_b_out_2"][0])
    cols["b_forget"] = np.broadcast_to(np.tile(v["b_forget"][0], 4), (P, 16))
    for name, key in (("inv_freq", "inv_freq"), ("pool_inv", "inv_window"), ("pool_edge", "edge"), ("neg_t", "neg_t")):
        cols[name] = const[key]
    vecs = np.concatenate([cols[name] for name in VEC], axis=1)
    pool_w = np.zeros((P, 2, P), np.float32)
    for i in range(4):
        at = 64 * (i % 2)
        pool_w[at:at + 64, i // 2, at:at + 64] = v["w_pool"][0][i]
    mlp_w = np.zeros((64, 3, 64), np.float32)
    mlp_w[:33, 0] = v["hy_f_w1_2"][0]
    mlp_w[:, 1] = v["hy_f_w2_2"][0]
    mlp_w[:, 2] = v["hy_f_w3_2"][0]
    arrays = {
        "weights": weights, "vecs": vecs, "ident": const["ident"],
        "x_t": v["x"][0].T.reshape(KT, P, T).transpose(1, 0, 2), "mem_t": v["mem"][0].T.reshape(KT, P, M).transpose(1, 0, 2),
        "positions": np.broadcast_to(v["positions"], (P, T)), "gate_w": gates.reshape(KT, P, 4).transpose(1, 0, 2),
        "mlp_w": mlp_w, "mlp_b": np.stack([v[k][0] for k in ("hy_f_b1_2", "hy_f_b2_2", "hy_f_b3_2", "hy_f_freq_2")], axis=1),
        "feat": const["feat"], "rot": const["rot"], "tri": const["tri"], "masks": const["masks"], "pool_w": pool_w,
        "f_out": v["hy_f_wout_2"][0].reshape(64, 2, D), "decay": np.broadcast_to(v["hy_decay_2"][0], (P, 2, D)),
    }
    nc = bacc.Bacc("TRN2", target_bir_lowering=False, num_devices=1)
    a = {}
    feeds = {}
    for name, x in arrays.items():
        feeds[f"{name}_dram"] = np.ascontiguousarray(x)
        a[name] = nc.dram_tensor(f"{name}_dram", x.shape, mybir.dt.from_np(x.dtype), kind="ExternalInput").ap()
    a["out"] = nc.dram_tensor("out_dram", (P, KT, T), F32, kind="ExternalOutput").ap()
    program(nc, a)
    r = run(nc, [feeds], core_ids=[0])
    return np.ascontiguousarray(r.results[0]["out_dram"].transpose(2, 1, 0)).reshape(1, T, D)
```
